# Optimizing a Trainium2 kernel written in Bass

```python
import math
import jax
import jax.numpy as jnp
from jax import lax

D_MODEL = 1024
BATCH = 1
SEQ = 512
DEPTH = 2

GRID_W = 64
CTX_LEN = 256
N_MOD = 9
D_FF = 2816
NORM_EPS = 1e-6

DN_HEADS = 4
DN_HEAD_DIM = 128
DN_WIDTH = DN_HEADS * DN_HEAD_DIM
DN_CHUNK = 64
SHORT_CONV = 5
DN_IN = 4 * DN_WIDTH + 4 * DN_HEADS

RW_HEADS = 8
RW_HEAD_DIM = 64
RW_WIDTH = RW_HEADS * RW_HEAD_DIM
DECAY_LORA = 64
ICLR_LORA = 64
GATE_LORA = 128
RW_GN_EPS = 64e-5
RW_IN = 3 * RW_WIDTH + 2 * DECAY_LORA + 2 * ICLR_LORA + GATE_LORA

MIX_WIDTH = DN_WIDTH + RW_WIDTH
N_IN = DN_IN + RW_IN

kernel_name = 'hybrid_deltanet_rwkv7_macaron_dit'

def rms_norm(x, gain):
    xf = x.astype(jnp.float32)
    y = xf * lax.rsqrt(jnp.mean(xf * xf, axis=-1, keepdims=True) + NORM_EPS)
    return (y * gain.astype(jnp.float32)).astype(x.dtype)

def l2_normalize(t):
    return t * lax.rsqrt(jnp.sum(t * t, axis=-1, keepdims=True) + NORM_EPS)

def modulate(h, shift, scale):
    return h * (1.0 + scale) + shift

def swiglu(h, w13, w2):
    gate, up = jnp.split(h @ w13, 2, axis=-1)
    return (jax.nn.silu(gate) * up) @ w2

def maybe_flip(t, axis, backward):
    return jnp.flip(t, axis) if backward else t

def raster_to_colmajor(t, rows):
    b, l, ch = t.shape
    return t.reshape(b, rows, GRID_W, ch).swapaxes(1, 2).reshape(b, l, ch)

def colmajor_to_raster(t, rows):
    b, l, ch = t.shape
    return t.reshape(b, GRID_W, rows, ch).swapaxes(1, 2).reshape(b, l, ch)

def centred_depthwise_conv(t, w):
    return lax.conv_general_dilated(t, w[:, None, :].astype(t.dtype), window_strides=(1,), padding='SAME',
                                    dimension_numbers=('NWC', 'WIO', 'NWC'), feature_group_count=t.shape[-1])

def centred_token_shift(t, mu):
    prev = jnp.pad(t, ((0, 0), (1, 0), (0, 0)))[:, :-1]
    nxt = jnp.pad(t, ((0, 0), (0, 1), (0, 0)))[:, 1:]
    return t + mu[0] * (prev - t) + mu[1] * (nxt - t)

def gated_delta_rule_chunked(q, k, v, g, beta, state):
    bsz, nh, seqlen, dk = q.shape
    dv = v.shape[-1]
    n_chunks = seqlen // DN_CHUNK
    f32 = jnp.float32
    q, k, v = [t.astype(f32).reshape(bsz, nh, n_chunks, DN_CHUNK, t.shape[-1]) for t in (q, k, v)]
    g = g.astype(f32).reshape(bsz, nh, n_chunks, DN_CHUNK)
    beta = beta.astype(f32).reshape(bsz, nh, n_chunks, DN_CHUNK)
    gc = jnp.cumsum(g, axis=-1)
    idx = jnp.arange(DN_CHUNK)
    lower = idx[:, None] >= idx[None, :]
    strict = idx[:, None] > idx[None, :]
    decay = jnp.exp(jnp.where(lower, gc[..., :, None] - gc[..., None, :], -jnp.inf))
    a_strict = jnp.where(strict, jnp.einsum('bhnid,bhnjd->bhnij', k, k) * decay * beta[..., :, None], 0.0)
    rhs = jnp.concatenate([k * (beta * jnp.exp(gc))[..., None], v * beta[..., None]], axis=-1)
    sol = lax.linalg.triangular_solve(a_strict, rhs, left_side=True, lower=True, unit_diagonal=True)
    w, u = sol[..., :dk], sol[..., dk:]
    attn = jnp.einsum('bhnid,bhnjd->bhnij', q, k) * decay
    q_dec = q * jnp.exp(gc)[..., None]
    k_dec = k * jnp.exp(gc[..., -1:] - gc)[..., None]
    chunk_decay = jnp.exp(gc[..., -1])

    def step(s, inp):
        w_n, u_n, attn_n, qd_n, kd_n, cd_n = inp
        v_new = u_n - jnp.einsum('bhcd,bhde->bhce', w_n, s)
        o_n = jnp.einsum('bhcd,bhde->bhce', qd_n, s) + jnp.einsum('bhij,bhje->bhie', attn_n, v_new)
        s = s * cd_n[..., None, None] + jnp.einsum('bhcd,bhce->bhde', kd_n, v_new)
        return s, o_n

    xs = tuple(jnp.moveaxis(t, 2, 0) for t in (w, u, attn, q_dec, k_dec, chunk_decay))
    state, o = lax.scan(step, state.astype(f32), xs)
    return jnp.moveaxis(o, 0, 2).reshape(bsz, nh, seqlen, dv), state

def deltanet_features(p, conv_w, a_log, dt_bias):
    bsz, seqlen, _ = p.shape
    p = p.astype(jnp.float32)
    qkv = jax.nn.silu(centred_depthwise_conv(p[..., :3 * DN_WIDTH], conv_w))
    q, k, v = [t.reshape(bsz, seqlen, DN_HEADS, DN_HEAD_DIM) for t in jnp.split(qkv, 3, axis=-1)]
    q = l2_normalize(q) * DN_HEAD_DIM ** -0.5
    k = l2_normalize(k)
    z = p[..., 3 * DN_WIDTH:4 * DN_WIDTH].reshape(bsz, seqlen, DN_HEADS, DN_HEAD_DIM)
    ab = p[..., 4 * DN_WIDTH:].reshape(bsz, seqlen, 2, 2, DN_HEADS)
    g = -jnp.exp(a_log) * jax.nn.softplus(ab[:, :, 0] + dt_bias)
    beta = jax.nn.sigmoid(ab[:, :, 1])
    bhl = lambda t: jnp.transpose(t, (0, 2, 1, 3))
    return bhl(q), bhl(k), bhl(v), jnp.transpose(g, (0, 2, 3, 1)), jnp.transpose(beta, (0, 2, 3, 1)), z

def gated_head_norm(o, z, w):
    o = jnp.transpose(o, (0, 2, 1, 3))
    o = o * lax.rsqrt(jnp.mean(o * o, axis=-1, keepdims=True) + NORM_EPS) * w
    o = o * jax.nn.silu(z)
    return o.reshape(o.shape[0], o.shape[1], DN_WIDTH)

def deltanet_group(p_ctx, p_lat, conv_w, a_log, dt_bias, norm_w):
    qc, kc, vc, gc, bc, zc = deltanet_features(p_ctx, conv_w, a_log, dt_bias)
    ql, kl, vl, gl, bl, zl = deltanet_features(p_lat, conv_w, a_log, dt_bias)
    zero = jnp.zeros((qc.shape[0], DN_HEADS, DN_HEAD_DIM, DN_HEAD_DIM), jnp.float32)
    o_ctx = jnp.zeros_like(vc)
    o_lat = jnp.zeros_like(vl)
    for d in range(2):
        bwd = d == 1
        oc, s_ctx = gated_delta_rule_chunked(*[maybe_flip(t, 2, bwd) for t in (qc, kc, vc, gc[:, d], bc[:, d])], zero)
        ol, _ = gated_delta_rule_chunked(*[maybe_flip(t, 2, bwd) for t in (ql, kl, vl, gl[:, d], bl[:, d])], s_ctx)
        o_ctx = o_ctx + maybe_flip(oc, 2, bwd)
        o_lat = o_lat + maybe_flip(ol, 2, bwd)
    return gated_head_norm(o_ctx, zc, norm_w), gated_head_norm(o_lat, zl, norm_w)

def rwkv7_scan(r, w, k, v, kk, a, state):
    def step(s, inp):
        r_t, w_t, k_t, v_t, kk_t, a_t = inp
        sa = jnp.einsum('bhvk,bhk->bhv', s, kk_t)
        s = s * w_t[:, :, None, :] - sa[..., None] * (kk_t * a_t)[:, :, None, :] + v_t[..., None] * k_t[:, :, None, :]
        return s, jnp.einsum('bhvk,bhk->bhv', s, r_t)

    xs = tuple(jnp.moveaxis(t, 1, 0) for t in (r, w, k, v, kk, a))
    state, y = lax.scan(step, state, xs)
    return jnp.moveaxis(y, 0, 1), state

def rwkv7_features(p, mu, w0, w2, a0, a2, g2, k_k, k_a):
    bsz, seqlen, _ = p.shape
    heads = lambda t: t.reshape(*t.shape[:-1], RW_HEADS, RW_HEAD_DIM)
    p = centred_token_shift(p.astype(jnp.float32), mu)
    r, k, v = jnp.split(p[..., :3 * RW_WIDTH], 3, axis=-1)
    o = 3 * RW_WIDTH
    lw = p[..., o:o + 2 * DECAY_LORA].reshape(bsz, seqlen, 2, DECAY_LORA)
    o += 2 * DECAY_LORA
    la = p[..., o:o + 2 * ICLR_LORA].reshape(bsz, seqlen, 2, ICLR_LORA)
    o += 2 * ICLR_LORA
    lg = p[..., o:]
    w_log = -jax.nn.softplus(-(w0 + jnp.einsum('bldr,drc->bldc', jnp.tanh(lw), w2))) - 0.5
    decay = jnp.exp(-jnp.exp(w_log))
    a = jax.nn.sigmoid(a0 + jnp.einsum('bldr,drc->bldc', la, a2))
    gate = jax.nn.sigmoid(lg) @ g2
    kk = l2_normalize(heads(k * k_k))
    k_dir = k[:, :, None, :] * (1.0 + (a - 1.0) * k_a)
    return heads(r), heads(v), kk, heads(decay), heads(a), heads(k_dir), gate

def head_group_norm(y, weight, bias):
    mean = jnp.mean(y, axis=-1, keepdims=True)
    yc = y - mean
    yn = yc * lax.rsqrt(jnp.mean(yc * yc, axis=-1, keepdims=True) + RW_GN_EPS)
    return yn.reshape(*y.shape[:-2], RW_WIDTH) * weight + bias

def rwkv7_group(p_ctx, p_lat, rows, mu, w0, w2, a0, a2, g2, k_k, k_a, u, ln):
    rc, vc, kkc, wc, ac, kc, gc = rwkv7_features(p_ctx, mu, w0, w2, a0, a2, g2, k_k, k_a)
    rl, vl, kkl, wl, al, kl, gl = rwkv7_features(raster_to_colmajor(p_lat, rows), mu, w0, w2, a0, a2, g2, k_k, k_a)
    zero = jnp.zeros((rc.shape[0], RW_HEADS, RW_HEAD_DIM, RW_HEAD_DIM), jnp.float32)
    y_ctx = jnp.zeros_like(rc)
    y_lat = jnp.zeros_like(rl)
    for d in range(2):
        bwd = d == 1
        yc, s_ctx = rwkv7_scan(*[maybe_flip(t, 1, bwd) for t in (rc, wc[:, :, d], kc[:, :, d], vc, kkc, ac[:, :, d])], zero)
        yl, _ = rwkv7_scan(*[maybe_flip(t, 1, bwd) for t in (rl, wl[:, :, d], kl[:, :, d], vl, kkl, al[:, :, d])], s_ctx)
        y_ctx = y_ctx + maybe_flip(yc, 1, bwd) + jnp.sum(rc * kc[:, :, d] * u[d], axis=-1, keepdims=True) * vc
        y_lat = y_lat + maybe_flip(yl, 1, bwd) + jnp.sum(rl * kl[:, :, d] * u[d], axis=-1, keepdims=True) * vl
    out_ctx = head_group_norm(y_ctx, ln[0], ln[1]) * gc
    out_lat = colmajor_to_raster(head_group_norm(y_lat, ln[0], ln[1]) * gl, rows)
    return out_ctx, out_lat

def token_mixing(h_ctx, h_lat, rows, w_in, dn_conv, dn_a_log, dn_dt_bias, dn_norm, rw_mu, rw_w0, rw_w2,
                 rw_a0, rw_a2, rw_g2, rw_kk, rw_ka, rw_u, rw_ln, w_out):
    p_ctx = h_ctx @ w_in
    p_lat = h_lat @ w_in
    dn_ctx, dn_lat = deltanet_group(p_ctx[..., :DN_IN], p_lat[..., :DN_IN], dn_conv, dn_a_log, dn_dt_bias, dn_norm)
    rw_ctx, rw_lat = rwkv7_group(p_ctx[..., DN_IN:], p_lat[..., DN_IN:], rows, rw_mu, rw_w0, rw_w2,
                                 rw_a0, rw_a2, rw_g2, rw_kk, rw_ka, rw_u, rw_ln)
    out_ctx = jnp.concatenate([dn_ctx, rw_ctx], axis=-1).astype(h_ctx.dtype) @ w_out
    out_lat = jnp.concatenate([dn_lat, rw_lat], axis=-1).astype(h_lat.dtype) @ w_out
    return out_ctx, out_lat

def setup_inputs(seed: int = 0) -> dict:
    key = jax.random.key(seed)
    ks = iter(jax.random.split(key, 32))
    nrm = lambda shape, scale: scale * jax.random.normal(next(ks), shape, jnp.float32)
    unif = lambda shape, lo, hi: jax.random.uniform(next(ks), shape, jnp.float32, lo, hi)
    dt = jnp.exp(unif((DEPTH, 2, DN_HEADS), math.log(1e-3), math.log(1e-1)))
    return {
        'x': nrm((BATCH, SEQ, D_MODEL), 1.0),
        'c': nrm((BATCH, D_MODEL), 1.0),
        'ctx': nrm((BATCH, CTX_LEN, D_MODEL), 1.0),
        'c_ctx': nrm((D_MODEL,), 1.0),
        'ada_w': nrm((DEPTH, D_MODEL, N_MOD * D_MODEL), D_MODEL ** -0.5),
        'ada_b': nrm((DEPTH, N_MOD * D_MODEL), 0.02),
        'norm_g': 1.0 + nrm((DEPTH, 3, D_MODEL), 0.05),
        'ffn_w13': nrm((DEPTH, 2, D_MODEL, 2 * D_FF), D_MODEL ** -0.5),
        'ffn_w2': nrm((DEPTH, 2, D_FF, D_MODEL), D_FF ** -0.5),
        'w_in': nrm((DEPTH, D_MODEL, N_IN), D_MODEL ** -0.5),
        'dn_conv': nrm((DEPTH, SHORT_CONV, 3 * DN_WIDTH), SHORT_CONV ** -0.5),
        'dn_a_log': jnp.log(unif((DEPTH, 2, DN_HEADS), 1.0, 16.0)),
        'dn_dt_bias': dt + jnp.log(-jnp.expm1(-dt)),
        'dn_norm': 1.0 + nrm((DEPTH, DN_HEAD_DIM), 0.05),
        'rw_mu': unif((DEPTH, 2, RW_IN), 0.0, 0.5),
        'rw_w0': unif((DEPTH, 2, RW_WIDTH), -5.5, -0.5),
        'rw_w2': nrm((DEPTH, 2, DECAY_LORA, RW_WIDTH), 0.1),
        'rw_a0': nrm((DEPTH, 2, RW_WIDTH), 0.1),
        'rw_a2': nrm((DEPTH, 2, ICLR_LORA, RW_WIDTH), 0.1),
        'rw_g2': nrm((DEPTH, GATE_LORA, RW_WIDTH), GATE_LORA ** -0.5),
        'rw_kk': 0.85 + nrm((DEPTH, RW_WIDTH), 0.05),
        'rw_ka': 1.0 + nrm((DEPTH, RW_WIDTH), 0.05),
        'rw_u': nrm((DEPTH, 2, RW_HEADS, RW_HEAD_DIM), 0.1),
        'rw_ln': jnp.stack([1.0 + nrm((DEPTH, RW_WIDTH), 0.05), nrm((DEPTH, RW_WIDTH), 0.01)], axis=1),
        'w_out': nrm((DEPTH, MIX_WIDTH, D_MODEL), MIX_WIDTH ** -0.5),
        'final_norm': 1.0 + nrm((D_MODEL,), 0.05),
    }

def reference(x, c, ctx, c_ctx, ada_w, ada_b, norm_g, ffn_w13, ffn_w2, w_in, dn_conv, dn_a_log, dn_dt_bias,
              dn_norm, rw_mu, rw_w0, rw_w2, rw_a0, rw_a2, rw_g2, rw_kk, rw_ka, rw_u, rw_ln, w_out, final_norm):
    rows = x.shape[1] // GRID_W
    h_lat, h_ctx = x, ctx
    s_lat = jax.nn.silu(c)[:, None, :]
    s_ctx = jax.nn.silu(c_ctx)[None, None, :]
    for i in range(DEPTH):
        last = i == DEPTH - 1
        m_lat = jnp.split(s_lat @ ada_w[i] + ada_b[i], N_MOD, axis=-1)
        m_ctx = jnp.split(s_ctx @ ada_w[i] + ada_b[i], N_MOD, axis=-1)
        h_lat = h_lat + 0.5 * m_lat[2] * swiglu(modulate(rms_norm(h_lat, norm_g[i, 0]), m_lat[0], m_lat[1]),
                                                ffn_w13[i, 0], ffn_w2[i, 0])
        h_ctx = h_ctx + 0.5 * m_ctx[2] * swiglu(modulate(rms_norm(h_ctx, norm_g[i, 0]), m_ctx[0], m_ctx[1]),
                                                ffn_w13[i, 0], ffn_w2[i, 0])
        mix_ctx, mix_lat = token_mixing(
            modulate(rms_norm(h_ctx, norm_g[i, 1]), m_ctx[3], m_ctx[4]),
            modulate(rms_norm(h_lat, norm_g[i, 1]), m_lat[3], m_lat[4]),
            rows, w_in[i], dn_conv[i], dn_a_log[i], dn_dt_bias[i], dn_norm[i], rw_mu[i], rw_w0[i], rw_w2[i],
            rw_a0[i], rw_a2[i], rw_g2[i], rw_kk[i], rw_ka[i], rw_u[i], rw_ln[i], w_out[i])
        h_lat = h_lat + m_lat[5] * mix_lat
        h_lat = h_lat + 0.5 * m_lat[8] * swiglu(modulate(rms_norm(h_lat, norm_g[i, 2]), m_lat[6], m_lat[7]),
                                                ffn_w13[i, 1], ffn_w2[i, 1])
        if not last:
            h_ctx = h_ctx + m_ctx[5] * mix_ctx
            h_ctx = h_ctx + 0.5 * m_ctx[8] * swiglu(modulate(rms_norm(h_ctx, norm_g[i, 2]), m_ctx[6], m_ctx[7]),
                                                    ffn_w13[i, 1], ffn_w2[i, 1])
    return rms_norm(h_lat, final_norm)


_drawn_inputs = setup_inputs


def setup_inputs(seed=0):
    import zlib

    import numpy as np

    out = dict(_drawn_inputs(seed))
    spreads = {}
    factors = {'rw_a0': 5.519, 'rw_u': 8.0}
    for name, (base, spread) in spreads.items():
        noise = np.random.default_rng([zlib.crc32(name.encode()), seed]).standard_normal(out[name].shape)
        drawn = base * np.exp(spread * noise) if base else spread * noise
        out[name] = jnp.asarray(drawn.astype(out[name].dtype))
    for name, factor in factors.items():
        out[name] = (out[name] * factor).astype(out[name].dtype)
    return out
```

```python
from contextlib import ExitStack

import concourse.bass as bass
from concourse import mybir

F32 = mybir.dt.float32
ALU = mybir.AluOpType
ACT = mybir.ActivationFunctionType

P = 128
D_MODEL, SEQ, CTX, DEPTH, GRID_W = 1024, 512, 256, 2, 64
GRID_H = SEQ // GRID_W
T = CTX + SEQ
KT = D_MODEL // P
D_FF = 2816
NF = D_FF // P
N_MOD = 9
EPS = 1e-6
DN_H, DN_W = 4, 512
DN_IN = 4 * DN_W + 4 * DN_H
DN_C = 128
RW_W, RW_C = 512, 64
NB = RW_W // P
RW_CHUNKS = T // RW_C
GN_EPS = 64e-5
DECAY_SCALE = 0.6065306597126334
SEGS = ((0, CTX), (CTX, SEQ))
PHASES_PER_LAYER = 14

A_ADAB, A_NORM, A_FINAL, A_LN, A_DNN, A_ROWS = 0, 72, 96, 104, 112, 113
B_CONV, B_MU, B_W0, B_A0, B_KK, B_KA, B_U, B_ROWS = 0, 60, 90, 98, 106, 110, 114, 122


def build(nc, x, c, ctx, c_ctx, ada_w, ada_b, norm_g, ffn_w13, ffn_w2, w_in, dn_conv, dn_a_log, dn_dt_bias,
          dn_norm, rw_mu, rw_w0, rw_w2, rw_a0, rw_a2, rw_g2, rw_kk, rw_ka, rw_u, rw_ln, w_out, final_norm,
          out):
    es = ExitStack()
    with es:
        def sb(name, shape):
            return es.enter_context(nc.sbuf_tensor(name, shape, F32))

        ARENA = 49152
        arena = sb("arena", [P, ARENA])

        def region(start, *dims):
            n = 1
            for d in dims:
                n *= d
            assert start + n <= ARENA
            flat = arena[:, start:start + n]
            if len(dims) == 1:
                return flat
            if len(dims) == 2:
                return flat.rearrange("p (a b) -> p a b", a=dims[0])
            if len(dims) == 3:
                return flat.rearrange("p (a b c) -> p a b c", a=dims[0], b=dims[1])
            return flat.rearrange("p (a b c d) -> p a b c d", a=dims[0], b=dims[1], c=dims[2])

        PS = es.enter_context(nc.psum_tensor("PS", [P, 8, 512], F32))

        ident = sb("ident", [P, P])
        flip = sb("flip", [P, P])
        ones = sb("ones", [P, P])
        headones = sb("headones", [P, P])
        upto_incl = sb("upto_incl", [P, P])
        upto_strict = sb("upto_strict", [P, P])
        level = sb("level", [P, 7, P])
        pair_incl = sb("pair_incl", [P, RW_C])
        keep = sb("keep", [P, T])
        prm = sb("prm", [P, DEPTH, 2, P])
        cs = sb("cs", [P, KT, 2])
        mod = sb("mod", [P, N_MOD * KT, 2])
        gain = sb("gain", [P, 3, KT, 2])
        drv = sb("drv", [P, 20])
        dn_rows = sb("dn_rows", [P, 2, 2 * DN_H])
        eps = sb("eps", [P, 3])
        ab_raw = sb("ab_raw", [P, 6, 16])

        h = region(0, KT, T)
        xn = region(6144, KT, T)
        hidden = region(12288, NF, T)
        w13_buf = region(29184, 2, KT, 2, P)
        w2_buf = region(33280, 2, NF, P)
        silu_buf = region(38912, 2, T)
        sq = region(40448, 2, T)
        rstd = region(41984, T)
        ada_buf = region(42752, 2, KT, 2 * P)
        tok_in = region(12288, 6, D_MODEL)
        prm_rows = region(18432, DEPTH, 2, P)
        c_rows = region(19200, P)
        qkv = region(12288, 3 * NB, T)
        zgate = region(21504, NB, T)
        dn_o = region(24576, NB, T)
        win_buf = region(46848, 2, KT, P)
        pad = region(31744, 2, 776)
        conv = region(33296, 2, 776)
        wab = region(34848, KT, 16)
        sm = 42752
        ag = region(sm, 6, 8)
        bt = region(sm + 48, 6, 8)
        t48a = region(sm + 96, 48)
        t48b = region(sm + 144, 48)
        g_ = region(sm + 192, 6, 8)
        gcum = region(sm + 240, 6, 8)
        begc = region(sm + 288, 6, 8)
        ab_flip = region(sm + 336, 6, 16)

        h_save = nc.dram_tensor("h_save", (P, KT * T), F32, kind="Internal").ap()
        mix_save = nc.dram_tensor("mix_save", (P, NB * T), F32, kind="Internal").ap()

        made = {}

        def sem(name):
            if name not in made:
                made[name] = es.enter_context(nc.semaphore(name))
            return made[name]

        phase_done = sem("phase_done")
        phases = {}

        def end_phase(eng, who):
            phases[who] = phases.get(who, 0) + 1
            eng.drain().then_inc(phase_done, 1)
            eng.wait_ge(phase_done, 4 * phases[who])

        def dma_after(eng, n):
            eng.wait_ge(phase_done, 4 * n)

        def start_of(layer, k):
            return 1 + PHASES_PER_LAYER * layer + k

        def bc(ap, axis, shape):
            return ap.unsqueeze(axis).broadcast_to(list(shape))

        prm_landed, tok_landed, masks_ready = sem("prm_landed"), sem("tok_landed"), sem("masks_ready")
        rows_transposed, tiles_transposed, tile_moved = sem("rows_transposed"), sem("tiles_transposed"), sem("tile_moved")
        N_PRM = 12 * DEPTH + 2

        def sp_setup(sp):
            for l in range(DEPTH):
                for tile, at, src in (
                    (0, A_ADAB, ada_b[l].rearrange("(a p) -> a p", p=P)),
                    (0, A_NORM, norm_g[l].rearrange("n (a p) -> (n a) p", p=P)),
                    (0, A_FINAL, final_norm.rearrange("(a p) -> a p", p=P)),
                    (0, A_LN, rw_ln[l].rearrange("n (a p) -> (n a) p", p=P)),
                    (0, A_DNN, dn_norm[l:l + 1, :]),
                    (1, B_CONV, dn_conv[l].rearrange("n (a p) -> (n a) p", p=P)),
                    (1, B_MU, rw_mu[l].rearrange("n (a p) -> (n a) p", p=P)),
                    (1, B_W0, rw_w0[l].rearrange("n (a p) -> (n a) p", p=P)),
                    (1, B_A0, rw_a0[l].rearrange("n (a p) -> (n a) p", p=P)),
                    (1, B_KK, rw_kk[l].rearrange("(a p) -> a p", p=P)),
                    (1, B_KA, rw_ka[l].rearrange("(a p) -> a p", p=P)),
                    (1, B_U, rw_u[l].rearrange("n (a g) p -> (n a) (g p)", g=2)),
                ):
                    sp.dma_start(prm_rows[at:at + src.shape[0], l, tile, :], src).then_inc(prm_landed, 16)
            sp.dma_start(c_rows[0:8, :], c_ctx.rearrange("(a p) -> a p", p=P)).then_inc(prm_landed, 16)
            sp.dma_start(c_rows[8:16, :], c[0].rearrange("(a p) -> a p", p=P)).then_inc(prm_landed, 16)
            sp.dma_start(tok_in[:, 0:2, :], ctx[0].rearrange("(a p) f -> p a f", p=P)).then_inc(tok_landed, 16)
            sp.dma_start(tok_in[:, 2:6, :], x[0].rearrange("(a p) f -> p a f", p=P)).then_inc(tok_landed, 16)

        def pool_setup(pool):
            m = masks_ready
            count = [0]

            def then(ins):
                count[0] += 1
                ins.then_inc(m, 1)
                pool.wait_ge(m, count[0])

            g = nc.gpsimd
            then(g.memset(ones[:, :], 1.0))
            then(g.memset(eps[:, 0:1], EPS))
            then(g.memset(eps[:, 1:2], GN_EPS))
            then(g.memset(eps[:, 2:3], P * EPS))
            then(g.memset(keep[:, :], 1.0))
            then(g.memset(keep[:, :].rearrange("p (a b) -> p a b", b=RW_C)[:, :, 0:1], 0.0))
            then(g.memset(headones[:, :], 0.0))
            then(g.memset(headones[0:64, 0:64], 1.0))
            then(g.memset(headones[64:128, 64:128], 1.0))
            then(g.affine_select(out=ident[:, :], in_=ones[:, :], compare_op=ALU.is_equal, fill=0.0, base=0,
                                 pattern=[[-1, P]], channel_multiplier=1))
            then(g.affine_select(out=flip[:, :], in_=ones[:, :], compare_op=ALU.is_equal, fill=0.0, base=-(P - 1),
                                 pattern=[[1, P]], channel_multiplier=1))
            then(g.affine_select(out=upto_incl[:, :], in_=ones[:, :], compare_op=ALU.is_ge, fill=0.0, base=0,
                                 pattern=[[1, P]], channel_multiplier=-1))
            then(g.affine_select(out=upto_strict[:, :], in_=ones[:, :], compare_op=ALU.is_ge, fill=0.0, base=-1,
                                 pattern=[[1, P]], channel_multiplier=-1))
            for half in range(2):
                v = pair_incl[64 * half:64 * half + 64, :]
                then(g.affine_select(out=v, in_=ones[64 * half:64 * half + 64, 0:RW_C], compare_op=ALU.is_ge,
                                     fill=0.0, base=0, pattern=[[1, RW_C]], channel_multiplier=-1))
            then(g.memset(level[:, :, :], 0.0))
            for l in range(7):
                w = 1 << l
                v = level[:, l, :].rearrange("p (b s j) -> p b s j", s=2, j=w)[:, :, 0, :]
                nb = P // (2 * w)
                then(g.memset(v, 1.0))
                then(g.affine_select(out=v, in_=v, compare_op=ALU.is_ge, fill=0.0, base=-w,
                                     pattern=[[-2 * w, nb], [0, w]], channel_multiplier=1))
                then(g.affine_select(out=v, in_=v, compare_op=ALU.is_ge, fill=0.0, base=2 * w - 1,
                                     pattern=[[2 * w, nb], [0, w]], channel_multiplier=-1))
            pool.sem_inc(masks_ready, 100)

        def pe_setup(pe):
            pe.wait_ge(masks_ready, 100)
            pe.wait_ge(prm_landed, 16 * N_PRM)
            for l in range(DEPTH):
                for tile, rows in ((0, A_ROWS), (1, B_ROWS)):
                    pe.transpose(PS[:, 0, (2 * l + tile) * P:(2 * l + tile) * P + rows],
                                 prm_rows[0:rows, l, tile, :], ident[0:rows, 0:rows])
            pe.transpose(PS[:, 1, 0:16], c_rows[0:16, :], ident[0:16, 0:16]).then_inc(rows_transposed, 1)
            pe.wait_ge(tok_landed, 32)
            for k in range(KT):
                b = 2 + 2 * (k % 3)
                if k >= 3:
                    pe.wait_ge(tile_moved, 2 * (k - 2))
                for t in range(6):
                    bank, at = (b, t * P) if t < 2 else (b + 1, (t - 2) * P)
                    mm = pe.transpose(PS[:, bank, at:at + P], tok_in[:, t, k * P:(k + 1) * P], ident[:, :])
                mm.then_inc(tiles_transposed, 1)

        def act_setup(act):
            act.wait_ge(rows_transposed, 1)
            nc.scalar.activation(cs[:, :, 0:1], PS[:, 1, 0:8].unsqueeze(2), ACT.Silu)
            nc.scalar.activation(cs[:, :, 1:2], PS[:, 1, 8:16].unsqueeze(2), ACT.Silu)

        def dve_setup(dve):
            dve.wait_ge(rows_transposed, 1)
            for l in range(DEPTH):
                for tile, rows in ((0, A_ROWS), (1, B_ROWS)):
                    nc.vector.tensor_copy(prm[:, l, tile, 0:rows],
                                          PS[:, 0, (2 * l + tile) * P:(2 * l + tile) * P + rows])
            for k in range(KT):
                b = 2 + 2 * (k % 3)
                dve.wait_ge(tiles_transposed, k + 1)
                nc.vector.tensor_copy(h[:, k, 0:CTX], PS[:, b, 0:CTX]).then_inc(tile_moved, 1)
                nc.vector.tensor_copy(h[:, k, CTX:T], PS[:, b + 1, 0:SEQ]).then_inc(tile_moved, 1)

        ADA_CHUNKS = N_MOD * KT // 2
        ada_landed = [sem("ada_landed0"), sem("ada_landed1")]
        ada_used, mod_ready = sem("ada_used"), sem("mod_ready")

        def sp_ada(sp, layer):
            src = ada_w[layer].rearrange("(k p) n -> p k n", p=P)
            with sp.Fori(0, ADA_CHUNKS // 2) as i:
                for b in range(2):
                    sp.wait_ge(ada_used, layer * ADA_CHUNKS + 2 * i + b + 1)
                    sp.dma_start(ada_buf[:, b], src[:, :, bass.ds((2 * i + b) * 2 * P, 2 * P)]).then_inc(ada_landed[b], 16)

        def pe_ada(pe, layer):
            if layer == 0:
                pe.sem_inc(ada_used, 2)
            with pe.Fori(0, ADA_CHUNKS // 2) as i:
                for b in range(2):
                    pe.wait_ge(ada_landed[b], 16 * (layer * ADA_CHUNKS // 2 + i + 1))
                    for f in range(2):
                        for k in range(KT):
                            mm = pe.matmul(PS[:, 0, bass.ds(8 * i + 4 * b + 2 * f, 2)], ada_buf[:, b, k, f * P:(f + 1) * P],
                                           cs[:, k, :], start=(k == 0), stop=(k == KT - 1))
                    mm.then_inc(ada_used, 1)

        def dve_ada(dve, layer):
            base = 9 * layer
            pa, pb_ = prm[:, layer, 0], prm[:, layer, 1]
            dve.wait_ge(ada_used, 2 + (layer + 1) * ADA_CHUNKS)
            nc.vector.tensor_tensor(mod[:, :, :], PS[:, 0, 0:2 * N_MOD * KT].rearrange("p (a s) -> p a s", s=2),
                                    bc(pa[:, A_ADAB:A_ADAB + 72], 2, [P, 72, 2]), ALU.add).then_inc(mod_ready, 1)
            dve.wait_ge(mod_ready, base + 1)
            for n in range(3):
                nc.vector.scalar_tensor_tensor(gain[:, n], mod[:, (3 * n + 1) * KT:(3 * n + 2) * KT, :], 1.0,
                                               bc(pa[:, A_NORM + n * KT:A_NORM + (n + 1) * KT], 2, [P, KT, 2]),
                                               ALU.add, ALU.mult).then_inc(mod_ready, 1)
            for n in (0, 2):
                v = mod[:, (3 * n + 2) * KT:(3 * n + 3) * KT, :]
                nc.vector.tensor_scalar(v, v, 0.5, None, ALU.mult).then_inc(mod_ready, 1)
            nc.vector.tensor_tensor(drv[:, 0:15], pb_[:, B_MU:B_MU + 15], pb_[:, B_MU + 15:B_MU + 30],
                                    ALU.add).then_inc(mod_ready, 1)
            dve.wait_ge(mod_ready, base + 7)
            nc.vector.tensor_scalar(drv[:, 0:15], drv[:, 0:15], -1.0, 1.0, ALU.mult, ALU.add).then_inc(mod_ready, 1)
            nc.vector.tensor_scalar(drv[:, 15:19], pb_[:, B_KA:B_KA + 4], -1.0, 1.0, ALU.mult, ALU.add).then_inc(mod_ready, 1)

        sq_ready, sq_summed, rstd_ready, normed, xn_ready = (
            sem("sq_ready"), sem("sq_summed"), sem("rstd_ready"), sem("normed"), sem("xn_ready"))

        def act_square(act, n, segs):
            a, z = segs[0][0], segs[-1][0] + segs[-1][1]
            for k in range(KT):
                if k >= 2:
                    act.wait_ge(sq_summed, KT * n + k - 1)
                nc.scalar.activation(sq[:, k % 2, a:z], h[:, k, a:z], ACT.Square).then_inc(sq_ready, 1)

        def pe_square_sum(pe, n, segs):
            for k in range(KT):
                pe.wait_ge(sq_ready, KT * n + k + 1)
                for s, (a, w) in enumerate(segs):
                    mm = pe.matmul(PS[:, s, 0:w], ones[:, :], sq[:, k % 2, a:a + w], start=(k == 0), stop=(k == KT - 1))
                mm.then_inc(sq_summed, 1)

        def act_root(act, n, segs):
            act.wait_ge(sq_summed, KT * (n + 1))
            for s, (a, w) in enumerate(segs):
                ins = nc.scalar.activation(rstd[:, a:a + w], PS[:, s, 0:w], ACT.Sqrt, scale=1.0 / D_MODEL, bias=eps[:, 0:1])
            ins.then_inc(rstd_ready, 1)

        def dve_rstd(dve, n, segs):
            dve.wait_ge(rstd_ready, 2 * n + 1)
            a, z = segs[0][0], segs[-1][0] + segs[-1][1]
            nc.vector.reciprocal(rstd[:, a:z], rstd[:, a:z]).then_inc(rstd_ready, 1)
            dve.wait_ge(rstd_ready, 2 * n + 2)

        def dve_norm(dve, n, segs):
            dve_rstd(dve, n, segs)
            a, z = segs[0][0], segs[-1][0] + segs[-1][1]
            for k in range(KT):
                nc.vector.tensor_tensor(xn[:, k, a:z], h[:, k, a:z], rstd[:, a:z], ALU.mult).then_inc(normed, 1)

        def act_modulate(act, n, which, segs):
            act_square(act, n, segs)
            act_root(act, n, segs)
            for k in range(KT):
                act.wait_ge(normed, KT * n + k + 1)
                for a, w in segs:
                    s = 0 if a == 0 else 1
                    ins = nc.scalar.activation(xn[:, k, a:a + w], xn[:, k, a:a + w], ACT.Identity,
                                               bias=mod[:, 3 * which * KT + k, s:s + 1], scale=gain[:, which, k, s:s + 1])
                ins.then_inc(xn_ready, 1)

        w13_landed = [sem("w13_landed0"), sem("w13_landed1")]
        w2_landed = [sem("w2_landed0"), sem("w2_landed1")]
        hidden_summed, silu_ready, hidden_ready = sem("hidden_summed"), sem("silu_ready"), sem("hidden_ready")
        ffn_summed, ffn_added = sem("ffn_summed"), sem("ffn_added")

        def sp_ffn(sp, n, layer, which):
            w13 = ffn_w13[layer, which].rearrange("(k p) (g f) -> p k g f", p=P, g=2)
            w2 = ffn_w2[layer, which].rearrange("(k p) f -> p k f", p=P)
            with sp.Fori(0, NF // 2) as i:
                for b in range(2):
                    sp.wait_ge(hidden_summed, n * NF + 2 * i + b + 1)
                    for g in range(2):
                        sp.dma_start(w13_buf[:, b, :, g, :],
                                     w13[:, :, g, bass.ds((2 * i + b) * P, P)]).then_inc(w13_landed[b], 16)
            with sp.Fori(0, KT // 2) as i:
                for b in range(2):
                    sp.wait_ge(ffn_summed, n * KT + 2 * i + b + 1)
                    sp.dma_start(w2_buf[:, b], w2[:, :, bass.ds((2 * i + b) * P, P)]).then_inc(w2_landed[b], 16)

        def pe_ffn(pe, n, segs):
            if n == 0:
                pe.sem_inc(hidden_summed, 2)
                pe.sem_inc(ffn_summed, 2)
            a = segs[0][0]
            half = (T - a) // 2
            with pe.Fori(0, NF // 2) as i:
                for b in range(2):
                    pe.wait_ge(w13_landed[b], 32 * (n * NF // 2 + i + 1))
                    pe.wait_ge(hidden_ready, n * NF + 2 * i + b + 1)
                    for g in range(2):
                        for k in range(KT):
                            for s in range(2):
                                mm = pe.matmul(PS[:, 4 * b + 2 * g + s, 0:half], w13_buf[:, b, k, g, :],
                                               xn[:, k, a + s * half:a + (s + 1) * half],
                                               start=(k == 0), stop=(k == KT - 1))
                    mm.then_inc(hidden_summed, 1)
            pe.wait_ge(hidden_ready, 2 + (n + 1) * NF)
            with pe.Fori(0, KT // 2) as i:
                for b in range(2):
                    pe.wait_ge(w2_landed[b], 16 * (n * KT // 2 + i + 1))
                    pe.wait_ge(ffn_added, n * KT + 2 * i + b + 1)
                    for f in range(NF):
                        for s, (a0, w) in enumerate(segs):
                            mm = pe.matmul(PS[:, 4 * b + s, 0:w], w2_buf[:, b, f, :], hidden[:, f, a0:a0 + w],
                                           start=(f == 0), stop=(f == NF - 1))
                    mm.then_inc(ffn_summed, 1)

        def act_ffn(act, n, segs):
            a = segs[0][0]
            half = (T - a) // 2
            with act.Fori(0, NF // 2) as i:
                for b in range(2):
                    act.wait_ge(hidden_summed, 2 + n * NF + 2 * i + b + 1)
                    act.wait_ge(hidden_ready, n * NF + 2 * i + b + 1)
                    nc.scalar.activation(silu_buf[:, b, a:T].rearrange("p (s w) -> p s w", s=2),
                                         PS[:, 4 * b:4 * b + 2, 0:half], ACT.Silu).then_inc(silu_ready, 1)

        def dve_ffn(dve, n, segs, which):
            if n == 0:
                dve.sem_inc(hidden_ready, 2)
                dve.sem_inc(ffn_added, 2)
            a = segs[0][0]
            half = (T - a) // 2
            with dve.Fori(0, NF // 2) as i:
                for b in range(2):
                    dve.wait_ge(silu_ready, n * NF + 2 * i + b + 1)
                    nc.vector.tensor_tensor(
                        hidden[:, bass.ds(2 * i + b, 1), a:T].rearrange("p o (s w) -> p (o s) w", s=2),
                        silu_buf[:, b, a:T].rearrange("p (s w) -> p s w", s=2), PS[:, 4 * b + 2:4 * b + 4, 0:half],
                        ALU.mult).then_inc(hidden_ready, 1)
            with dve.Fori(0, KT // 2) as i:
                for b in range(2):
                    dve.wait_ge(ffn_summed, 2 + n * KT + 2 * i + b + 1)
                    for s, (a0, w) in enumerate(segs):
                        at = 0 if a0 == 0 else 1
                        v = h[:, bass.ds(2 * i + b, 1), a0:a0 + w].rearrange("p o w -> p (o w)")
                        g = mod[:, bass.ds((3 * which + 2) * KT + 2 * i + b, 1), at:at + 1].rearrange("p o w -> p (o w)")
                        ins = nc.vector.scalar_tensor_tensor(v, PS[:, 4 * b + s, 0:w], g, v, ALU.mult, ALU.add)
                    ins.then_inc(ffn_added, 1)

        DNB = 4 * NB
        win_landed = [sem("win_landed0"), sem("win_landed1")]
        wab_landed = sem("wab_landed")
        proj_summed, proj_moved, pad_zeroed = sem("proj_summed"), sem("proj_moved"), sem("pad_zeroed")
        conv_step, conv_used = sem("conv_step"), sem("conv_used")
        ab_summed, ab_step, ab_act = sem("ab_summed"), sem("ab_step"), sem("ab_act")
        qk_squared, qk_summed, qk_rooted, qk_inverted, qk_scaled = (
            sem("qk_squared"), sem("qk_summed"), sem("qk_rooted"), sem("qk_inverted"), sem("qk_scaled"))

        def sp_proj_dn(sp, layer):
            w = w_in[layer].rearrange("(k p) n -> p k n", p=P)
            sp.dma_start(wab[:, :, :], w[:, :, 4 * DN_W:DN_IN]).then_inc(wab_landed, 16)
            sp.dma_start(dn_rows[:, 0, :], dn_a_log[layer].rearrange("d h -> (d h)").partition_broadcast(P)).then_inc(wab_landed, 16)
            sp.dma_start(dn_rows[:, 1, :], dn_dt_bias[layer].rearrange("d h -> (d h)").partition_broadcast(P)).then_inc(wab_landed, 16)
            with sp.Fori(0, DNB // 2) as i:
                for b in range(2):
                    sp.wait_ge(proj_summed, layer * (DNB + KT) + 2 * i + b + 1)
                    sp.dma_start(win_buf[:, b], w[:, :, bass.ds((2 * i + b) * P, P)]).then_inc(win_landed[b], 16)

        def pool_proj_dn(pool, layer):
            nc.gpsimd.memset(pad[:, :, :], 0.0).then_inc(pad_zeroed, 1)

        def pe_proj_dn(pe, layer):
            if layer == 0:
                pe.sem_inc(proj_summed, 2)
            with pe.Fori(0, DNB // 2) as i:
                for b in range(2):
                    pe.wait_ge(win_landed[b], 16 * (layer * (DNB + KT) // 2 + i + 1))
                    pe.wait_ge(proj_moved, layer * (DNB + KT) + 2 * i + b + 1)
                    for k in range(KT):
                        for s, (a, w) in enumerate(SEGS):
                            mm = pe.matmul(PS[:, 2 * b + s, 0:w], win_buf[:, b, k, :], xn[:, k, a:a + w],
                                           start=(k == 0), stop=(k == KT - 1))
                    mm.then_inc(proj_summed, 1)
            pe.wait_ge(wab_landed, 48 * (layer + 1))
            for t in range(6):
                for k in range(KT):
                    mm = pe.matmul(PS[:, 4, 16 * t:16 * t + 16], xn[:, k, t * P:(t + 1) * P], wab[:, k, :],
                                   start=(k == 0), stop=(k == KT - 1))
            mm.then_inc(ab_summed, 1)
            pe.wait_ge(ab_step, 16 * layer + 1)
            pe.matmul(PS[:, 5, 0:96], flip[:, :], ab_raw[:, :, :].rearrange("p a b -> p (a b)"),
                      start=True, stop=True).then_inc(ab_summed, 1)
            pe.wait_ge(ab_step, 16 * layer + 11)
            pe.matmul(PS[:, 6, 0:48], upto_incl[:, :], g_[:, :, :].rearrange("p a b -> p (a b)"),
                      start=True, stop=True).then_inc(ab_summed, 1)
            with pe.Fori(0, NB) as i:
                for b in range(2):
                    pe.wait_ge(qk_squared, layer * 2 * NB + 2 * i + b + 1)
                    pe.wait_ge(qk_rooted, layer * 2 * NB + 2 * i + b + 1)
                    for s, (a, w) in enumerate(SEGS):
                        mm = pe.matmul(PS[:, 2 * b + s, 0:w], ones[:, :], sq[:, b, a:a + w], start=True, stop=True)
                    mm.then_inc(qk_summed, 1)

        def act_proj_dn(act, layer):
            if layer == 0:
                act.sem_inc(proj_moved, 2)
                act.sem_inc(conv_used, 2)
                act.sem_inc(qk_rooted, 2)
            act.wait_ge(pad_zeroed, 2 * layer + 1)
            with act.Fori(0, 3 * NB // 2) as i:
                for b in range(2):
                    act.wait_ge(proj_summed, 2 + layer * (DNB + KT) + 2 * i + b + 1)
                    nc.scalar.activation(pad[:, b, 2:2 + CTX], PS[:, 2 * b, 0:CTX], ACT.Copy)
                    nc.scalar.activation(pad[:, b, 6 + CTX:6 + T], PS[:, 2 * b + 1, 0:SEQ], ACT.Copy).then_inc(proj_moved, 1)
                    act.wait_ge(conv_step, 5 * (layer * 3 * NB + 2 * i + b + 1))
                    m = bass.ds(2 * i + b, 1)
                    nc.scalar.activation(qkv[:, m, 0:CTX], conv[:, b:b + 1, 0:CTX], ACT.Silu)
                    nc.scalar.activation(qkv[:, m, CTX:T], conv[:, b:b + 1, 4 + CTX:4 + T], ACT.Silu).then_inc(conv_used, 1)
            with act.Fori(0, NB // 2) as i:
                for b in range(2):
                    act.wait_ge(proj_summed, 2 + layer * (DNB + KT) + 3 * NB + 2 * i + b + 1)
                    m = bass.ds(2 * i + b, 1)
                    nc.scalar.activation(zgate[:, m, 0:CTX], PS[:, 2 * b:2 * b + 1, 0:CTX], ACT.Silu)
                    nc.scalar.activation(zgate[:, m, CTX:T], PS[:, 2 * b + 1:2 * b + 2, 0:SEQ], ACT.Silu).then_inc(proj_moved, 1)
            a0, d0 = 4 * layer, 16 * layer
            act.wait_ge(wab_landed, 48 * (layer + 1))
            act.wait_ge(ab_step, d0 + 8)
            nc.scalar.activation(t48b[:, :], t48b[:, :], ACT.Exp, scale=-1.0).then_inc(ab_act, 1)
            act.wait_ge(ab_act, a0 + 1)
            nc.scalar.activation(t48b[:, :], t48b[:, :], ACT.Ln, bias=1.0)
            nc.scalar.activation(dn_rows[:, 0, :], dn_rows[:, 0, :], ACT.Exp).then_inc(ab_act, 1)
            nc.scalar.activation(bt[:, :, :], bt[:, :, :], ACT.Sigmoid).then_inc(ab_act, 1)
            act.wait_ge(ab_step, d0 + 12)
            nc.scalar.activation(begc[:, :, :], gcum[:, :, :], ACT.Exp).then_inc(ab_act, 1)
            act.wait_ge(conv_used, 2 + 3 * NB * (layer + 1))
            for part in range(2):
                n0 = layer * 2 * NB + part * NB
                with act.Fori(0, NB // 2) as i:
                    for b in range(2):
                        nc.scalar.activation(sq[:, b:b + 1, :], qkv[:, bass.ds(part * NB + 2 * i + b, 1), :],
                                             ACT.Square).then_inc(qk_squared, 1)
                    for b in range(2):
                        act.wait_ge(qk_summed, n0 + 2 * i + b + 1)
                        act.wait_ge(qk_scaled, n0 + 2 * i + b + 1)
                        for s, (a, w) in enumerate(SEGS):
                            ins = nc.scalar.activation(conv[:, b, a:a + w], PS[:, 2 * b + s, 0:w], ACT.Sqrt,
                                                       scale=float(P) if part == 0 else 1.0,
                                                       bias=eps[:, 2:3] if part == 0 else eps[:, 0:1])
                        ins.then_inc(qk_rooted, 1)

        def dve_proj_dn(dve, layer):
            v = nc.vector
            if layer == 0:
                dve.sem_inc(qk_scaled, 2)
            with dve.Fori(0, 3 * NB // 2) as i:
                for b in range(2):
                    n = layer * 3 * NB + 2 * i + b
                    dve.wait_ge(proj_moved, 2 + layer * (DNB + KT) + 2 * i + b + 1)
                    dve.wait_ge(conv_used, n + 1)
                    tap = lambda t: prm[:, layer, 1, bass.ds(B_CONV + t * 3 * NB + 2 * i + b, 1)]
                    v.tensor_scalar(conv[:, b, 0:772], pad[:, b, 0:772], tap(0), None, ALU.mult).then_inc(conv_step, 1)
                    for t in range(1, 5):
                        dve.wait_ge(conv_step, 5 * n + t)
                        v.scalar_tensor_tensor(conv[:, b, 0:772], pad[:, b, t:t + 772], tap(t), conv[:, b, 0:772],
                                               ALU.mult, ALU.add).then_inc(conv_step, 1)
            d0, H = 16 * layer, DN_H
            F = PS[:, 5, 0:96].rearrange("p (t c) -> p t c", c=16)
            dve.wait_ge(ab_summed, 3 * layer + 1)
            v.tensor_copy(ab_raw[:, :, :].rearrange("p a b -> p (a b)"), PS[:, 4, 0:96]).then_inc(ab_step, 1)
            dve.wait_ge(ab_step, d0 + 1)
            dve.wait_ge(ab_summed, 3 * layer + 2)
            v.tensor_copy(ag[:, :, 0:H], ab_raw[:, :, 0:H])
            v.tensor_copy(bt[:, :, 0:H], ab_raw[:, :, 2 * H:3 * H])
            v.tensor_copy(ag[:, 0:2, H:2 * H], F[:, 1::-1, H:2 * H])
            v.tensor_copy(ag[:, 2:6, H:2 * H], F[:, 5:1:-1, H:2 * H])
            v.tensor_copy(bt[:, 0:2, H:2 * H], F[:, 1::-1, 3 * H:4 * H])
            v.tensor_copy(bt[:, 2:6, H:2 * H], F[:, 5:1:-1, 3 * H:4 * H]).then_inc(ab_step, 1)
            dve.wait_ge(ab_step, d0 + 2)
            dve.wait_ge(wab_landed, 48 * (layer + 1))
            t48a3, t48b3 = t48a.rearrange("p (s u) -> p s u", u=8), t48b.rearrange("p (s u) -> p s u", u=8)
            v.tensor_tensor(t48a3, ag[:, :, :], bc(dn_rows[:, 1, :], 1, [P, 6, 8]), ALU.add).then_inc(ab_step, 1)
            dve.wait_ge(ab_step, d0 + 3)
            v.scalar_tensor_tensor(t48b[:, :], t48a[:, :], -1.0, t48a[:, :], ALU.mult, ALU.max).then_inc(ab_step, 5)
            dve.wait_ge(ab_act, 4 * layer + 2)
            v.scalar_tensor_tensor(t48a[:, :], t48a[:, :], 0.0, t48b[:, :], ALU.max, ALU.add).then_inc(ab_step, 1)
            dve.wait_ge(ab_step, d0 + 9)
            v.scalar_tensor_tensor(g_[:, :, :], t48a3, -1.0, bc(dn_rows[:, 0, :], 1, [P, 6, 8]),
                                   ALU.mult, ALU.mult).then_inc(ab_step, 2)
            dve.wait_ge(ab_summed, 3 * layer + 3)
            v.tensor_copy(gcum[:, :, :].rearrange("p a b -> p (a b)"), PS[:, 6, 0:48]).then_inc(ab_step, 1)
            dve.wait_ge(ab_act, 4 * layer + 4)
            v.tensor_tensor(begc[:, :, :], begc[:, :, :], bt[:, :, :], ALU.mult).then_inc(ab_step, 4)
            with dve.Fori(0, NB) as i:
                for b in range(2):
                    n = layer * 2 * NB + 2 * i + b
                    dve.wait_ge(qk_rooted, 2 + n + 1)
                    v.reciprocal(conv[:, b, 0:T], conv[:, b, 0:T]).then_inc(qk_inverted, 1)
                    dve.wait_ge(qk_inverted, n + 1)
                    q = qkv[:, bass.ds(2 * i + b, 1), :]
                    v.tensor_tensor(q, q, conv[:, b:b + 1, 0:T], ALU.mult).then_inc(qk_scaled, 1)

        def dnbuf(n, g):
            return region(27648 + (2 * n + g) * 512, DN_H, P)

        NAMES = "KT QD VT UG EB DM DMT KTOK VTOK AT X Y S AV".split()
        dn = {name: [dnbuf(n, g) for g in range(2)] for n, name in enumerate(NAMES)}
        KTc, QD, VT, UG, EB, DM, DMT, KTOK, VTOK, AT, X, Y, S, AV = (dn[n] for n in NAMES)
        LEVELS_DN, LEVELS_RW = 7, 6
        STEPS = 6 + RW_CHUNKS
        XS = 6 * LEVELS_DN + RW_CHUNKS * LEVELS_RW
        TS = XS - STEPS

        def dsem(name):
            return [sem(f"{name}{g}") for g in range(2)]

        k_built, q_built, v_built, ug_built = dsem("k_built"), dsem("q_built"), dsem("v_built"), dsem("ug_built")
        gc_spread, kk_ready, kq_ready = dsem("gc_spread"), dsem("kk_ready"), dsem("kq_ready")
        ktok_ready, vtok_ready = dsem("ktok_ready"), dsem("vtok_ready")
        ktok_moved, vtok_moved = dsem("ktok_moved"), dsem("vtok_moved")
        eb_ready, dd_ready, dd_split, dm_ready, dm_weighted = (
            dsem("eb_ready"), dsem("dd_ready"), dsem("dd_split"), dsem("dm_ready"), dsem("dm_weighted"))
        q_decayed, v_weighted, k_decayed = dsem("q_decayed"), dsem("v_weighted"), dsem("k_decayed")
        a_ready, attn_ready = dsem("a_ready"), dsem("attn_ready")
        at_turned, at_moved = dsem("at_turned"), dsem("at_moved")
        tx_summed, tx_masked, xd_summed, x_ready, x_turned, y_ready = (
            dsem("tx_summed"), dsem("tx_masked"), dsem("xd_summed"), dsem("x_ready"), dsem("x_turned"), dsem("y_ready"))
        ks_ready, r_ready, vn_summed, vn_ready, s_summed, o_summed = (
            dsem("ks_ready"), dsem("r_ready"), dsem("vn_summed"), dsem("vn_ready"), dsem("s_summed"), dsem("o_summed"))
        s_updated, o_added, x0_step = dsem("s_updated"), dsem("o_added"), dsem("x0_step")
        kst_ready, s_scaled = dsem("kst_ready"), dsem("s_scaled")

        def dn_loops(layer):
            for (a, w), first in zip(SEGS, (0, CTX // DN_C)):
                yield first, w // DN_C, a, w

        def pool_dn(pool, layer):
            gp = nc.gpsimd
            for g in range(2):
                gp.memset(S[g], 0.0).then_inc(s_updated[g], 1)
            gp.memset(dn_o[:, :, :], 0.0).then_inc(o_added[0], 1)
            for first, steps, a, w in dn_loops(layer):
                with pool.Fori(0, steps) as i:
                    it, own = STEPS * layer + first + i, 6 * layer + first + i
                    for g in range(2):
                        pool.wait_ge(o_added[g], own + (layer + 1 if g == 0 else 1))
                        pool.wait_ge(s_updated[g], it + 2 * layer + 1)

                        def chunk(part):
                            v = qkv[:, part * NB:(part + 1) * NB, a:a + w]
                            return v[:, :, bass.ds(i * DN_C if g == 0 else w - DN_C - i * DN_C, DN_C)]

                        def way(t):
                            return t if g == 0 else t[:, :, ::-1]
                        u = slice(g * DN_H, (g + 1) * DN_H)
                        gp.tensor_tensor(UG[g], bc(upto_incl[:, :], 1, [P, DN_H, P]),
                                         bc(g_[:, bass.ds(first + i, 1), u].rearrange("p o u -> p (o u)"), 2, [P, DN_H, P]),
                                         ALU.mult).then_inc(ug_built[g], 1)
                        gp.tensor_copy(way(KTc[g]), chunk(1)).then_inc(k_built[g], 1)
                        gp.tensor_copy(way(QD[g]), chunk(0)).then_inc(q_built[g], 1)
                        gp.tensor_copy(way(VT[g]), chunk(2)).then_inc(v_built[g], 1)
                    for g in range(2):
                        u = slice(g * DN_H, (g + 1) * DN_H)
                        row = lambda t: bc(t[:, bass.ds(first + i, 1), u].rearrange("p o u -> p (o u)"), 2, [P, DN_H, P])
                        pool.wait_ge(dm_ready[g], own + 1)
                        gp.tensor_tensor(DM[g], DM[g], row(bt), ALU.mult).then_inc(dm_weighted[g], 1)
                        pool.wait_ge(ktok_moved[g], it + 1)
                        gp.tensor_tensor(KTOK[g], KTOK[g], DMT[g][:, :, P - 1:P].broadcast_to([P, DN_H, P]),
                                         ALU.mult).then_inc(k_decayed[g], 1)
                        pool.wait_ge(k_decayed[g], own + 1)
                        gp.tensor_tensor(DMT[g], DMT[g], bc(upto_incl[:, :], 1, [P, DN_H, P]), ALU.mult).then_inc(dm_weighted[g], 1)
                        pool.wait_ge(eb_ready[g], it + 1)
                        pool.wait_ge(q_built[g], own + 1)
                        pool.wait_ge(kq_ready[g], it + 1)
                        gp.tensor_tensor(QD[g], QD[g], EB[g], ALU.mult).then_inc(q_decayed[g], 1)
                        pool.wait_ge(phase_done, 4)
                        pool.wait_ge(vtok_moved[g], it + 1)
                        gp.tensor_tensor(VTOK[g], VTOK[g], row(bt), ALU.mult).then_inc(v_weighted[g], 1)

        def pe_dn(pe, layer):
            for first, steps, a, w in dn_loops(layer):
                with pe.Fori(0, steps) as i:
                    it, own = STEPS * layer + first + i, 6 * layer + first + i
                    for g in range(2):
                        c = 4 * g
                        pe.wait_ge(ug_built[g], it + 1)
                        pe.matmul(PS[:, c, :], ones[:, :], UG[g].rearrange("p a b -> p (a b)"),
                                  start=True, stop=True).then_inc(gc_spread[g], 1)
                        pe.wait_ge(k_built[g], it + 1)
                        for u in range(DN_H):
                            mm = pe.matmul(PS[:, c + 1, u * P:(u + 1) * P], KTc[g][:, u, :], KTc[g][:, u, :], start=True, stop=True)
                        mm.then_inc(kk_ready[g], 1)
                        pe.wait_ge(q_built[g], own + 1)
                        for u in range(DN_H):
                            mm = pe.matmul(PS[:, c + 2, u * P:(u + 1) * P], KTc[g][:, u, :], QD[g][:, u, :], start=True, stop=True)
                        mm.then_inc(kq_ready[g], 1)
                        for u in range(DN_H):
                            mm = pe.transpose(PS[:, c + 3, u * P:(u + 1) * P], KTc[g][:, u, :], ident[:, :])
                        mm.then_inc(ktok_ready[g], 1)
                    for g in range(2):
                        c = 4 * g
                        pe.wait_ge(v_built[g], it + 1)
                        pe.wait_ge(eb_ready[g], it + 1)
                        pe.wait_ge(dd_ready[g], it + 1)
                        for u in range(DN_H):
                            mm = pe.transpose(PS[:, c, u * P:(u + 1) * P], VT[g][:, u, :], ident[:, :])
                        mm.then_inc(vtok_ready[g], 1)
                    for g in range(2):
                        c = 4 * g
                        pe.wait_ge(a_ready[g], it + 1)
                        pe.wait_ge(ktok_moved[g], it + 1)
                        for u in range(DN_H):
                            mm = pe.transpose(PS[:, c + 3, u * P:(u + 1) * P], DM[g][:, u, :], ident[:, :])
                        mm.then_inc(at_turned[g], 1)
                    n = LEVELS_DN
                    for l in range(n):
                        if l > 0:
                            for g in range(2):
                                c = 4 * g
                                pe.wait_ge(x_ready[g], XS * layer + n * (first + i) + l)
                                if l == 1:
                                    pe.wait_ge(at_moved[g], it + 1)
                                for u in range(DN_H):
                                    mm = pe.matmul(PS[:, c + 1, u * P:(u + 1) * P], AT[g][:, u, :], X[g][:, u, :], start=True, stop=True)
                                mm.then_inc(tx_summed[g], 1)
                            for g in range(2):
                                c = 4 * g
                                pe.wait_ge(tx_masked[g], TS * layer + (n - 1) * (first + i) + l)
                                pe.wait_ge(y_ready[g], XS * layer + n * (first + i) + l)
                                if l == 1:
                                    pe.wait_ge(attn_ready[g], it + 1)
                                for u in range(DN_H):
                                    mm = pe.matmul(PS[:, c + 2, u * P:(u + 1) * P], Y[g][:, u, :], UG[g][:, u, :], start=True, stop=True)
                                mm.then_inc(xd_summed[g], 1)
                        for g in range(2):
                            c = 4 * g
                            pe.wait_ge(x_ready[g], XS * layer + n * (first + i) + l + 1)
                            if l == 0:
                                pe.wait_ge(vtok_moved[g], it + 1)
                            for u in range(DN_H):
                                mm = pe.transpose(PS[:, c, u * P:(u + 1) * P], X[g][:, u, :], ident[:, :])
                            mm.then_inc(x_turned[g], 1)
                        if l == 0:
                            for g in range(2):
                                pe.wait_ge(s_updated[g], it + 2 * layer + 1)
                                pe.wait_ge(at_moved[g], it + 1)
                                for u in range(DN_H):
                                    mm = pe.matmul(PS[:, 4 * g + 3, u * P:(u + 1) * P], KTc[g][:, u, :], S[g][:, u, :], start=True, stop=True)
                                mm.then_inc(ks_ready[g], 1)
                    for g in range(2):
                        c = 4 * g
                        pe.wait_ge(y_ready[g], XS * layer + n * (first + i) + n)
                        pe.wait_ge(r_ready[g], it + 1)
                        for u in range(DN_H):
                            mm = pe.matmul(PS[:, c + 1, u * P:(u + 1) * P], Y[g][:, u, :], VTOK[g][:, u, :], start=True, stop=True)
                        mm.then_inc(vn_summed[g], 1)
                    for g in range(2):
                        c = 4 * g
                        pe.wait_ge(vn_ready[g], it + 1)
                        pe.wait_ge(k_decayed[g], own + 1)
                        pe.wait_ge(q_decayed[g], it + 1)
                        for u in range(DN_H):
                            mm = pe.matmul(PS[:, c + 2, u * P:(u + 1) * P], KTOK[g][:, u, :], AV[g][:, u, :], start=True, stop=True)
                        mm.then_inc(s_summed[g], 1)
                        for u in range(DN_H):
                            pe.matmul(PS[:, c + 3, u * P:(u + 1) * P], S[g][:, u, :], QD[g][:, u, :], start=True, stop=False)
                            mm = pe.matmul(PS[:, c + 3, u * P:(u + 1) * P], AV[g][:, u, :], DMT[g][:, u, :], start=False, stop=True)
                        mm.then_inc(o_summed[g], 1)

        def bank(b):
            return PS[:, b, :].rearrange("p (u t) -> p u t", u=4)

        def act_dn(act, layer):
            sc = nc.scalar
            n = LEVELS_DN
            for first, steps, a, w in dn_loops(layer):
                with act.Fori(0, steps) as i:
                    it, own = STEPS * layer + first + i, 6 * layer + first + i
                    for g in range(2):
                        act.wait_ge(gc_spread[g], own + 1)
                        sc.activation(EB[g], bank(4 * g), ACT.Exp).then_inc(eb_ready[g], 1)
                    for g in range(2):
                        act.wait_ge(dd_split[g], 2 * own + 2)
                        sc.activation(DM[g], DM[g], ACT.Exp, scale=-1.0)
                        sc.activation(DMT[g], DMT[g], ACT.Exp).then_inc(dm_ready[g], 1)
                        act.wait_ge(ktok_ready[g], it + 1)
                        sc.activation(KTOK[g], bank(4 * g + 3), ACT.Copy).then_inc(ktok_moved[g], 1)
                        act.wait_ge(vtok_ready[g], it + 1)
                        sc.activation(VTOK[g], bank(4 * g), ACT.Copy).then_inc(vtok_moved[g], 1)
                    for g in range(2):
                        act.wait_ge(at_turned[g], it + 1)
                        sc.activation(AT[g], bank(4 * g + 3), ACT.Copy).then_inc(at_moved[g], 1)
                    for l in range(n):
                        for g in range(2):
                            act.wait_ge(x_turned[g], XS * layer + n * (first + i) + l + 1)
                            if l > 0:
                                act.wait_ge(xd_summed[g], TS * layer + (n - 1) * (first + i) + l)
                            sc.activation(Y[g], bank(4 * g), ACT.Copy).then_inc(y_ready[g], 1)
                    for g in range(2):
                        act.wait_ge(vn_summed[g], it + 1)
                        sc.activation(AV[g], bank(4 * g + 1), ACT.Copy).then_inc(vn_ready[g], 1)

        def dve_dn(dve, layer):
            v = nc.vector
            n = LEVELS_DN
            if layer == 0:
                dve.sem_inc(o_added[1], 1)
            for first, steps, a, w in dn_loops(layer):
                with dve.Fori(0, steps) as i:
                    it, own = STEPS * layer + first + i, 6 * layer + first + i
                    for g in range(2):
                        u = slice(g * DN_H, (g + 1) * DN_H)
                        row = lambda t: bc(t[:, bass.ds(first + i, 1), u].rearrange("p o u -> p (o u)"), 2, [P, DN_H, P])
                        dve.wait_ge(eb_ready[g], it + 1)
                        v.tensor_tensor(AV[g], bank(4 * g), row(gcum), ALU.subtract).then_inc(dd_ready[g], 1)
                        dve.wait_ge(dd_ready[g], it + 1)
                        v.tensor_scalar(DM[g], AV[g], 0.0, None, ALU.max).then_inc(dd_split[g], 1)
                        v.tensor_scalar(DMT[g], AV[g], 0.0, None, ALU.min).then_inc(dd_split[g], 1)
                    for g in range(2):
                        dve.wait_ge(dm_weighted[g], 2 * own + 1)
                        dve.wait_ge(kk_ready[g], it + 1)
                        v.tensor_tensor(DM[g], DM[g], bank(4 * g + 1), ALU.mult).then_inc(a_ready[g], 1)
                        dve.wait_ge(a_ready[g], it + 1)
                        v.tensor_tensor(X[g], DM[g], bc(level[:, 0, :], 1, [P, DN_H, P]), ALU.mult).then_inc(x0_step[g], 1)
                        dve.wait_ge(x0_step[g], it + 1)
                        v.tensor_tensor(X[g], bc(ident[:, :], 1, [P, DN_H, P]), X[g], ALU.subtract).then_inc(x_ready[g], 1)
                        dve.wait_ge(dm_weighted[g], 2 * own + 2)
                        dve.wait_ge(kq_ready[g], it + 1)
                        v.tensor_tensor(DMT[g], DMT[g], bank(4 * g + 2), ALU.mult).then_inc(attn_ready[g], 1)
                    for l in range(1, n):
                        for g in range(2):
                            dve.wait_ge(tx_summed[g], TS * layer + (n - 1) * (first + i) + l)
                            v.tensor_tensor(UG[g], bank(4 * g + 1), bc(level[:, l, :], 1, [P, DN_H, P]),
                                            ALU.mult).then_inc(tx_masked[g], 1)
                        for g in range(2):
                            dve.wait_ge(xd_summed[g], TS * layer + (n - 1) * (first + i) + l)
                            dve.wait_ge(x_turned[g], XS * layer + n * (first + i) + l)
                            v.tensor_tensor(X[g], X[g], bank(4 * g + 2), ALU.subtract).then_inc(x_ready[g], 1)
                        if l == 1:
                            for g in range(2):
                                u = slice(g * DN_H, (g + 1) * DN_H)
                                row = lambda t: bc(t[:, bass.ds(first + i, 1), u].rearrange("p o u -> p (o u)"), 2, [P, DN_H, P])
                                dve.wait_ge(ks_ready[g], it + 1)
                                v.tensor_tensor(AV[g], bank(4 * g + 3), row(begc), ALU.mult).then_inc(kst_ready[g], 1)
                    for g in range(2):
                        dve.wait_ge(v_weighted[g], it + 1)
                        dve.wait_ge(kst_ready[g], it + 1)
                        v.tensor_tensor(VTOK[g], VTOK[g], AV[g], ALU.subtract).then_inc(r_ready[g], 1)
                    for g in range(2):
                        dve.wait_ge(o_summed[g], it + 1)
                        v.tensor_tensor(S[g], S[g], EB[g][:, :, P - 1:P].broadcast_to([P, DN_H, P]), ALU.mult).then_inc(s_scaled[g], 1)
                    for g in range(2):
                        o = dn_o[:, :, a:a + w][:, :, bass.ds(i * DN_C if g == 0 else w - DN_C - i * DN_C, DN_C)]
                        new = bank(4 * g + 3) if g == 0 else bank(4 * g + 3)[:, :, ::-1]
                        dve.wait_ge(phase_done, 4)
                        dve.wait_ge(o_added[0], own + layer + 1)
                        dve.wait_ge(o_added[1], own + 1)
                        v.tensor_tensor(o, o, new, ALU.add).then_inc(o_added[g], 1)
                        dve.wait_ge(s_scaled[g], it + 1)
                        v.tensor_tensor(S[g], S[g], bank(4 * g + 2), ALU.add).then_inc(s_updated[g], 1)

        ho_squared, ho_summed, ho_rooted, ho_step, mix_saved, h_saved = (
            sem("ho_squared"), sem("ho_summed"), sem("ho_rooted"), sem("ho_step"), sem("mix_saved"), sem("h_saved"))

        def act_dn_out(act, layer):
            for u in range(DN_H):
                n = 2 * DN_H * layer + u
                if u >= 2:
                    act.wait_ge(ho_summed, n - 1)
                nc.scalar.activation(sq[:, u % 2, :], dn_o[:, u, :], ACT.Square).then_inc(ho_squared, 1)
            for u in range(DN_H):
                n = 2 * DN_H * layer + u
                act.wait_ge(ho_summed, n + 1)
                if u >= 2:
                    act.wait_ge(ho_step, 3 * (layer * DN_H + u - 2) + 2)
                for s, (a, w) in enumerate(SEGS):
                    ins = nc.scalar.activation(conv[:, u % 2, a:a + w], PS[:, 2 * u + s, 0:w], ACT.Sqrt,
                                               scale=1.0 / P, bias=eps[:, 0:1])
                ins.then_inc(ho_rooted, 1)

        def pe_dn_out(pe, layer):
            for u in range(DN_H):
                pe.wait_ge(ho_squared, 2 * DN_H * layer + u + 1)
                for s, (a, w) in enumerate(SEGS):
                    mm = pe.matmul(PS[:, 2 * u + s, 0:w], ones[:, :], sq[:, u % 2, a:a + w], start=True, stop=True)
                mm.then_inc(ho_summed, 1)

        def dve_dn_out(dve, layer):
            for u in range(DN_H):
                n = 2 * DN_H * layer + u
                dve.wait_ge(ho_rooted, n + 1)
                nc.vector.reciprocal(conv[:, u % 2, 0:T], conv[:, u % 2, 0:T]).then_inc(ho_step, 1)
                dve.wait_ge(ho_step, 3 * (layer * DN_H + u) + 1)
                nc.vector.tensor_tensor(dn_o[:, u, :], dn_o[:, u, :], conv[:, u % 2, 0:T], ALU.mult).then_inc(ho_step, 1)
                dve.wait_ge(ho_step, 3 * (layer * DN_H + u) + 2)
                nc.vector.scalar_tensor_tensor(zgate[:, u, :], dn_o[:, u, :], prm[:, layer, 0, A_DNN:A_DNN + 1],
                                               zgate[:, u, :], ALU.mult, ALU.mult).then_inc(ho_step, 1)

        def sp_save_h(sp, layer):
            sp.dma_start(h_save, h[:, :, :].rearrange("p a b -> p (a b)")).then_inc(h_saved, 16)
            sp.wait_ge(h_saved, 16 * (layer + 1))

        def sp_save_mix(sp, layer):
            sp.dma_start(mix_save, zgate[:, :, :].rearrange("p a b -> p (a b)")).then_inc(mix_saved, 16)
            sp.wait_ge(mix_saved, 16 * (layer + 1))

        RB = 15
        rproj = region(12288, RB, T)
        R_, K_, V_ = rproj[:, 0:NB], rproj[:, NB:2 * NB], rproj[:, 2 * NB:3 * NB]
        lora_w, lora_a, lora_g = rproj[:, 12], rproj[:, 13], rproj[:, 14]
        winr_buf = region(43776, 3, KT, P)
        pad3 = region(36864, 3, 776)
        shifted = region(39192, 772)
        winr_landed = [sem(f"winr_landed{b}") for b in range(3)]
        rproj_summed, rproj_moved, shift_step = (
            sem("rproj_summed"), sem("rproj_moved"), sem("shift_step"))

        def sp_proj_rw(sp, layer):
            w = w_in[layer].rearrange("(k p) n -> p k n", p=P)
            with sp.Fori(0, RB // 3) as i:
                for b in range(3):
                    sp.wait_ge(rproj_summed, layer * RB + 3 * i + b + 1)
                    sp.dma_start(winr_buf[:, b], w[:, :, bass.ds((3 * i + b) * P + DN_IN, P)]).then_inc(winr_landed[b], 16)

        def pool_proj_rw(pool, layer):
            nc.gpsimd.memset(pad3[:, :, :], 0.0).then_inc(pad_zeroed, 1)

        def pe_proj_rw(pe, layer):
            if layer == 0:
                pe.sem_inc(rproj_summed, 3)
            with pe.Fori(0, RB // 3) as i:
                for b in range(3):
                    pe.wait_ge(winr_landed[b], 16 * (layer * RB // 3 + i + 1))
                    pe.wait_ge(rproj_moved, layer * RB + 3 * i + b + 1)
                    for k in range(KT):
                        for s, (a, w) in enumerate(SEGS):
                            mm = pe.matmul(PS[:, 2 * b + s, 0:w], winr_buf[:, b, k, :], xn[:, k, a:a + w],
                                           start=(k == 0), stop=(k == KT - 1))
                    mm.then_inc(rproj_summed, 1)

        def act_proj_rw(act, layer):
            if layer == 0:
                act.sem_inc(rproj_moved, 3)
            act.wait_ge(pad_zeroed, 2 * layer + 2)
            with act.Fori(0, RB // 3) as i:
                for b in range(3):
                    n = layer * RB + 3 * i + b
                    act.wait_ge(rproj_summed, 3 + n + 1)
                    if b == 0:
                        act.wait_ge(shift_step, 3 * (layer * RB + 3 * i) + 3)
                    nc.scalar.activation(pad3[:, b, 1:1 + CTX], PS[:, 2 * b, 0:CTX], ACT.Copy)
                    nc.scalar.activation(pad3[:, b, 3 + CTX:3 + T].rearrange("p (c r) -> p r c", r=GRID_H),
                                         PS[:, 2 * b + 1, 0:SEQ].rearrange("p (r c) -> p r c", r=GRID_H),
                                         ACT.Copy).then_inc(rproj_moved, 1)

        def dve_proj_rw(dve, layer):
            v = nc.vector
            if layer == 0:
                dve.sem_inc(shift_step, 3)
            with dve.Fori(0, RB // 3) as i:
                for b in range(3):
                    n = layer * RB + 3 * i + b
                    m = 3 * i + b
                    dve.wait_ge(rproj_moved, 3 + n + 1)
                    dve.wait_ge(shift_step, 3 * n + 3)
                    v.tensor_scalar(shifted[:, 0:770], pad3[:, b, 1:771], drv[:, bass.ds(m, 1)], None,
                                    ALU.mult).then_inc(shift_step, 1)
                    dve.wait_ge(shift_step, 3 * n + 4)
                    v.scalar_tensor_tensor(shifted[:, 0:770], pad3[:, b, 0:770], prm[:, layer, 1, bass.ds(B_MU + m, 1)],
                                           shifted[:, 0:770], ALU.mult, ALU.add).then_inc(shift_step, 1)
                    dve.wait_ge(shift_step, 3 * n + 5)
                    for at, off, w in ((0, 0, CTX), (CTX, CTX + 2, SEQ)):
                        ins = v.scalar_tensor_tensor(rproj[:, bass.ds(m, 1), at:at + w].rearrange("p o w -> p (o w)"),
                                                     pad3[:, b, off + 2:off + 2 + w],
                                                     prm[:, layer, 1, bass.ds(B_MU + RB + m, 1)], shifted[:, off:off + w],
                                                     ALU.mult, ALU.add)
                    ins.then_inc(shift_step, 1)

        KK = region(24576, NB, T)
        KP = [region(0, NB, T), region(38400, NB, T)]
        KKP = [region(3072, NB, T), region(23808, NB, T)]
        RP = [region(6144, NB, T), region(41472, NB, T)]
        BP = [region(9216, NB, T), region(27648, NB, T)]
        VF = region(30720, NB, T)
        BON = region(33792, NB, T)
        g2w = region(36864, RW_W)
        w2w = region(37376, RW_W)
        a2w = region(37888, RW_W)
        SG_, AA, G_, E1, E2, KD = (region(44544 + n * T, T) for n in range(6))
        PC = sb("PC", [P, 2, NB, RW_CHUNKS])
        lora_landed = sem("lora_landed")
        kk_step = sem("kk_step")
        kk_squared, kk_summed, kk_rooted = ho_squared, ho_summed, ho_rooted
        K0 = lambda layer: 2 * NB * layer + NB
        lora_acted, lora_summed, gates_ready, fe_exp, fe_dve, fe_pool = (
            sem("lora_acted"), sem("lora_summed"), sem("gates_ready"), sem("fe_exp"), sem("fe_dve"), sem("fe_pool"))

        def sp_feat(sp, layer):
            sp.dma_start(g2w, rw_g2[layer]).then_inc(lora_landed, 16)
            sp.dma_start(w2w, rw_w2[layer].rearrange("d r c -> (d r) c")).then_inc(lora_landed, 16)
            sp.dma_start(a2w, rw_a2[layer].rearrange("d r c -> (d r) c")).then_inc(lora_landed, 16)

        bonus_summed = sem("bonus_summed")

        def act_feat(act, layer):
            sc = nc.scalar
            sc.activation(lora_w, lora_w, ACT.Tanh)
            sc.activation(lora_g, lora_g, ACT.Sigmoid).then_inc(lora_acted, 1)
            for j in range(NB):
                n, m = NB * layer + j, K0(layer) + j
                act.wait_ge(kk_step, 3 * n + 1)
                if j >= 2:
                    act.wait_ge(kk_summed, m - 1)
                sc.activation([E1, E2][j % 2], KK[:, j, :], ACT.Square).then_inc(kk_squared, 1)
                act.wait_ge(kk_summed, m + 1)
                if j >= 1:
                    act.wait_ge(kk_step, 3 * n)
                for s, (a, w) in enumerate(SEGS):
                    ins = sc.activation(KD[:, a:a + w], PS[:, s, 0:w], ACT.Sqrt, bias=eps[:, 0:1])
                ins.then_inc(kk_rooted, 1)
            act.wait_ge(h_saved, 16 * (layer + 1))
            for u in range(2 * NB):
                j, d = u // 2, u % 2
                n = 2 * NB * layer + u
                act.wait_ge(lora_summed, n + 1)
                if u >= 1:
                    act.wait_ge(fe_pool, 4 * n)
                    act.wait_ge(fe_dve, 8 * n)
                c = 4 * (u % 2)
                for s, (a, w) in enumerate(SEGS):
                    sc.activation(SG_[:, a:a + w], PS[:, c + s, 0:w], ACT.Sigmoid,
                                  bias=prm[:, layer, 1, B_W0 + d * NB + j:B_W0 + d * NB + j + 1])
                    ins = sc.activation(AA[:, a:a + w], PS[:, c + 2 + s, 0:w], ACT.Sigmoid,
                                        bias=prm[:, layer, 1, B_A0 + d * NB + j:B_A0 + d * NB + j + 1])
                ins.then_inc(gates_ready, 1)
                act.wait_ge(fe_dve, 8 * n + 1)
                sc.activation(E1, G_, ACT.Exp, scale=-DECAY_SCALE).then_inc(fe_exp, 1)
                sc.activation(E2, G_, ACT.Exp, scale=DECAY_SCALE).then_inc(fe_exp, 1)
                last = G_[:, RW_C - 1::RW_C] if d == 0 else G_[:, 0::RW_C]
                pc = PC[:, d, j, :] if d == 0 else PC[:, d, j, ::-1]
                sc.activation(pc, last, ACT.Exp, scale=-DECAY_SCALE).then_inc(fe_exp, 1)
                act.wait_ge(fe_dve, 8 * n + 2)
                sc.activation(SG_, SG_, ACT.Exp, scale=-DECAY_SCALE).then_inc(fe_exp, 1)

        def pe_feat(pe, layer):
            for j in range(NB):
                m = K0(layer) + j
                pe.wait_ge(kk_squared, m + 1)
                if j >= 1:
                    pe.wait_ge(kk_rooted, m)
                for s, (a, w) in enumerate(SEGS):
                    mm = pe.matmul(PS[:, s, 0:w], headones[:, :], [E1, E2][j % 2][:, a:a + w], start=True, stop=True)
                mm.then_inc(kk_summed, 1)
            pe.wait_ge(lora_landed, 48 * (layer + 1))
            pe.wait_ge(lora_acted, layer + 1)
            pe.wait_ge(kk_rooted, K0(layer) + NB)
            for u in range(2 * NB):
                j, d = u // 2, u % 2
                n = 2 * NB * layer + u
                if u >= 2:
                    pe.wait_ge(gates_ready, n - 1)
                c = 4 * (u % 2)
                rows = slice(64 * d, 64 * d + 64)
                for o, (wt, src) in enumerate(((w2w, lora_w), (a2w, lora_a))):
                    for s, (a, w) in enumerate(SEGS):
                        mm = pe.matmul(PS[:, c + 2 * o + s, 0:w], wt[rows, j * P:(j + 1) * P], src[rows, a:a + w],
                                       start=True, stop=True)
                mm.then_inc(lora_summed, 1)
            for j in range(NB):
                n = NB * layer + j
                pe.wait_ge(fe_dve, 8 * (2 * NB * layer + 2 * j + 2))
                if j == 0:
                    pe.wait_ge(gates_ready, 2 * NB * (layer + 1))
                for s, (a, w) in enumerate(SEGS):
                    mm = pe.matmul(PS[:, 2 * j + s, 0:w], headones[:, :], BON[:, j, a:a + w], start=True, stop=True)
                mm.then_inc(bonus_summed, 1)

        def dve_feat(dve, layer):
            v = nc.vector
            for j in range(NB):
                v.tensor_scalar(KK[:, j, :], K_[:, j, :], prm[:, layer, 1, B_KK + j:B_KK + j + 1], None,
                                ALU.mult).then_inc(kk_step, 1)
                n = NB * layer + j
                dve.wait_ge(kk_rooted, K0(layer) + j + 1)
                v.reciprocal(KD, KD).then_inc(kk_step, 1)
                dve.wait_ge(kk_step, 3 * n + 2)
                v.tensor_tensor(KK[:, j, :], KK[:, j, :], KD, ALU.mult).then_inc(kk_step, 1)
            dve.wait_ge(kk_step, 3 * NB * (layer + 1))
            dve.wait_ge(h_saved, 16 * (layer + 1))
            for u in range(2 * NB):
                j, d = u // 2, u % 2
                n = 2 * NB * layer + u
                way = (lambda t: t) if d == 0 else (lambda t: t[:, ::-1])
                col = lambda c0: prm[:, layer, 1, c0:c0 + 1]
                dve.wait_ge(gates_ready, n + 1)
                if u >= 1:
                    dve.wait_ge(fe_pool, 4 * n)
                v.tensor_tensor_scan(way(G_), keep[:, :], way(SG_), 0.0, ALU.mult, ALU.add).then_inc(fe_dve, 1)
                dve.wait_ge(fe_dve, 8 * n + 1)
                v.tensor_tensor(SG_, G_, SG_, ALU.subtract).then_inc(fe_dve, 1)
                v.tensor_scalar(KD, AA, col(B_KA + j), drv[:, 15 + j:16 + j], ALU.mult, ALU.add).then_inc(fe_dve, 1)
                dve.wait_ge(fe_dve, 8 * n + 3)
                v.tensor_tensor(KD, KD, K_[:, j, :], ALU.mult).then_inc(fe_dve, 1)
                dve.wait_ge(fe_dve, 8 * n + 4)
                dve.wait_ge(fe_exp, 4 * n + 3)
                if d == 0:
                    v.scalar_tensor_tensor(BON[:, j, :], KD, col(B_U + d * NB + j), R_[:, j, :], ALU.mult, ALU.mult).then_inc(fe_dve, 2)
                else:
                    v.scalar_tensor_tensor(G_, KD, col(B_U + d * NB + j), R_[:, j, :], ALU.mult, ALU.mult).then_inc(fe_dve, 1)
                    dve.wait_ge(fe_dve, 8 * n + 5)
                    v.tensor_tensor(BON[:, j, :], BON[:, j, :], G_, ALU.add).then_inc(fe_dve, 1)
                v.tensor_tensor(way(KP[d][:, j, :]), KD, E2, ALU.mult).then_inc(fe_dve, 1)
                v.tensor_tensor(way(RP[d][:, j, :]), R_[:, j, :], E1, ALU.mult).then_inc(fe_dve, 1)
            for j in range(NB):
                n = NB * layer + j
                dve.wait_ge(bonus_summed, n + 1)
                for s, (a, w) in enumerate(SEGS):
                    ins = v.tensor_tensor(BON[:, j, a:a + w], PS[:, 2 * j + s, 0:w], V_[:, j, a:a + w], ALU.mult)

        def pool_feat(pool, layer):
            gp = nc.gpsimd
            gp.tensor_copy(VF[:, :, :], V_[:, :, ::-1])
            for u in range(2 * NB):
                j, d = u // 2, u % 2
                n = 2 * NB * layer + u
                way = (lambda t: t) if d == 0 else (lambda t: t[:, ::-1])
                pool.wait_ge(gates_ready, n + 1)
                pool.wait_ge(fe_dve, 8 * n + 3)
                gp.tensor_tensor(AA, AA, KK[:, j, :], ALU.mult).then_inc(fe_pool, 1)
                pool.wait_ge(fe_pool, 4 * n + 1)
                pool.wait_ge(fe_exp, 4 * n + 2)
                gp.tensor_tensor(way(BP[d][:, j, :]), AA, E2, ALU.mult).then_inc(fe_pool, 1)
                pool.wait_ge(fe_exp, 4 * n + 4)
                gp.tensor_tensor(way(KKP[d][:, j, :]), SG_, KK[:, j, :], ALU.mult).then_inc(fe_pool, 2)

        RWBUF = ([12288 + 1024 * n for n in range(6)] + [21504, 37376] + [44544 + 1024 * n for n in range(4)])

        def rwbuf(n):
            return [region(RWBUF[n] + 512 * g, NB, P) for g in range(2)]

        BDK, BDB, BDKK, BDV, KPT, BPT, VTK, AM, ATT, AUK, ARK, ST = (rwbuf(n) for n in range(12))
        XR, YR, TR = BDB, BDK, BDV
        y_moved = dsem("y_moved")
        bp_built, bpt_ready, bpt_moved, auk_ready, auk_moved = q_decayed, v_weighted, kst_ready, eb_ready, dd_ready

        def rw_loops():
            for (a, w), first, back in zip(SEGS, (0, CTX // RW_C), (SEQ, 0)):
                yield first, w // RW_C, (a, back)

        def pool_rw(pool, layer):
            gp = nc.gpsimd
            for g in range(2):
                gp.memset(ST[g], 0.0).then_inc(s_updated[g], 1)
            for first, steps, base in rw_loops():
                with pool.Fori(0, steps) as i:
                    it, own = STEPS * layer + 6 + first + i, RW_CHUNKS * layer + first + i
                    for g in range(2):
                        pool.wait_ge(s_updated[g], it + 2 * (layer + 1))
                        pool.wait_ge(y_moved[g], own + 1)
                        for dst, src, ready in ((BDKK, KKP[g], ug_built), (BDB, BP[g], bp_built),
                                                (BDK, KP[g], k_built), (BDV, (V_, VF)[g], v_built)):
                            cols = src[:, :, bass.ds(base[g] + i * RW_C, RW_C)]
                            ins = gp.tensor_tensor(dst[g].rearrange("p u (b t) -> p u b t", b=2), bc(cols, 2, [P, NB, 2, RW_C]),
                                                   bc(headones[:, :].rearrange("p (b t) -> p b t", b=2), 1, [P, NB, 2, RW_C]),
                                                   ALU.mult)
                            ins.then_inc(ready[g], 1)

        def quad(pe, bank_, lhs, rhs, start=True, stop=True, width=P, at=0):
            for u in range(NB):
                mm = pe.matmul(PS[:, bank_, at + u * width:at + (u + 1) * width], lhs[:, u, :], rhs[:, u, :],
                               start=start, stop=stop)
            return mm

        def quad_turn(pe, bank_, src):
            for u in range(NB):
                mm = pe.transpose(PS[:, bank_, u * P:(u + 1) * P], src[:, u, :], ident[:, :])
            return mm

        def pe_rw(pe, layer):
            n = LEVELS_RW
            for first, steps, base in rw_loops():
                with pe.Fori(0, steps) as i:
                    it = STEPS * layer + 6 + first + i
                    own = RW_CHUNKS * layer + first + i
                    xs = XS * layer + 6 * LEVELS_DN + n * (first + i)
                    ts = TS * layer + 6 * (LEVELS_DN - 1) + (n - 1) * (first + i)
                    rp = [RP[g][:, :, bass.ds(base[g] + i * RW_C, RW_C)] for g in range(2)]
                    for g in range(2):
                        c = 4 * g
                        pe.wait_ge(ug_built[g], it + 1)
                        pe.wait_ge(bp_built[g], it + 1)
                        quad(pe, c, BDKK[g], BDB[g]).then_inc(kk_ready[g], 1)
                        pe.wait_ge(k_built[g], it + 1)
                        quad(pe, c + 1, BDK[g], BDKK[g]).then_inc(auk_ready[g], 1)
                        quad_turn(pe, c + 3, BDK[g]).then_inc(ktok_ready[g], 1)
                        quad(pe, c + 2, BDK[g], rp[g], width=RW_C)
                        quad(pe, c + 2, BDB[g], rp[g], width=RW_C, at=NB * RW_C).then_inc(kq_ready[g], 1)
                    for g in range(2):
                        c = 4 * g
                        pe.wait_ge(a_ready[g], it + 1)
                        quad_turn(pe, c, BDB[g]).then_inc(bpt_ready[g], 1)
                        pe.wait_ge(v_built[g], it + 1)
                        pe.wait_ge(auk_moved[g], it + 1)
                        quad_turn(pe, c + 1, BDV[g]).then_inc(vtok_ready[g], 1)
                        pe.wait_ge(ktok_moved[g], it + 1)
                        quad_turn(pe, c + 3, AM[g]).then_inc(at_turned[g], 1)
                    for l in range(n):
                        if l > 0:
                            for g in range(2):
                                pe.wait_ge(x_ready[g], xs + l)
                                if l == 1:
                                    pe.wait_ge(at_moved[g], it + 1)
                                    pe.wait_ge(vtok_moved[g], it + 1)
                                quad(pe, 4 * g + 1, ATT[g], XR[g]).then_inc(tx_summed[g], 1)
                            for g in range(2):
                                pe.wait_ge(tx_masked[g], ts + l)
                                pe.wait_ge(y_ready[g], xs + l)
                                if l == 1:
                                    pe.wait_ge(attn_ready[g], it + 1)
                                quad(pe, 4 * g + 2, YR[g], TR[g]).then_inc(xd_summed[g], 1)
                        for g in range(2):
                            pe.wait_ge(x_ready[g], xs + l + 1)
                            if l == 0:
                                pe.wait_ge(bpt_moved[g], it + 1)
                            quad_turn(pe, 4 * g, XR[g]).then_inc(x_turned[g], 1)
                        if l == 0:
                            for g in range(2):
                                pe.wait_ge(s_updated[g], it + 2 * (layer + 1))
                                pe.wait_ge(at_moved[g], it + 1)
                                pe.wait_ge(vtok_moved[g], it + 1)
                                for u in range(NB):
                                    o = PS[:, 4 * g + 3, u * P:(u + 1) * P]
                                    pe.matmul(o, BDKK[g][:, u, :], ST[g][:, u, :], start=True, stop=False)
                                    mm = pe.matmul(o, AUK[g][:, u, :], VTK[g][:, u, :], start=False, stop=True)
                                mm.then_inc(ks_ready[g], 1)
                    for g in range(2):
                        pe.wait_ge(y_ready[g], xs + n)
                        pe.wait_ge(r_ready[g], it + 1)
                        quad(pe, 4 * g + 1, YR[g], AM[g]).then_inc(vn_summed[g], 1)
                    for g in range(2):
                        c = 4 * g
                        pe.wait_ge(vn_ready[g], it + 1)
                        for u in range(NB):
                            o = PS[:, c + 2, u * P:(u + 1) * P]
                            pe.matmul(o, KPT[g][:, u, :], VTK[g][:, u, :], start=True, stop=False)
                            mm = pe.matmul(o, BPT[g][:, u, :], ATT[g][:, u, :], start=False, stop=True)
                        mm.then_inc(s_summed[g], 1)
                        for u in range(NB):
                            o = PS[:, c + 3, u * RW_C:(u + 1) * RW_C]
                            pe.matmul(o, ST[g][:, u, :], rp[g][:, u, :], start=True, stop=False)
                            pe.matmul(o, VTK[g][:, u, :], ARK[g].rearrange("p u t -> p (u t)")[:, u * RW_C:(u + 1) * RW_C],
                                      start=False, stop=False)
                            mm = pe.matmul(o, ATT[g][:, u, :],
                                           ARK[g].rearrange("p u t -> p (u t)")[:, (NB + u) * RW_C:(NB + u + 1) * RW_C],
                                           start=False, stop=True)
                        mm.then_inc(o_summed[g], 1)

        def act_rw(act, layer):
            sc = nc.scalar
            n = LEVELS_RW
            if layer == 0:
                for g in range(2):
                    act.sem_inc(y_moved[g], 1)
            for first, steps, base in rw_loops():
                with act.Fori(0, steps) as i:
                    it = STEPS * layer + 6 + first + i
                    own = RW_CHUNKS * layer + first + i
                    xs = XS * layer + 6 * LEVELS_DN + n * (first + i)
                    ts = TS * layer + 6 * (LEVELS_DN - 1) + (n - 1) * (first + i)
                    for g in range(2):
                        act.wait_ge(kk_ready[g], it + 1)
                        sc.activation(AM[g], bank(4 * g), ACT.Copy).then_inc(a_ready[g], 1)
                        act.wait_ge(ktok_ready[g], it + 1)
                        sc.activation(KPT[g], bank(4 * g + 3), ACT.Copy).then_inc(ktok_moved[g], 1)
                    for g in range(2):
                        act.wait_ge(bpt_ready[g], it + 1)
                        sc.activation(BPT[g], bank(4 * g), ACT.Copy).then_inc(bpt_moved[g], 1)
                        act.wait_ge(vtok_ready[g], it + 1)
                        sc.activation(VTK[g], bank(4 * g + 1), ACT.Copy).then_inc(vtok_moved[g], 1)
                        act.wait_ge(at_turned[g], it + 1)
                        sc.activation(ATT[g], bank(4 * g + 3), ACT.Copy).then_inc(at_moved[g], 1)
                    for l in range(n):
                        for g in range(2):
                            act.wait_ge(x_turned[g], xs + l + 1)
                            if l > 0:
                                act.wait_ge(xd_summed[g], ts + l)
                            sc.activation(YR[g], bank(4 * g), ACT.Copy).then_inc(y_ready[g], 1)
                        if l == 1:
                            for g in range(2):
                                act.wait_ge(ks_ready[g], it + 1)
                                act.wait_ge(x0_step[g], it + 1)
                                sc.activation(AM[g], bank(4 * g + 3), ACT.Copy, scale=-1.0).then_inc(r_ready[g], 1)
                    for g in range(2):
                        act.wait_ge(vn_summed[g], it + 1)
                        sc.activation(ATT[g], bank(4 * g + 1), ACT.Copy).then_inc(vn_ready[g], 1)
                    for g in range(2):
                        act.wait_ge(o_summed[g], it + 1)
                        sc.activation(RP[g][:, :, bass.ds(base[g] + i * RW_C, RW_C)],
                                      PS[:, 4 * g + 3, 0:NB * RW_C].rearrange("p (u t) -> p u t", u=NB),
                                      ACT.Copy).then_inc(y_moved[g], 1)

        def dve_rw(dve, layer):
            v = nc.vector
            n = LEVELS_RW
            for first, steps, base in rw_loops():
                with dve.Fori(0, steps) as i:
                    it = STEPS * layer + 6 + first + i
                    own = RW_CHUNKS * layer + first + i
                    xs = XS * layer + 6 * LEVELS_DN + n * (first + i)
                    ts = TS * layer + 6 * (LEVELS_DN - 1) + (n - 1) * (first + i)
                    for g in range(2):
                        dve.wait_ge(auk_ready[g], it + 1)
                        v.tensor_tensor(AUK[g], bank(4 * g + 1), bc(upto_strict[:, :], 1, [P, NB, P]),
                                        ALU.mult).then_inc(auk_moved[g], 1)
                        dve.wait_ge(a_ready[g], it + 1)
                        dve.wait_ge(kq_ready[g], it + 1)
                        dve.wait_ge(bpt_ready[g], it + 1)
                        v.tensor_tensor(XR[g], AM[g], bc(level[:, 0, :], 1, [P, NB, P]), ALU.mult).then_inc(x0_step[g], 1)
                        dve.wait_ge(x0_step[g], it + 1)
                        v.tensor_tensor(XR[g], bc(ident[:, :], 1, [P, NB, P]), XR[g], ALU.subtract).then_inc(x_ready[g], 1)
                        v.tensor_tensor(ARK[g].rearrange("p u t -> p (u t)").rearrange("p (u t) -> p u t", t=RW_C),
                                        PS[:, 4 * g + 2, :].rearrange("p (u t) -> p u t", t=RW_C),
                                        bc(pair_incl[:, :], 1, [P, 2 * NB, RW_C]), ALU.mult).then_inc(attn_ready[g], 1)
                    for l in range(1, n):
                        for g in range(2):
                            dve.wait_ge(tx_summed[g], ts + l)
                            v.tensor_tensor(TR[g], bank(4 * g + 1), bc(level[:, l, :], 1, [P, NB, P]),
                                            ALU.mult).then_inc(tx_masked[g], 1)
                        for g in range(2):
                            dve.wait_ge(xd_summed[g], ts + l)
                            dve.wait_ge(x_turned[g], xs + l)
                            v.tensor_tensor(XR[g], XR[g], bank(4 * g + 2), ALU.subtract).then_inc(x_ready[g], 1)
                    for g in range(2):
                        dve.wait_ge(o_summed[g], it + 1)
                        v.tensor_tensor(ST[g], ST[g], bank(4 * g + 2), ALU.add).then_inc(s_scaled[g], 1)
                    for g in range(2):
                        dve.wait_ge(s_scaled[g], it + 1)
                        v.tensor_tensor(ST[g], ST[g], PC[:, g, :, bass.ds(base[g] // RW_C + i, 1)].broadcast_to([P, NB, P]),
                                        ALU.mult).then_inc(s_updated[g], 1)

        go_step, go_summed, go_act = sem("go_step"), sem("go_summed"), sem("go_act")
        h_loaded = sem("h_loaded")
        mix_dn = region(18432, NB, T)
        mix_rw = region(12288, NB, T)
        gtmp = [region(44544 + n * T, T) for n in range(4)]

        def sp_rw_out(sp, layer):
            sp.dma_start(h[:, :, :].rearrange("p a b -> p (a b)"), h_save).then_inc(h_loaded, 16)

        def sp_load_mix(sp, layer):
            sp.dma_start(mix_dn[:, :, :].rearrange("p a b -> p (a b)"), mix_save).then_inc(h_loaded, 16)
            sp.wait_ge(h_loaded, 32 * (layer + 1))

        def dve_rw_out(dve, layer):
            v = nc.vector
            y = RP[0]
            d0, s0, a0 = 28 * layer, 12 * layer, 8 * layer
            for j in range(NB):
                v.tensor_tensor(y[:, j, :], y[:, j, :], RP[1][:, j, ::-1], ALU.add).then_inc(go_step, 1)
                dve.wait_ge(go_step, d0 + 2 * j + 1)
                v.tensor_tensor(y[:, j, :], y[:, j, :], BON[:, j, :], ALU.add).then_inc(go_step, 1)
            for j in range(NB):
                dve.wait_ge(go_step, d0 + 2 * j + 2)
                dve.wait_ge(go_summed, s0 + j + 1)
                for s, (a, w) in enumerate(SEGS):
                    ins = v.scalar_tensor_tensor(y[:, j, a:a + w], PS[:, 2 * j + s, 0:w], -1.0 / 64, y[:, j, a:a + w],
                                                 ALU.mult, ALU.add)
                ins.then_inc(go_step, 1)
            for j in range(NB):
                col = lambda c0: prm[:, layer, 0, c0 + j:c0 + j + 1]
                dve.wait_ge(go_act, a0 + NB + j + 1)
                v.reciprocal(gtmp[j], gtmp[j]).then_inc(go_step, 1)
                dve.wait_ge(go_step, d0 + 12 + 4 * j + 1)
                v.tensor_tensor(y[:, j, :], y[:, j, :], gtmp[j], ALU.mult).then_inc(go_step, 1)
                dve.wait_ge(go_step, d0 + 12 + 4 * j + 2)
                v.tensor_scalar(y[:, j, :], y[:, j, :], col(A_LN), col(A_LN + NB), ALU.mult, ALU.add).then_inc(go_step, 1)
                dve.wait_ge(go_step, d0 + 12 + 4 * j + 3)
                dve.wait_ge(go_summed, s0 + 2 * NB + j + 1)
                v.tensor_tensor(mix_rw[:, j, 0:CTX], y[:, j, 0:CTX], PS[:, 2 * j, 0:CTX], ALU.mult)
                v.tensor_tensor(mix_rw[:, j, CTX:T].rearrange("p (r c) -> p c r", r=GRID_H),
                                y[:, j, CTX:T].rearrange("p (c r) -> p c r", r=GRID_H),
                                PS[:, 2 * j + 1, 0:SEQ].rearrange("p (c r) -> p c r", r=GRID_H),
                                ALU.mult).then_inc(go_step, 1)

        def pe_rw_out(pe, layer):
            y = RP[0]
            d0, s0, a0 = 28 * layer, 12 * layer, 8 * layer

            def spread(lhs, src, j):
                for s, (a, w) in enumerate(SEGS):
                    mm = pe.matmul(PS[:, 2 * j + s, 0:w], lhs, src[:, a:a + w], start=True, stop=True)
                mm.then_inc(go_summed, 1)

            for j in range(NB):
                pe.wait_ge(go_step, d0 + 2 * j + 2)
                spread(headones[:, :], y[:, j, :], j)
            for j in range(NB):
                pe.wait_ge(go_act, a0 + j + 1)
                spread(headones[:, :], gtmp[j], j)
            for j in range(NB):
                pe.wait_ge(go_act, a0 + NB + j + 1)
                spread(g2w[:, j * P:(j + 1) * P], lora_g, j)

        def act_rw_out(act, layer):
            y = RP[0]
            d0, s0 = 28 * layer, 12 * layer
            for j in range(NB):
                act.wait_ge(go_step, d0 + 8 + j + 1)
                nc.scalar.activation(gtmp[j], y[:, j, :], ACT.Square).then_inc(go_act, 1)
            for j in range(NB):
                act.wait_ge(go_summed, s0 + NB + j + 1)
                for s, (a, w) in enumerate(SEGS):
                    ins = nc.scalar.activation(gtmp[j][:, a:a + w], PS[:, 2 * j + s, 0:w], ACT.Sqrt, scale=1.0 / 64, bias=eps[:, 1:2])
                ins.then_inc(go_act, 1)

        WB = DNB + KT

        def sp_wout(sp, layer):
            w = w_out[layer].rearrange("(k p) n -> p k n", p=P)
            with sp.Fori(0, KT // 2) as i:
                for b in range(2):
                    sp.wait_ge(proj_summed, layer * WB + DNB + 2 * i + b + 1)
                    sp.dma_start(win_buf[:, b], w[:, :, bass.ds((2 * i + b) * P, P)]).then_inc(win_landed[b], 16)

        def pe_wout(pe, layer, segs):
            pe.wait_ge(h_loaded, 32 * (layer + 1))
            with pe.Fori(0, KT // 2) as i:
                for b in range(2):
                    pe.wait_ge(win_landed[b], 16 * (layer * WB // 2 + DNB // 2 + i + 1))
                    pe.wait_ge(proj_moved, layer * WB + DNB + 2 * i + b + 1)
                    for k in range(KT):
                        src = mix_dn[:, k, :] if k < NB else mix_rw[:, k - NB, :]
                        for s, (a, w) in enumerate(segs):
                            mm = pe.matmul(PS[:, 2 * b + s, 0:w], win_buf[:, b, k, :], src[:, a:a + w],
                                           start=(k == 0), stop=(k == KT - 1))
                    mm.then_inc(proj_summed, 1)

        def dve_wout(dve, layer, segs):
            dve.wait_ge(h_loaded, 32 * (layer + 1))
            with dve.Fori(0, KT // 2) as i:
                for b in range(2):
                    dve.wait_ge(proj_summed, 2 + layer * WB + DNB + 2 * i + b + 1)
                    for s, (a0, w) in enumerate(segs):
                        at = 0 if a0 == 0 else 1
                        hv = h[:, bass.ds(2 * i + b, 1), a0:a0 + w].rearrange("p o w -> p (o w)")
                        g = mod[:, bass.ds(5 * KT + 2 * i + b, 1), at:at + 1].rearrange("p o w -> p (o w)")
                        ins = nc.vector.scalar_tensor_tensor(hv, PS[:, 2 * b + s, 0:w], g, hv, ALU.mult, ALU.add)
                    ins.then_inc(proj_moved, 1)

        out_tok = region(12288, SEQ // P, D_MODEL)
        out_turned, out_moved, stored = tiles_transposed, tile_moved, tok_landed
        N_LAST = 3 * DEPTH

        def act_final(act):
            act_square(act, N_LAST, SEGS[1:])
            act_root(act, N_LAST, SEGS[1:])
            for k in range(KT):
                act.wait_ge(normed, KT * N_LAST + k + 1)
                nc.scalar.activation(xn[:, k, CTX:T], xn[:, k, CTX:T], ACT.Copy,
                                     scale=prm[:, 0, 0, A_FINAL + k:A_FINAL + k + 1]).then_inc(xn_ready, 1)

        def pe_final(pe):
            pe_square_sum(pe, N_LAST, SEGS[1:])
            pe.wait_ge(xn_ready, KT * (N_LAST + 1))
            pe.wait_ge(rstd_ready, 2 * N_LAST + 2)
            for t in range(SEQ // P):
                for k in range(KT):
                    mm = pe.transpose(PS[:, 2 * t + k // 4, (k % 4) * P:(k % 4 + 1) * P],
                                      xn[:, k, CTX + t * P:CTX + (t + 1) * P], ident[:, :])
                mm.then_inc(out_turned, 1)

        def dve_final(dve):
            dve_norm(dve, N_LAST, SEGS[1:])
            for t in range(SEQ // P):
                dve.wait_ge(out_turned, KT + t + 1)
                nc.vector.tensor_copy(out_tok[:, t, :].rearrange("p (b f) -> p b f", b=2),
                                      PS[:, 2 * t:2 * t + 2, :]).then_inc(out_moved, 1)

        def sp_final(sp):
            o = out[0].rearrange("(t p) f -> t p f", p=P)
            for t in range(SEQ // P):
                sp.wait_ge(out_moved, 2 * KT + t + 1)
                sp.dma_start(o[t], out_tok[:, t, :]).then_inc(stored, 16)
            sp.wait_ge(stored, 32 + 16 * (SEQ // P))

        block = es.enter_context(nc.Block())

        def segs_of(layer):
            return SEGS if layer < DEPTH - 1 else SEGS[1:]

        @block.sync
        def _(sp):
            sp_setup(sp)
            for layer in range(DEPTH):
                dma_after(sp, start_of(layer, 0))
                sp_ada(sp, layer)
                dma_after(sp, start_of(layer, 2))
                sp_ffn(sp, 2 * layer, layer, 0)
                dma_after(sp, start_of(layer, 4))
                sp_proj_dn(sp, layer)
                sp_save_h(sp, layer)
                dma_after(sp, start_of(layer, 7))
                sp_save_mix(sp, layer)
                sp_proj_rw(sp, layer)
                dma_after(sp, start_of(layer, 8))
                sp_feat(sp, layer)
                dma_after(sp, start_of(layer, 10))
                sp_rw_out(sp, layer)
                sp_load_mix(sp, layer)
                dma_after(sp, start_of(layer, 11))
                sp_wout(sp, layer)
                dma_after(sp, start_of(layer, 13))
                sp_ffn(sp, 2 * layer + 1, layer, 1)
            dma_after(sp, start_of(DEPTH, 0))
            sp_final(sp)

        @block.gpsimd
        def _(pool):
            end = lambda: end_phase(pool, "pool")
            pool_setup(pool)
            end()
            for layer in range(DEPTH):
                for _ in range(4):
                    end()
                pool_proj_dn(pool, layer)
                end()
                pool_dn(pool, layer)
                end()
                end()
                pool_proj_rw(pool, layer)
                end()
                pool_feat(pool, layer)
                end()
                pool_rw(pool, layer)
                for _ in range(5):
                    end()

        @block.tensor
        def _(pe):
            end = lambda: end_phase(pe, "pe")
            pe_setup(pe)
            end()
            for layer in range(DEPTH):
                pe_ada(pe, layer)
                end()
                pe_square_sum(pe, 3 * layer, SEGS)
                end()
                pe_ffn(pe, 2 * layer, SEGS)
                end()
                pe_square_sum(pe, 3 * layer + 1, SEGS)
                end()
                pe_proj_dn(pe, layer)
                end()
                pe_dn(pe, layer)
                end()
                pe_dn_out(pe, layer)
                end()
                pe_proj_rw(pe, layer)
                end()
                pe_feat(pe, layer)
                end()
                pe_rw(pe, layer)
                end()
                pe_rw_out(pe, layer)
                end()
                pe_wout(pe, layer, segs_of(layer))
                end()
                pe_square_sum(pe, 3 * layer + 2, segs_of(layer))
                end()
                pe_ffn(pe, 2 * layer + 1, segs_of(layer))
                end()
            pe_final(pe)

        @block.scalar
        def _(act):
            end = lambda: end_phase(act, "act")
            act_setup(act)
            end()
            for layer in range(DEPTH):
                end()
                act_modulate(act, 3 * layer, 0, SEGS)
                end()
                act_ffn(act, 2 * layer, SEGS)
                end()
                act_modulate(act, 3 * layer + 1, 1, SEGS)
                end()
                act_proj_dn(act, layer)
                end()
                act_dn(act, layer)
                end()
                act_dn_out(act, layer)
                end()
                act_proj_rw(act, layer)
                end()
                act_feat(act, layer)
                end()
                act_rw(act, layer)
                end()
                act_rw_out(act, layer)
                end()
                end()
                act_modulate(act, 3 * layer + 2, 2, segs_of(layer))
                end()
                act_ffn(act, 2 * layer + 1, segs_of(layer))
                end()
            act_final(act)

        @block.vector
        def _(dve):
            end = lambda: end_phase(dve, "dve")
            dve_setup(dve)
            end()
            for layer in range(DEPTH):
                dve_ada(dve, layer)
                end()
                dve_norm(dve, 3 * layer, SEGS)
                end()
                dve_ffn(dve, 2 * layer, SEGS, 0)
                end()
                dve_norm(dve, 3 * layer + 1, SEGS)
                end()
                dve_proj_dn(dve, layer)
                end()
                dve_dn(dve, layer)
                end()
                dve_dn_out(dve, layer)
                end()
                dve_proj_rw(dve, layer)
                end()
                dve_feat(dve, layer)
                end()
                dve_rw(dve, layer)
                end()
                dve_rw_out(dve, layer)
                end()
                dve_wout(dve, layer, segs_of(layer))
                end()
                dve_norm(dve, 3 * layer + 2, segs_of(layer))
                end()
                dve_ffn(dve, 2 * layer + 1, segs_of(layer), 2)
                end()
            dve_final(dve)


_INS = ['x', 'c', 'ctx', 'c_ctx', 'ada_w', 'ada_b', 'norm_g', 'ffn_w13', 'ffn_w2', 'w_in', 'dn_conv', 'dn_a_log',
        'dn_dt_bias', 'dn_norm', 'rw_mu', 'rw_w0', 'rw_w2', 'rw_a0', 'rw_a2', 'rw_g2', 'rw_kk', 'rw_ka', 'rw_u',
        'rw_ln', 'w_out', 'final_norm']
_OUTS = [((1, SEQ, D_MODEL), 'float32')]


def kernel(**inputs):
    import numpy as _np
    import concourse.bacc as _bacc
    from concourse import mybir as _mybir
    from concourse.bass_utils import run_bass_kernel_spmd as _run

    nc = _bacc.Bacc("TRN2", target_bir_lowering=False, num_devices=1)
    arrays, args = {}, []
    for name in _INS:
        a = _np.ascontiguousarray(inputs[name])
        arrays[f"in_{name}_dram"] = a
        args.append(nc.dram_tensor(f"in_{name}_dram", a.shape, _mybir.dt.from_np(a.dtype), kind="ExternalInput").ap())
    for i, (shape, dtype) in enumerate(_OUTS):
        dt = _mybir.dt.from_np(_np.dtype(dtype))
        args.append(nc.dram_tensor(f"out_{i}_dram", shape, dt, kind="ExternalOutput").ap())
    build(nc, *args)
    r = _run(nc, [arrays], core_ids=[0])
    got = tuple(r.results[0][f"out_{i}_dram"] for i in range(len(_OUTS)))
    return got[0]
```

```python
from contextlib import ExitStack

import concourse.bass as bass
from concourse import mybir

F32 = mybir.dt.float32
F32R = mybir.dt.float32r
ALU = mybir.AluOpType
ACT = mybir.ActivationFunctionType

P = 128
D_MODEL, SEQ, CTX, DEPTH, GRID_W = 1024, 512, 256, 2, 64
GRID_H = SEQ // GRID_W
T = CTX + SEQ
KT = D_MODEL // P
D_FF = 2816
NF = D_FF // P
N_MOD = 9
EPS = 1e-6
DN_H, DN_W = 4, 512
DN_IN = 4 * DN_W + 4 * DN_H
DN_C = 128
RW_W, RW_C = 512, 64
NB = RW_W // P
RW_CHUNKS = T // RW_C
GN_EPS = 64e-5
DECAY_SCALE = 0.6065306597126334
SEGS = ((0, CTX), (CTX, SEQ))
PHASES_PER_LAYER = 14

A_ADAB, A_NORM, A_FINAL, A_LN, A_DNN, A_ROWS = 0, 72, 96, 104, 112, 113
B_CONV, B_MU, B_W0, B_A0, B_KK, B_KA, B_U, B_ROWS = 0, 60, 90, 98, 106, 110, 114, 122


def build(nc, x, c, ctx, c_ctx, ada_w, ada_b, norm_g, ffn_w13, ffn_w2, w_in, dn_conv, dn_a_log, dn_dt_bias,
          dn_norm, rw_mu, rw_w0, rw_w2, rw_a0, rw_a2, rw_g2, rw_kk, rw_ka, rw_u, rw_ln, w_out, final_norm,
          out):
    es = ExitStack()
    with es:
        def sb(name, shape):
            return es.enter_context(nc.sbuf_tensor(name, shape, F32))

        ARENA = 49152
        FF_PARTS = ((0, 8), (8, 8), (16, 6))
        FF_MAX = 8
        WBLOCK = 2 * KT * P
        HI, LO = 0, 1
        ADA_AT, HID_AT = KT * T + 2 * WBLOCK + 2 * T, 27136

        def placed(placing, name, shape, dtype=F32):
            return placing.enter_context(nc.sbuf_tensor(name, shape, dtype))

        with ExitStack() as placing:
            placed(placing, "below_ffn", [P, KT * T])
            raw_w = placed(placing, "raw_w", [P, 2, WBLOCK])
            silu_buf = placed(placing, "silu_buf", [P, 2, T])
            placed(placing, "guest_place", [P, 3 * KT * P])
            x_split = [placed(placing, name, [P, KT, T], F32R) for name in ("x_hi", "x_lo")]
            hid_split = [placed(placing, name, [P, FF_MAX, T], F32R) for name in ("hidden_hi", "hidden_lo")]
            w_split = [placed(placing, name, [P, 2, WBLOCK], F32R) for name in ("w_hi", "w_lo")]
        with ExitStack() as placing:
            placed(placing, "below_xn", [P, HID_AT])
            xn_ffn = placed(placing, "xn_ffn", [P, KT, T])
        arena = sb("arena", [P, ARENA])

        def region(start, *dims):
            n = 1
            for d in dims:
                n *= d
            assert start + n <= ARENA
            flat = arena[:, start:start + n]
            if len(dims) == 1:
                return flat
            if len(dims) == 2:
                return flat.rearrange("p (a b) -> p a b", a=dims[0])
            if len(dims) == 3:
                return flat.rearrange("p (a b c) -> p a b c", a=dims[0], b=dims[1])
            return flat.rearrange("p (a b c d) -> p a b c d", a=dims[0], b=dims[1], c=dims[2])

        PS = es.enter_context(nc.psum_tensor("PS", [P, 8, 512], F32))

        ident = sb("ident", [P, P])
        flip = sb("flip", [P, P])
        ones = sb("ones", [P, P])
        headones = sb("headones", [P, P])
        upto_incl = sb("upto_incl", [P, P])
        upto_strict = sb("upto_strict", [P, P])
        level = sb("level", [P, 7, P])
        pair_incl = sb("pair_incl", [P, RW_C])
        keep = sb("keep", [P, T])
        prm = sb("prm", [P, DEPTH, 2, P])
        cs = sb("cs", [P, KT, 2])
        mod = sb("mod", [P, N_MOD * KT, 2])
        gain = sb("gain", [P, 3, KT, 2])
        drv = sb("drv", [P, 20])
        dn_rows = sb("dn_rows", [P, 2, 2 * DN_H])
        eps = sb("eps", [P, 3])
        ab_raw = sb("ab_raw", [P, 6, 16])
        band = sb("band", [P, 15])
        pair_band = sb("pair_band", [P, 14])

        pair_spread = sb("pair_spread", [8, NB * P])

        def to_row(u):
            return band[:, 7 - u:15 - u]

        def to_pair_rows(j):
            return pair_band[:, 6 - 2 * j:14 - 2 * j]

        def from_row(u):
            return ident[0:8, u:u + 1].broadcast_to([8, P])

        def from_pair_rows(j):
            return pair_spread[:, j * P:(j + 1) * P]

        h = region(0, KT, T)
        xn = region(6144, KT, T)
        sq = region(40448, 2, T)
        rstd = region(41984, T)
        ada_buf = region(ADA_AT, 3, KT, P)
        ada_first = region(20480, 6, KT, 4 * P)
        tok_in = region(12288, 6, D_MODEL)
        prm_rows = region(18432, DEPTH, 2, P)
        c_rows = region(19200, P)
        qkv = region(12288, 3 * NB, T)
        zgate = region(21504, NB, T)
        dn_o = region(24576, NB, T)
        win_buf = region(46848, 2, KT, P)
        pad = region(31744, 2, 776)
        conv = region(33296, 2, 776)
        wab = region(34848, KT, 16)
        sm = 42752
        ag = region(sm, 6, 8)
        bt = region(sm + 48, 6, 8)
        t48a = region(sm + 96, 48)
        t48b = region(sm + 144, 48)
        g_ = region(sm + 192, 6, 8)
        gcum = region(sm + 240, 6, 8)
        begc = region(sm + 288, 6, 8)
        ab_flip = region(sm + 336, 6, 16)

        h_save = nc.dram_tensor("h_save", (P, KT * T), F32, kind="Internal").ap()
        mix_save = nc.dram_tensor("mix_save", (P, NB * T), F32, kind="Internal").ap()

        made = {}

        def sem(name):
            if name not in made:
                made[name] = es.enter_context(nc.semaphore(name))
            return made[name]

        phase_done = sem("phase_done")
        phases = {}

        def end_phase(eng, who):
            phases[who] = phases.get(who, 0) + 1
            eng.drain().then_inc(phase_done, 1)
            eng.wait_ge(phase_done, 4 * phases[who])

        def dma_after(eng, n):
            eng.wait_ge(phase_done, 4 * n)

        def start_of(layer, k):
            return 1 + PHASES_PER_LAYER * layer + k

        def bc(ap, axis, shape):
            return ap.unsqueeze(axis).broadcast_to(list(shape))

        prm_landed, tok_landed, masks_ready = sem("prm_landed"), sem("tok_landed"), sem("masks_ready")
        rows_transposed, tiles_transposed, tile_moved = sem("rows_transposed"), sem("tiles_transposed"), sem("tile_moved")
        N_PRM = 12 * DEPTH + 2

        def sp_setup(sp):
            for l in range(DEPTH):
                for tile, at, src in (
                    (0, A_ADAB, ada_b[l].rearrange("(a p) -> a p", p=P)),
                    (0, A_NORM, norm_g[l].rearrange("n (a p) -> (n a) p", p=P)),
                    (0, A_FINAL, final_norm.rearrange("(a p) -> a p", p=P)),
                    (0, A_LN, rw_ln[l].rearrange("n (a p) -> (n a) p", p=P)),
                    (0, A_DNN, dn_norm[l:l + 1, :]),
                    (1, B_CONV, dn_conv[l].rearrange("n (a p) -> (n a) p", p=P)),
                    (1, B_MU, rw_mu[l].rearrange("n (a p) -> (n a) p", p=P)),
                    (1, B_W0, rw_w0[l].rearrange("n (a p) -> (n a) p", p=P)),
                    (1, B_A0, rw_a0[l].rearrange("n (a p) -> (n a) p", p=P)),
                    (1, B_KK, rw_kk[l].rearrange("(a p) -> a p", p=P)),
                    (1, B_KA, rw_ka[l].rearrange("(a p) -> a p", p=P)),
                    (1, B_U, rw_u[l].rearrange("n (a g) p -> (n a) (g p)", g=2)),
                ):
                    sp.dma_start(prm_rows[at:at + src.shape[0], l, tile, :], src).then_inc(prm_landed, 16)
            sp.dma_start(c_rows[0:8, :], c_ctx.rearrange("(a p) -> a p", p=P)).then_inc(prm_landed, 16)
            sp.dma_start(c_rows[8:16, :], c[0].rearrange("(a p) -> a p", p=P)).then_inc(prm_landed, 16)
            sp.dma_start(tok_in[:, 0:2, :], ctx[0].rearrange("(a p) f -> p a f", p=P)).then_inc(tok_landed, 16)
            sp.dma_start(tok_in[:, 2:6, :], x[0].rearrange("(a p) f -> p a f", p=P)).then_inc(tok_landed, 16)

        def pool_setup(pool):
            m = masks_ready
            count = [0]

            def then(ins):
                count[0] += 1
                ins.then_inc(m, 1)
                pool.wait_ge(m, count[0])

            g = nc.gpsimd
            then(g.memset(ones[:, :], 1.0))
            then(g.memset(eps[:, 0:1], EPS))
            then(g.memset(eps[:, 1:2], GN_EPS))
            then(g.memset(eps[:, 2:3], P * EPS))
            then(g.memset(keep[:, :], 1.0))
            then(g.memset(keep[:, :].rearrange("p (a b) -> p a b", b=RW_C)[:, :, 0:1], 0.0))
            then(g.memset(band[:, :], 0.0))
            then(g.memset(band[:, 7:8], 1.0))
            then(g.memset(pair_band[:, :], 0.0))
            then(g.memset(pair_band[0:64, 6:7], 1.0))
            then(g.memset(pair_band[64:128, 7:8], 1.0))
            then(g.memset(pair_spread[:, :], 1.0))
            then(g.affine_select(out=pair_spread[:, :], in_=pair_spread[:, :], compare_op=ALU.is_equal, fill=0.0, base=0,
                                 pattern=[[-1, 2 * NB], [0, 64]], channel_multiplier=1))
            then(g.memset(headones[:, :], 0.0))
            then(g.memset(headones[0:64, 0:64], 1.0))
            then(g.memset(headones[64:128, 64:128], 1.0))
            then(g.affine_select(out=ident[:, :], in_=ones[:, :], compare_op=ALU.is_equal, fill=0.0, base=0,
                                 pattern=[[-1, P]], channel_multiplier=1))
            then(g.affine_select(out=flip[:, :], in_=ones[:, :], compare_op=ALU.is_equal, fill=0.0, base=-(P - 1),
                                 pattern=[[1, P]], channel_multiplier=1))
            then(g.affine_select(out=upto_incl[:, :], in_=ones[:, :], compare_op=ALU.is_ge, fill=0.0, base=0,
                                 pattern=[[1, P]], channel_multiplier=-1))
            then(g.affine_select(out=upto_strict[:, :], in_=ones[:, :], compare_op=ALU.is_ge, fill=0.0, base=-1,
                                 pattern=[[1, P]], channel_multiplier=-1))
            for half in range(2):
                v = pair_incl[64 * half:64 * half + 64, :]
                then(g.affine_select(out=v, in_=ones[64 * half:64 * half + 64, 0:RW_C], compare_op=ALU.is_ge,
                                     fill=0.0, base=0, pattern=[[1, RW_C]], channel_multiplier=-1))
            then(g.memset(level[:, :, :], 0.0))
            for l in range(7):
                w = 1 << l
                v = level[:, l, :].rearrange("p (b s j) -> p b s j", s=2, j=w)[:, :, 0, :]
                nb = P // (2 * w)
                then(g.memset(v, 1.0))
                then(g.affine_select(out=v, in_=v, compare_op=ALU.is_ge, fill=0.0, base=-w,
                                     pattern=[[-2 * w, nb], [0, w]], channel_multiplier=1))
                then(g.affine_select(out=v, in_=v, compare_op=ALU.is_ge, fill=0.0, base=2 * w - 1,
                                     pattern=[[2 * w, nb], [0, w]], channel_multiplier=-1))
            pool.sem_inc(masks_ready, 100)

        def pe_setup(pe):
            pe.wait_ge(masks_ready, 100)
            pe.wait_ge(prm_landed, 16 * N_PRM)
            for l in range(DEPTH):
                for tile, rows in ((0, A_ROWS), (1, B_ROWS)):
                    pe.transpose(PS[:, 0, (2 * l + tile) * P:(2 * l + tile) * P + rows],
                                 prm_rows[0:rows, l, tile, :], ident[0:rows, 0:rows])
            pe.transpose(PS[:, 1, 0:16], c_rows[0:16, :], ident[0:16, 0:16]).then_inc(rows_transposed, 1)
            pe.wait_ge(tok_landed, 32)
            for k in range(KT):
                b = 2 + 2 * (k % 3)
                if k >= 3:
                    pe.wait_ge(tile_moved, 2 * (k - 2))
                for t in range(6):
                    bank, at = (b, t * P) if t < 2 else (b + 1, (t - 2) * P)
                    mm = pe.transpose(PS[:, bank, at:at + P], tok_in[:, t, k * P:(k + 1) * P], ident[:, :])
                mm.then_inc(tiles_transposed, 1)

        def act_setup(act):
            act.wait_ge(rows_transposed, 1)
            nc.scalar.activation(cs[:, :, 0:1], PS[:, 1, 0:8].unsqueeze(2), ACT.Silu)
            nc.scalar.activation(cs[:, :, 1:2], PS[:, 1, 8:16].unsqueeze(2), ACT.Silu)

        def dve_setup(dve):
            dve.wait_ge(rows_transposed, 1)
            for l in range(DEPTH):
                for tile, rows in ((0, A_ROWS), (1, B_ROWS)):
                    nc.vector.tensor_copy(prm[:, l, tile, 0:rows],
                                          PS[:, 0, (2 * l + tile) * P:(2 * l + tile) * P + rows])
            for k in range(KT):
                b = 2 + 2 * (k % 3)
                dve.wait_ge(tiles_transposed, k + 1)
                nc.vector.tensor_copy(h[:, k, 0:CTX], PS[:, b, 0:CTX]).then_inc(tile_moved, 1)
                nc.vector.tensor_copy(h[:, k, CTX:T], PS[:, b + 1, 0:SEQ]).then_inc(tile_moved, 1)

        ADA_TILES = N_MOD * KT
        ADA_FIRST = 3 * KT
        ada_first_landed = sem("ada_first_landed")
        ada_landed = [sem(f"ada_landed{b}") for b in range(3)]
        ada_used, ada_first_used, mod_ready = sem("ada_used"), sem("ada_first_used"), sem("mod_ready")
        GUESTS = 6
        PER_PART = GUESTS * KT // 2
        assert PER_PART == ADA_FIRST

        def ada_sums(f):
            return 4 + f // PER_PART, 384 + 2 * (f % PER_PART)

        def ada_guest(n):
            if n == 0:
                return 0, ADA_FIRST, ADA_TILES - ADA_FIRST, 0
            if n % 2 == 1 and n < 2 * DEPTH - 1:
                return (n + 1) // 2, 0, ADA_TILES, ADA_TILES - ADA_FIRST + (n - 1) // 2 * ADA_TILES
            return None

        def sp_ada_first(sp):
            src = ada_w[0].rearrange("(k p) n -> p k n", p=P)
            for j in range(ADA_FIRST // 4):
                sp.dma_start(ada_first[:, j], src[:, :, j * 4 * P:(j + 1) * 4 * P]).then_inc(ada_first_landed, 16)

        def pe_ada_first(pe):
            pe.wait_ge(ada_first_landed, 16 * ADA_FIRST // 4)
            for f in range(ADA_FIRST):
                bank_, at = ada_sums(f)
                for k in range(KT):
                    mm = pe.matmul(PS[:, bank_, at:at + 2], ada_first[:, f // 4, k, f % 4 * P:(f % 4 + 1) * P],
                                   cs[:, k, :], start=(k == 0), stop=(k == KT - 1))
            mm.then_inc(ada_first_used, 1)

        def pool_ada_guest(pool, n):
            if ada_guest(n) is None:
                return
            layer, first, tiles, before = ada_guest(n)
            if n == 0:
                pool.sem_inc(ada_used, 3)
            src = ada_w[layer].rearrange("(k p) n -> p k n", p=P)
            with pool.Fori(0, tiles // 3) as i:
                for b in range(3):
                    pool.wait_ge(ada_used, before + 3 * i + b + 1)
                    pool.dma_start(ada_buf[:, b], src[:, :, bass.ds((first + 3 * i + b) * P, P)]).then_inc(ada_landed[b], 16)

        def pe_ada_tile(pe, guest, part, i, m, at):
            layer, first, tiles, before = guest
            b = at % 3
            n = before + part * PER_PART + m * GUESTS + at
            pe.wait_ge(ada_landed[b], 16 * (i * (2 * GUESTS // 3) + n // 3 + 1))
            bank_, col = ada_sums(first + part * PER_PART)
            for k in range(KT):
                mm = pe.matmul(PS[:, bank_, bass.ds(4 * GUESTS * i + col + 2 * (m * GUESTS + at), 2)],
                               ada_buf[:, b, k, :], cs[:, k, :], start=(k == 0), stop=(k == KT - 1))
            mm.then_inc(ada_used, 1)

        mod_steps = [0]

        def dve_ada(dve, layer, first, tiles):
            pa, pb_ = prm[:, layer, 0], prm[:, layer, 1]
            a, z = first, first + tiles

            def then(ins, wait=False):
                mod_steps[0] += 1
                ins.then_inc(mod_ready, 1)
                if wait:
                    dve.wait_ge(mod_ready, mod_steps[0])

            for f in range(a, z, PER_PART):
                bank_, at = ada_sums(f)
                then(nc.vector.tensor_tensor(mod[:, f:f + PER_PART, :],
                                             PS[:, bank_, at:at + 2 * PER_PART].rearrange("p (a s) -> p a s", s=2),
                                             bc(pa[:, A_ADAB + f:A_ADAB + f + PER_PART], 2, [P, PER_PART, 2]), ALU.add), True)
            for n in range(a // (3 * KT), z // (3 * KT)):
                then(nc.vector.scalar_tensor_tensor(gain[:, n], mod[:, (3 * n + 1) * KT:(3 * n + 2) * KT, :], 1.0,
                                                    bc(pa[:, A_NORM + n * KT:A_NORM + (n + 1) * KT], 2, [P, KT, 2]),
                                                    ALU.add, ALU.mult))
                if n != 1:
                    v = mod[:, (3 * n + 2) * KT:(3 * n + 3) * KT, :]
                    then(nc.vector.tensor_scalar(v, v, 0.5, None, ALU.mult))
            if first == 0:
                then(nc.vector.tensor_tensor(drv[:, 0:15], pb_[:, B_MU:B_MU + 15], pb_[:, B_MU + 15:B_MU + 30], ALU.add), True)
                then(nc.vector.tensor_scalar(drv[:, 0:15], drv[:, 0:15], -1.0, 1.0, ALU.mult, ALU.add))
                then(nc.vector.tensor_scalar(drv[:, 15:19], pb_[:, B_KA:B_KA + 4], -1.0, 1.0, ALU.mult, ALU.add))

        def dve_ada_first(dve):
            dve.wait_ge(ada_first_used, 1)
            dve_ada(dve, 0, 0, ADA_FIRST)

        def dve_ada_guest(dve, n):
            if ada_guest(n) is None:
                return
            layer, first, tiles, before = ada_guest(n)
            dve.wait_ge(ffn_added, 2 + (n + 1) * SUMS)
            dve.wait_ge(ada_used, 3 + before + tiles)
            dve_ada(dve, layer, first, tiles)

        sq_ready, sq_summed, rstd_ready, normed, xn_ready = (
            sem("sq_ready"), sem("sq_summed"), sem("rstd_ready"), sem("normed"), sem("xn_ready"))

        def act_square(act, n, segs):
            a, z = segs[0][0], segs[-1][0] + segs[-1][1]
            for k in range(KT):
                if k >= 2:
                    act.wait_ge(sq_summed, KT * n + k - 1)
                nc.scalar.activation(sq[:, k % 2, a:z], h[:, k, a:z], ACT.Square).then_inc(sq_ready, 1)

        def pe_square_sum(pe, n, segs):
            for k in range(KT):
                pe.wait_ge(sq_ready, KT * n + k + 1)
                for s, (a, w) in enumerate(segs):
                    mm = pe.matmul(PS[:, s, 0:w], ones[:, :], sq[:, k % 2, a:a + w], start=(k == 0), stop=(k == KT - 1))
                mm.then_inc(sq_summed, 1)

        def act_root(act, n, segs):
            act.wait_ge(sq_summed, KT * (n + 1))
            for s, (a, w) in enumerate(segs):
                ins = nc.scalar.activation(rstd[:, a:a + w], PS[:, s, 0:w], ACT.Sqrt, scale=1.0 / D_MODEL, bias=eps[:, 0:1])
            ins.then_inc(rstd_ready, 1)

        def dve_rstd(dve, n, segs):
            dve.wait_ge(rstd_ready, 2 * n + 1)
            a, z = segs[0][0], segs[-1][0] + segs[-1][1]
            nc.vector.reciprocal(rstd[:, a:z], rstd[:, a:z]).then_inc(rstd_ready, 1)
            dve.wait_ge(rstd_ready, 2 * n + 2)

        def dve_norm(dve, n, segs, xn=xn):
            dve_rstd(dve, n, segs)
            a, z = segs[0][0], segs[-1][0] + segs[-1][1]
            for k in range(KT):
                nc.vector.tensor_tensor(xn[:, k, a:z], h[:, k, a:z], rstd[:, a:z], ALU.mult).then_inc(normed, 1)

        x_high_ready = sem("x_high_ready")

        def dve_norm_split(dve, n, ffn, segs):
            dve_norm(dve, n, segs, xn_ffn)
            a = segs[0][0]
            for k in range(KT):
                dve.wait_ge(x_high_ready, KT * ffn + k + 1)
                nc.vector.tensor_tensor(x_split[LO][:, k, a:T], xn_ffn[:, k, a:T], x_split[HI][:, k, a:T].bitcast(F32), ALU.subtract)

        def act_modulate(act, n, which, segs, ffn=None):
            y = xn if ffn is None else xn_ffn
            act_square(act, n, segs)
            act_root(act, n, segs)
            for k in range(KT):
                act.wait_ge(normed, KT * n + k + 1)
                for a, w in segs:
                    s = 0 if a == 0 else 1
                    ins = nc.scalar.activation(y[:, k, a:a + w], y[:, k, a:a + w], ACT.Identity,
                                               bias=mod[:, 3 * which * KT + k, s:s + 1], scale=gain[:, which, k, s:s + 1])
                ins.then_inc(xn_ready, 1)
            if ffn is not None:
                a = segs[0][0]
                for k in range(KT):
                    act.wait_ge(xn_ready, KT * n + k + 1)
                    nc.scalar.activation(x_split[HI][:, k, a:T], y[:, k, a:T], ACT.Copy).then_inc(x_high_ready, 1)

        PASSES = ((HI, HI), (HI, LO), (LO, HI))
        raw_landed = [sem("raw_landed0"), sem("raw_landed1")]
        w_high_ready, w_low_ready, block_used = sem("w_high_ready"), sem("w_low_ready"), sem("block_used")
        hidden_summed, silu_ready, product_ready, high_ready, hidden_ready = (
            sem("hidden_summed"), sem("silu_ready"), sem("product_ready"), sem("high_ready"), sem("hidden_ready"))
        ffn_summed, ffn_added = sem("ffn_summed"), sem("ffn_added")
        BLOCKS = NF + len(FF_PARTS) * KT // 2
        SUMS = len(FF_PARTS) * KT

        def ff_parts():
            for part, (f0, tiles) in enumerate(FF_PARTS):
                yield f0, tiles, f0 + part * KT // 2, part

        def sp_ffn(sp, n, layer, which):
            w13 = ffn_w13[layer, which].rearrange("(k p) (g f) -> p k g f", p=P, g=2)
            w2 = ffn_w2[layer, which].rearrange("(k p) f -> p k f", p=P)
            for f0, tiles, blocks, part in ff_parts():
                first = n * BLOCKS + blocks
                with sp.Fori(0, tiles // 2) as i:
                    for b in range(2):
                        sp.wait_ge(w_low_ready, first + 2 * i + b + 1)
                        dst = raw_w[:, b].rearrange("p (k g f) -> p k g f", k=KT, g=2)
                        for g in range(2):
                            sp.dma_start(dst[:, :, g, :], w13[:, :, g, bass.ds((f0 + 2 * i + b) * P, P)]).then_inc(raw_landed[b], 16)
                with sp.Fori(0, KT // 4) as i:
                    for b in range(2):
                        sp.wait_ge(w_low_ready, first + tiles + 2 * i + b + 1)
                        dst = raw_w[:, b, 0:tiles * 2 * P].rearrange("p (f c) -> p f c", f=tiles)
                        for half in (slice(0, tiles // 2), slice(tiles // 2, tiles)):
                            src = w2[:, f0 + half.start:f0 + half.stop, bass.ds((2 * i + b) * 2 * P, 2 * P)]
                            sp.dma_start(dst[:, half, :], src).then_inc(raw_landed[b], 16)

        def act_split(act, first, i, b):
            act.wait_ge(raw_landed[b], 32 * (first // 2 + i + 1))
            act.wait_ge(block_used, first + 2 * i + b + 1)
            nc.scalar.activation(w_split[HI][:, b, :], raw_w[:, b], ACT.Copy).then_inc(w_high_ready, 1)

        def dve_split(dve, first, i, b):
            dve.wait_ge(w_high_ready, first + 2 * i + b + 1)
            nc.vector.tensor_tensor(w_split[LO][:, b, :], raw_w[:, b],
                                    w_split[HI][:, b, :].bitcast(F32), ALU.subtract).then_inc(w_low_ready, 1)

        def pe_ffn(pe, n, segs):
            if n == 0:
                pe.sem_inc(block_used, 2)
            a = segs[0][0]
            half = (T - a) // 2
            guest = ada_guest(n)
            for f0, tiles, blocks, part in ff_parts():
                first = n * BLOCKS + blocks
                if part > 0:
                    pe.wait_ge(ffn_added, 2 + n * SUMS + part * KT - 1)
                with pe.Fori(0, tiles // 2) as i:
                    for b in range(2):
                        m = n * NF + f0 + 2 * i + b
                        pe.wait_ge(w_low_ready, 2 + first + 2 * i + b + 1)
                        pe.wait_ge(product_ready, m + 1)
                        w = [part_[:, b].rearrange("p (k g f) -> p k g f", k=KT, g=2) for part_ in w_split]
                        for g in range(2):
                            if g == 1 and b == 0 and part > 0:
                                pe.wait_ge(ffn_added, 2 + n * SUMS + part * KT)
                            for k in range(KT):
                                for q, (wo, xo) in enumerate(PASSES):
                                    for s in range(2):
                                        mm = pe.matmul(PS[:, 4 * b + 2 * g + s, 0:half], w[wo][:, k, g, :],
                                                       x_split[xo][:, k, a + s * half:a + (s + 1) * half],
                                                       start=(k == 0 and q == 0), stop=(k == KT - 1 and q == 2))
                        mm.then_inc(block_used, 1)
                pe.wait_ge(hidden_ready, 2 + n * NF + f0 + tiles - 1)
                with pe.Fori(0, KT // 4) as i:
                    for b in range(2):
                        pe.wait_ge(w_low_ready, 2 + first + tiles + 2 * i + b + 1)
                        w = [part_[:, b, 0:tiles * 2 * P].rearrange("p (f c) -> p f c", f=tiles) for part_ in w_split]
                        guests = guest is not None and part * PER_PART < guest[2]
                        for c in range(2):
                            pe.wait_ge(ffn_added, n * SUMS + part * KT + 4 * i + 2 * b + c + 1)
                            for f in range(tiles):
                                late = f - (tiles - GUESTS + 1)
                                if late == 0 and b == 0 and c == 0:
                                    pe.wait_ge(hidden_ready, 2 + n * NF + f0 + tiles)
                                if guests and late >= 0 and late % 2 == 0:
                                    pe_ada_tile(pe, guest, part, i, b, c * (GUESTS // 2) + late // 2)
                                for q, (wo, xo) in enumerate(PASSES):
                                    for s, (a0, wd) in enumerate(segs):
                                        mm = pe.matmul(PS[:, 2 * c + s, 0:wd], w[wo][:, f, c * P:(c + 1) * P],
                                                       hid_split[xo][:, f, a0:a0 + wd],
                                                       start=(f == 0 and q == 0), stop=(f == tiles - 1 and q == 2))
                            mm.then_inc(ffn_summed if c == 0 else block_used, 1)

        def act_ffn(act, n, segs):
            a = segs[0][0]
            half = (T - a) // 2
            for f0, tiles, blocks, part in ff_parts():
                first = n * BLOCKS + blocks
                if part == 0:
                    act_split(act, first, 0, 0)
                with act.Fori(0, tiles // 2) as i:
                    for b in range(2):
                        m = n * NF + f0 + 2 * i + b
                        if b == 0:
                            act_split(act, first, i, 1)
                        else:
                            act_split(act, first + 2, i, 0)
                        act.wait_ge(block_used, 2 + first + 2 * i + b + 1)
                        act.wait_ge(hidden_ready, m + 1)
                        nc.scalar.activation(silu_buf[:, b, a:T].rearrange("p (s w) -> p s w", s=2),
                                             PS[:, 4 * b:4 * b + 2, 0:half], ACT.Silu).then_inc(silu_ready, 1)
                        act.wait_ge(product_ready, 2 + m + 1)
                        nc.scalar.activation(hid_split[HI][:, bass.ds(2 * i + b, 1), a:T], silu_buf[:, b:b + 1, a:T],
                                             ACT.Copy).then_inc(high_ready, 1)
                second, last = first + tiles, part == len(FF_PARTS) - 1
                with act.Fori(0, KT // 4 - (1 if last else 0)) as i:
                    act_split(act, second, i, 1)
                    act_split(act, second + 2, i, 0)
                if last:
                    act_split(act, second, KT // 4 - 1, 1)

        def dve_ffn(dve, n, segs, which):
            if n == 0:
                dve.sem_inc(w_low_ready, 2)
                dve.sem_inc(product_ready, 2)
                dve.sem_inc(hidden_ready, 2)
                dve.sem_inc(ffn_added, 2)
            a = segs[0][0]
            half = (T - a) // 2

            def add(block, part, i, b):
                for c in range(2):
                    if c == 0:
                        dve.wait_ge(ffn_summed, n * SUMS // 2 + part * KT // 2 + 2 * i + b + 1)
                    else:
                        dve.wait_ge(block_used, 2 + block + 2 * i + b + 1)
                    f = 4 * i + 2 * b + c
                    for s, (a0, w) in enumerate(segs):
                        at = 0 if a0 == 0 else 1
                        v = h[:, bass.ds(f, 1), a0:a0 + w].rearrange("p o w -> p (o w)")
                        g = mod[:, bass.ds((3 * which + 2) * KT + f, 1), at:at + 1].rearrange("p o w -> p (o w)")
                        ins = nc.vector.scalar_tensor_tensor(v, PS[:, 2 * c + s, 0:w], g, v, ALU.mult, ALU.add)
                    ins.then_inc(ffn_added, 1)

            for f0, tiles, blocks, part in ff_parts():
                first = n * BLOCKS + blocks
                if part == 0:
                    dve_split(dve, first, 0, 0)
                with dve.Fori(0, tiles // 2) as i:
                    for b in range(2):
                        m = n * NF + f0 + 2 * i + b
                        if b == 0:
                            dve_split(dve, first, i, 1)
                        else:
                            dve_split(dve, first + 2, i, 0)
                        dve.wait_ge(silu_ready, m + 1)
                        prod = silu_buf[:, b, a:T]
                        nc.vector.tensor_tensor(prod.rearrange("p (s w) -> p s w", s=2),
                                                prod.rearrange("p (s w) -> p s w", s=2),
                                                PS[:, 4 * b + 2:4 * b + 4, 0:half], ALU.mult).then_inc(product_ready, 1)
                        dve.wait_ge(high_ready, m + 1)
                        tile = bass.ds(2 * i + b, 1)
                        nc.vector.tensor_tensor(hid_split[LO][:, tile, a:T].rearrange("p o w -> p (o w)"), prod,
                                                hid_split[HI][:, tile, a:T].rearrange("p o w -> p (o w)").bitcast(F32),
                                                ALU.subtract).then_inc(hidden_ready, 1)
                second, last = first + tiles, part == len(FF_PARTS) - 1
                if part > 0:
                    dve.wait_ge(ffn_added, 2 + n * SUMS + part * KT)
                with dve.Fori(0, KT // 4 - (1 if last else 0)) as i:
                    dve_split(dve, second, i, 1)
                    add(second, part, i, 0)
                    dve_split(dve, second + 2, i, 0)
                    add(second, part, i, 1)
                if last:
                    dve_split(dve, second, KT // 4 - 1, 1)
                    add(second, part, KT // 4 - 1, 0)
                    add(second, part, KT // 4 - 1, 1)
            dve_ada_guest(dve, n)
        DNB = 4 * NB
        win_landed = [sem("win_landed0"), sem("win_landed1")]
        wab_landed = sem("wab_landed")
        proj_summed, proj_moved, pad_zeroed = sem("proj_summed"), sem("proj_moved"), sem("pad_zeroed")
        conv_step, conv_used = sem("conv_step"), sem("conv_used")
        ab_summed, ab_step, ab_act = sem("ab_summed"), sem("ab_step"), sem("ab_act")
        qk_squared, qk_summed, qk_rooted, qk_inverted, qk_scaled = (
            sem("qk_squared"), sem("qk_summed"), sem("qk_rooted"), sem("qk_inverted"), sem("qk_scaled"))

        qk_spread = sem("qk_spread")

        def sp_proj_dn(sp, layer):
            w = w_in[layer].rearrange("(k p) n -> p k n", p=P)
            sp.dma_start(wab[:, :, :], w[:, :, 4 * DN_W:DN_IN]).then_inc(wab_landed, 16)
            sp.dma_start(dn_rows[:, 0, :], dn_a_log[layer].rearrange("d h -> (d h)").partition_broadcast(P)).then_inc(wab_landed, 16)
            sp.dma_start(dn_rows[:, 1, :], dn_dt_bias[layer].rearrange("d h -> (d h)").partition_broadcast(P)).then_inc(wab_landed, 16)
            with sp.Fori(0, DNB // 2) as i:
                for b in range(2):
                    sp.wait_ge(proj_summed, layer * (DNB + KT) + 2 * i + b + 1)
                    sp.dma_start(win_buf[:, b], w[:, :, bass.ds((2 * i + b) * P, P)]).then_inc(win_landed[b], 16)

        def pool_proj_dn(pool, layer):
            nc.gpsimd.memset(pad[:, :, :], 0.0).then_inc(pad_zeroed, 1)

        def pe_proj_dn(pe, layer):
            if layer == 0:
                pe.sem_inc(proj_summed, 2)

            def project(i, b):
                pe.wait_ge(win_landed[b], 16 * (layer * (DNB + KT) // 2 + i + 1))
                pe.wait_ge(proj_moved, layer * (DNB + KT) + 2 * i + b + 1)
                for k in range(KT):
                    for s, (a, w) in enumerate(SEGS):
                        mm = pe.matmul(PS[:, 2 * b + s, 0:w], win_buf[:, b, k, :], xn[:, k, a:a + w],
                                       start=(k == 0), stop=(k == KT - 1))
                mm.then_inc(proj_summed, 1)

            with pe.Fori(0, 3 * NB // 2) as i:
                for b in range(2):
                    project(i, b)
            for z in range(NB):
                project(3 * NB // 2 + z // 2, z % 2)
                for u in (2 * z, 2 * z + 1):
                    pe.wait_ge(qk_squared, layer * 2 * NB + u + 1)
                    for bank_, at, (a, w) in zip((6, 7), (CTX, 0), SEGS):
                        mm = pe.matmul(PS[0:8, bank_, at:at + w], to_row(u), sq[:, u % 2, a:a + w],
                                       start=(u == 0), stop=(u == 2 * NB - 1))
                    mm.then_inc(qk_summed, 1)
            pe.wait_ge(wab_landed, 48 * (layer + 1))
            for t in range(6):
                for k in range(KT):
                    mm = pe.matmul(PS[:, 4, 16 * t:16 * t + 16], xn[:, k, t * P:(t + 1) * P], wab[:, k, :],
                                   start=(k == 0), stop=(k == KT - 1))
            mm.then_inc(ab_summed, 1)
            pe.wait_ge(ab_step, 16 * layer + 1)
            pe.matmul(PS[:, 5, 0:96], flip[:, :], ab_raw[:, :, :].rearrange("p a b -> p (a b)"),
                      start=True, stop=True).then_inc(ab_summed, 1)
            pe.wait_ge(ab_step, 16 * layer + 11)
            pe.matmul(PS[:, 6, 0:48], upto_incl[:, :], g_[:, :, :].rearrange("p a b -> p (a b)"),
                      start=True, stop=True).then_inc(ab_summed, 1)
            pe.wait_ge(qk_inverted, layer + 1)
            pe.wait_ge(proj_moved, 2 + layer * (DNB + KT) + DNB)
            for u in range(2 * NB):
                if u >= 2:
                    pe.wait_ge(qk_scaled, layer * 2 * NB + u - 1)
                for s, (a, w) in enumerate(SEGS):
                    mm = pe.matmul(PS[:, 2 * (u % 2) + s, 0:w], from_row(u), conv[0:8, 0, a:a + w], start=True, stop=True)
                mm.then_inc(qk_spread, 1)

        def act_proj_dn(act, layer):
            if layer == 0:
                act.sem_inc(proj_moved, 2)
                act.sem_inc(conv_used, 2)
            act.wait_ge(pad_zeroed, 2 * layer + 1)
            with act.Fori(0, 3 * NB // 2) as i:
                for b in range(2):
                    act.wait_ge(proj_summed, 2 + layer * (DNB + KT) + 2 * i + b + 1)
                    nc.scalar.activation(pad[:, b, 2:2 + CTX], PS[:, 2 * b, 0:CTX], ACT.Copy)
                    nc.scalar.activation(pad[:, b, 6 + CTX:6 + T], PS[:, 2 * b + 1, 0:SEQ], ACT.Copy).then_inc(proj_moved, 1)
                    act.wait_ge(conv_step, 5 * (layer * 3 * NB + 2 * i + b + 1))
                    m = bass.ds(2 * i + b, 1)
                    nc.scalar.activation(qkv[:, m, 0:CTX], conv[:, b:b + 1, 0:CTX], ACT.Silu)
                    nc.scalar.activation(qkv[:, m, CTX:T], conv[:, b:b + 1, 4 + CTX:4 + T], ACT.Silu).then_inc(conv_used, 1)
            act.wait_ge(conv_used, 2 + 3 * NB * (layer + 1))
            for z in range(NB):
                for u in (2 * z, 2 * z + 1):
                    if u >= 2:
                        act.wait_ge(qk_summed, layer * 2 * NB + u - 1)
                    nc.scalar.activation(sq[:, u % 2, :], qkv[:, u, :], ACT.Square).then_inc(qk_squared, 1)
                b = z % 2
                act.wait_ge(proj_summed, 2 + layer * (DNB + KT) + 3 * NB + z + 1)
                nc.scalar.activation(zgate[:, z, 0:CTX], PS[:, 2 * b, 0:CTX], ACT.Silu)
                nc.scalar.activation(zgate[:, z, CTX:T], PS[:, 2 * b + 1, 0:SEQ], ACT.Silu).then_inc(proj_moved, 1)
            act.wait_ge(qk_summed, 2 * NB * (layer + 1))
            for bank_, at, (a, w) in zip((6, 7), (CTX, 0), SEGS):
                ins = nc.scalar.activation(conv[0:8, 0, a:a + w], PS[0:8, bank_, at:at + w], ACT.Sqrt, bias=eps[0:8, 0:1])
            ins.then_inc(qk_rooted, 1)
            a0, d0 = 4 * layer, 16 * layer
            act.wait_ge(wab_landed, 48 * (layer + 1))
            act.wait_ge(ab_step, d0 + 8)
            nc.scalar.activation(t48b[:, :], t48b[:, :], ACT.Exp, scale=-1.0).then_inc(ab_act, 1)
            act.wait_ge(ab_act, a0 + 1)
            nc.scalar.activation(t48b[:, :], t48b[:, :], ACT.Ln, bias=1.0)
            nc.scalar.activation(dn_rows[:, 0, :], dn_rows[:, 0, :], ACT.Exp).then_inc(ab_act, 1)
            nc.scalar.activation(bt[:, :, :], bt[:, :, :], ACT.Sigmoid).then_inc(ab_act, 1)
            act.wait_ge(ab_step, d0 + 12)
            nc.scalar.activation(begc[:, :, :], gcum[:, :, :], ACT.Exp).then_inc(ab_act, 1)

        def dve_proj_dn(dve, layer):
            v = nc.vector
            with dve.Fori(0, 3 * NB // 2) as i:
                for b in range(2):
                    n = layer * 3 * NB + 2 * i + b
                    dve.wait_ge(proj_moved, 2 + layer * (DNB + KT) + 2 * i + b + 1)
                    dve.wait_ge(conv_used, n + 1)
                    tap = lambda t: prm[:, layer, 1, bass.ds(B_CONV + t * 3 * NB + 2 * i + b, 1)]
                    v.tensor_scalar(conv[:, b, 0:772], pad[:, b, 0:772], tap(0), None, ALU.mult).then_inc(conv_step, 1)
                    for t in range(1, 5):
                        dve.wait_ge(conv_step, 5 * n + t)
                        v.scalar_tensor_tensor(conv[:, b, 0:772], pad[:, b, t:t + 772], tap(t), conv[:, b, 0:772],
                                               ALU.mult, ALU.add).then_inc(conv_step, 1)
            dve.wait_ge(qk_rooted, layer + 1)
            v.reciprocal(conv[0:8, 0, 0:T], conv[0:8, 0, 0:T]).then_inc(qk_inverted, 1)
            d0, H = 16 * layer, DN_H
            F = PS[:, 5, 0:96].rearrange("p (t c) -> p t c", c=16)
            dve.wait_ge(ab_summed, 3 * layer + 1)
            v.tensor_copy(ab_raw[:, :, :].rearrange("p a b -> p (a b)"), PS[:, 4, 0:96]).then_inc(ab_step, 1)
            dve.wait_ge(ab_step, d0 + 1)
            dve.wait_ge(ab_summed, 3 * layer + 2)
            v.tensor_copy(ag[:, :, 0:H], ab_raw[:, :, 0:H])
            v.tensor_copy(bt[:, :, 0:H], ab_raw[:, :, 2 * H:3 * H])
            v.tensor_copy(ag[:, 0:2, H:2 * H], F[:, 1::-1, H:2 * H])
            v.tensor_copy(ag[:, 2:6, H:2 * H], F[:, 5:1:-1, H:2 * H])
            v.tensor_copy(bt[:, 0:2, H:2 * H], F[:, 1::-1, 3 * H:4 * H])
            v.tensor_copy(bt[:, 2:6, H:2 * H], F[:, 5:1:-1, 3 * H:4 * H]).then_inc(ab_step, 1)
            dve.wait_ge(ab_step, d0 + 2)
            dve.wait_ge(wab_landed, 48 * (layer + 1))
            t48a3, t48b3 = t48a.rearrange("p (s u) -> p s u", u=8), t48b.rearrange("p (s u) -> p s u", u=8)
            v.tensor_tensor(t48a3, ag[:, :, :], bc(dn_rows[:, 1, :], 1, [P, 6, 8]), ALU.add).then_inc(ab_step, 1)
            dve.wait_ge(ab_step, d0 + 3)
            v.scalar_tensor_tensor(t48b[:, :], t48a[:, :], -1.0, t48a[:, :], ALU.mult, ALU.max).then_inc(ab_step, 5)
            dve.wait_ge(ab_act, 4 * layer + 2)
            v.scalar_tensor_tensor(t48a[:, :], t48a[:, :], 0.0, t48b[:, :], ALU.max, ALU.add).then_inc(ab_step, 1)
            dve.wait_ge(ab_step, d0 + 9)
            v.scalar_tensor_tensor(g_[:, :, :], t48a3, -1.0, bc(dn_rows[:, 0, :], 1, [P, 6, 8]),
                                   ALU.mult, ALU.mult).then_inc(ab_step, 2)
            dve.wait_ge(ab_summed, 3 * layer + 3)
            v.tensor_copy(gcum[:, :, :].rearrange("p a b -> p (a b)"), PS[:, 6, 0:48]).then_inc(ab_step, 1)
            dve.wait_ge(ab_act, 4 * layer + 4)
            v.tensor_tensor(begc[:, :, :], begc[:, :, :], bt[:, :, :], ALU.mult).then_inc(ab_step, 4)
            for u in range(2 * NB):
                dve.wait_ge(qk_spread, layer * 2 * NB + u + 1)
                for s, (a, w) in enumerate(SEGS):
                    q, factors = qkv[:, u, a:a + w], PS[:, 2 * (u % 2) + s, 0:w]
                    if u < NB:
                        ins = v.scalar_tensor_tensor(q, q, P ** -0.5, factors, ALU.mult, ALU.mult)
                    else:
                        ins = v.tensor_tensor(q, q, factors, ALU.mult)
                ins.then_inc(qk_scaled, 1)

        def dnbuf(n, g):
            return region(27648 + (2 * n + g) * 512, DN_H, P)

        NAMES = "KT QD VT UG EB DM DMT KTOK VTOK AT X Y S AV".split()
        dn = {name: [dnbuf(n, g) for g in range(2)] for n, name in enumerate(NAMES)}
        KTc, QD, VT, UG, EB, DM, DMT, KTOK, VTOK, AT, X, Y, S, AV = (dn[n] for n in NAMES)
        TD, QE = ([region(43776 + 1024 * n + 512 * g, DN_H, P) for g in range(2)] for n in range(2))
        LEVELS_DN, LEVELS_RW = 7, 6

        EVEN = P // 2

        def even(t, l, axes="p u"):
            v = t.rearrange(f"{axes} (b s j) -> {axes} b s j", s=2, j=1 << l)
            return v[:, :, :, 0, :] if axes == "p u" else v[:, :, 0, :]

        def packed(t, l):
            return t.rearrange("p (u b j) -> p u b j", u=4, j=1 << l)

        def packed_bank(b, l):
            return packed(PS[:, b, 0:4 * EVEN], l)

        def packed_sbuf(t, l):
            return packed(t.rearrange("p a b -> p (a b)")[:, 0:4 * EVEN], l)

        def level_mask(l):
            m = even(level[:, l, :], l, "p")
            return bc(m, 1, [P, 4, m.shape[1], m.shape[2]])

        def times_even(pe, b, lhs, x, l):
            for u in range(4):
                mm = pe.matmul(packed_bank(b, l)[:, u], lhs[:, u, :], even(x[:, u, :], l, "p"), start=True, stop=True)
            return mm

        def times_packed(pe, b, lhs, x):
            for u in range(4):
                mm = pe.matmul(PS[:, b, u * EVEN:(u + 1) * EVEN], lhs[:, u, :],
                               x.rearrange("p a b -> p (a b)")[:, u * EVEN:(u + 1) * EVEN], start=True, stop=True)
            return mm

        STEPS = 6 + RW_CHUNKS
        XS = 6 * LEVELS_DN + RW_CHUNKS * LEVELS_RW
        TS = XS - STEPS

        def dsem(name):
            return [sem(f"{name}{g}") for g in range(2)]

        k_built, q_built, v_built, ug_built = dsem("k_built"), dsem("q_built"), dsem("v_built"), dsem("ug_built")
        gc_spread, kk_ready, kq_ready = dsem("gc_spread"), dsem("kk_ready"), dsem("kq_ready")
        ktok_ready, vtok_ready = dsem("ktok_ready"), dsem("vtok_ready")
        ktok_moved, vtok_moved = dsem("ktok_moved"), dsem("vtok_moved")
        eb_ready, dd_ready, dd_split, dm_ready, dm_weighted = (
            dsem("eb_ready"), dsem("dd_ready"), dsem("dd_split"), dsem("dm_ready"), dsem("dm_weighted"))
        q_decayed, v_weighted, k_decayed = dsem("q_decayed"), dsem("v_weighted"), dsem("k_decayed")
        a_ready, attn_ready = dsem("a_ready"), dsem("attn_ready")
        at_turned, at_moved = dsem("at_turned"), dsem("at_moved")
        tx_summed, tx_masked, xd_summed, x_ready, x_turned, y_ready = (
            dsem("tx_summed"), dsem("tx_masked"), dsem("xd_summed"), dsem("x_ready"), dsem("x_turned"), dsem("y_ready"))
        ks_ready, r_ready, vn_summed, vn_ready, s_summed, o_summed = (
            dsem("ks_ready"), dsem("r_ready"), dsem("vn_summed"), dsem("vn_ready"), dsem("s_summed"), dsem("o_summed"))
        s_updated, o_added, x0_step = dsem("s_updated"), dsem("o_added"), dsem("x0_step")
        kst_ready, s_scaled = dsem("kst_ready"), dsem("s_scaled")

        def dn_loops(layer):
            for (a, w), first in zip(SEGS, (0, CTX // DN_C)):
                yield first, w // DN_C, a, w

        def pool_dn(pool, layer):
            gp = nc.gpsimd
            for g in range(2):
                gp.memset(S[g], 0.0).then_inc(s_updated[g], 1)
            gp.memset(dn_o[:, :, :], 0.0).then_inc(o_added[0], 1)

            def step(first, a, w, i, last_used):
                it, own = STEPS * layer + first + i, 6 * layer + first + i

                def used(semaphore, n):
                    if last_used:
                        pool.wait_ge(phase_done, 4)
                        pool.wait_ge(semaphore, n)

                for g in range(2):
                    def chunk(part):
                        v = qkv[:, part * NB:(part + 1) * NB, a:a + w]
                        return v[:, :, bass.ds(i * DN_C if g == 0 else w - DN_C - i * DN_C, DN_C)]

                    def way(t):
                        return t if g == 0 else t[:, :, ::-1]
                    u = slice(g * DN_H, (g + 1) * DN_H)
                    used(gc_spread[g], own)
                    gp.tensor_tensor(UG[g], bc(upto_incl[:, :], 1, [P, DN_H, P]),
                                     bc(g_[:, bass.ds(first + i, 1), u].rearrange("p o u -> p (o u)"), 2, [P, DN_H, P]),
                                     ALU.mult).then_inc(ug_built[g], 1)
                    used(ks_ready[g], it)
                    gp.tensor_copy(way(KTc[g]), chunk(1)).then_inc(k_built[g], 1)
                    used(kq_ready[g], it)
                    used(q_decayed[g], it)
                    gp.tensor_copy(way(QD[g]), chunk(0)).then_inc(q_built[g], 1)
                    used(vtok_ready[g], it)
                    gp.tensor_copy(way(VT[g]), chunk(2)).then_inc(v_built[g], 1)
                for g in range(2):
                    u = slice(g * DN_H, (g + 1) * DN_H)
                    row = lambda t: bc(t[:, bass.ds(first + i, 1), u].rearrange("p o u -> p (o u)"), 2, [P, DN_H, P])
                    pool.wait_ge(dm_ready[g], own + 1)
                    gp.tensor_tensor(DM[g], DM[g], row(bt), ALU.mult).then_inc(dm_weighted[g], 1)
                    pool.wait_ge(ktok_moved[g], it + 1)
                    gp.tensor_tensor(KTOK[g], KTOK[g], DMT[g][:, :, P - 1:P].broadcast_to([P, DN_H, P]),
                                     ALU.mult).then_inc(k_decayed[g], 1)
                    pool.wait_ge(k_decayed[g], own + 1)
                    gp.tensor_tensor(DMT[g], DMT[g], bc(upto_incl[:, :], 1, [P, DN_H, P]), ALU.mult).then_inc(dm_weighted[g], 1)
                    pool.wait_ge(eb_ready[g], it + 1)
                    pool.wait_ge(q_built[g], own + 1)
                    used(o_summed[g], it)
                    gp.tensor_tensor(QE[g], QD[g], EB[g], ALU.mult).then_inc(q_decayed[g], 1)
                    pool.wait_ge(phase_done, 4)
                    pool.wait_ge(vtok_moved[g], it + 1)
                    gp.tensor_tensor(VTOK[g], VTOK[g], row(bt), ALU.mult).then_inc(v_weighted[g], 1)

            for first, steps, a, w in dn_loops(layer):
                if first == 0:
                    step(first, a, w, 0, False)
                with pool.Fori(1 if first == 0 else 0, steps) as i:
                    step(first, a, w, i, True)

        def pe_dn(pe, layer):
            for first, steps, a, w in dn_loops(layer):
                with pe.Fori(0, steps) as i:
                    it, own = STEPS * layer + first + i, 6 * layer + first + i
                    for g in range(2):
                        c = 4 * g
                        pe.wait_ge(ug_built[g], it + 1)
                        pe.matmul(PS[:, c, :], ones[:, :], UG[g].rearrange("p a b -> p (a b)"),
                                  start=True, stop=True).then_inc(gc_spread[g], 1)
                        pe.wait_ge(k_built[g], it + 1)
                        for u in range(DN_H):
                            mm = pe.matmul(PS[:, c + 1, u * P:(u + 1) * P], KTc[g][:, u, :], KTc[g][:, u, :], start=True, stop=True)
                        mm.then_inc(kk_ready[g], 1)
                        pe.wait_ge(s_updated[g], it + 2 * layer + 1)
                        pe.wait_ge(q_built[g], own + 1)
                        for u in range(DN_H):
                            mm = pe.matmul(PS[:, c + 2, u * P:(u + 1) * P], KTc[g][:, u, :], QD[g][:, u, :], start=True, stop=True)
                        mm.then_inc(kq_ready[g], 1)
                        pe.wait_ge(o_added[g], own + (layer + 1 if g == 0 else 1))
                        for u in range(DN_H):
                            mm = pe.transpose(PS[:, c + 3, u * P:(u + 1) * P], KTc[g][:, u, :], ident[:, :])
                        mm.then_inc(ktok_ready[g], 1)
                    for g in range(2):
                        c = 4 * g
                        pe.wait_ge(v_built[g], it + 1)
                        pe.wait_ge(eb_ready[g], it + 1)
                        pe.wait_ge(dd_ready[g], it + 1)
                        for u in range(DN_H):
                            mm = pe.transpose(PS[:, c, u * P:(u + 1) * P], VT[g][:, u, :], ident[:, :])
                        mm.then_inc(vtok_ready[g], 1)
                    for g in range(2):
                        c = 4 * g
                        pe.wait_ge(a_ready[g], it + 1)
                        pe.wait_ge(ktok_moved[g], it + 1)
                        for u in range(DN_H):
                            mm = pe.transpose(PS[:, c + 3, u * P:(u + 1) * P], DM[g][:, u, :], ident[:, :])
                        mm.then_inc(at_turned[g], 1)
                    n = LEVELS_DN
                    for l in range(n):
                        if l > 0:
                            for g in range(2):
                                c = 4 * g
                                pe.wait_ge(x_ready[g], XS * layer + n * (first + i) + l)
                                if l == 1:
                                    pe.wait_ge(at_moved[g], it + 1)
                                times_even(pe, c + 1, AT[g], X[g], l).then_inc(tx_summed[g], 1)
                            for g in range(2):
                                c = 4 * g
                                pe.wait_ge(tx_masked[g], TS * layer + (n - 1) * (first + i) + l)
                                pe.wait_ge(y_ready[g], XS * layer + n * (first + i) + l)
                                if l == 1:
                                    pe.wait_ge(attn_ready[g], it + 1)
                                times_packed(pe, c + 2, Y[g], TD[g]).then_inc(xd_summed[g], 1)
                        for g in range(2):
                            c = 4 * g
                            pe.wait_ge(x_ready[g], XS * layer + n * (first + i) + l + 1)
                            if l == 0:
                                pe.wait_ge(vtok_moved[g], it + 1)
                            for u in range(DN_H):
                                mm = pe.transpose(PS[:, c, u * P:(u + 1) * P], X[g][:, u, :], ident[:, :])
                            mm.then_inc(x_turned[g], 1)
                        if l == 0:
                            for g in range(2):
                                pe.wait_ge(s_updated[g], it + 2 * layer + 1)
                                pe.wait_ge(at_moved[g], it + 1)
                                for u in range(DN_H):
                                    mm = pe.matmul(PS[:, 4 * g + 3, u * P:(u + 1) * P], KTc[g][:, u, :], S[g][:, u, :], start=True, stop=True)
                                mm.then_inc(ks_ready[g], 1)
                    for g in range(2):
                        c = 4 * g
                        pe.wait_ge(y_ready[g], XS * layer + n * (first + i) + n)
                        pe.wait_ge(r_ready[g], it + 1)
                        for u in range(DN_H):
                            mm = pe.matmul(PS[:, c + 1, u * P:(u + 1) * P], Y[g][:, u, :], VTOK[g][:, u, :], start=True, stop=True)
                        mm.then_inc(vn_summed[g], 1)
                    for g in range(2):
                        c = 4 * g
                        pe.wait_ge(vn_ready[g], it + 1)
                        pe.wait_ge(k_decayed[g], own + 1)
                        pe.wait_ge(q_decayed[g], it + 1)
                        for u in range(DN_H):
                            mm = pe.matmul(PS[:, c + 2, u * P:(u + 1) * P], KTOK[g][:, u, :], AV[g][:, u, :], start=True, stop=True)
                        mm.then_inc(s_summed[g], 1)
                        for u in range(DN_H):
                            pe.matmul(PS[:, c + 3, u * P:(u + 1) * P], S[g][:, u, :], QE[g][:, u, :], start=True, stop=False)
                            mm = pe.matmul(PS[:, c + 3, u * P:(u + 1) * P], AV[g][:, u, :], DMT[g][:, u, :], start=False, stop=True)
                        mm.then_inc(o_summed[g], 1)

        def bank(b):
            return PS[:, b, :].rearrange("p (u t) -> p u t", u=4)

        def act_dn(act, layer):
            sc = nc.scalar
            n = LEVELS_DN
            for first, steps, a, w in dn_loops(layer):
                with act.Fori(0, steps) as i:
                    it, own = STEPS * layer + first + i, 6 * layer + first + i
                    for g in range(2):
                        act.wait_ge(gc_spread[g], own + 1)
                        act.wait_ge(s_updated[g], it + 2 * layer + 1)
                        sc.activation(EB[g], bank(4 * g), ACT.Exp).then_inc(eb_ready[g], 1)
                    for g in range(2):
                        act.wait_ge(dd_split[g], 2 * own + 2)
                        sc.activation(DM[g], DM[g], ACT.Exp, scale=-1.0)
                        sc.activation(DMT[g], DMT[g], ACT.Exp).then_inc(dm_ready[g], 1)
                        act.wait_ge(ktok_ready[g], it + 1)
                        sc.activation(KTOK[g], bank(4 * g + 3), ACT.Copy).then_inc(ktok_moved[g], 1)
                        act.wait_ge(vtok_ready[g], it + 1)
                        sc.activation(VTOK[g], bank(4 * g), ACT.Copy).then_inc(vtok_moved[g], 1)
                    for g in range(2):
                        act.wait_ge(at_turned[g], it + 1)
                        sc.activation(AT[g], bank(4 * g + 3), ACT.Copy).then_inc(at_moved[g], 1)
                    for l in range(n):
                        for g in range(2):
                            act.wait_ge(x_turned[g], XS * layer + n * (first + i) + l + 1)
                            if l > 0:
                                act.wait_ge(xd_summed[g], TS * layer + (n - 1) * (first + i) + l)
                            sc.activation(Y[g], bank(4 * g), ACT.Copy).then_inc(y_ready[g], 1)
                    for g in range(2):
                        act.wait_ge(vn_summed[g], it + 1)
                        sc.activation(AV[g], bank(4 * g + 1), ACT.Copy).then_inc(vn_ready[g], 1)

        def dve_dn(dve, layer):
            v = nc.vector
            n = LEVELS_DN
            if layer == 0:
                dve.sem_inc(o_added[1], 1)
            for first, steps, a, w in dn_loops(layer):
                with dve.Fori(0, steps) as i:
                    it, own = STEPS * layer + first + i, 6 * layer + first + i
                    for g in range(2):
                        u = slice(g * DN_H, (g + 1) * DN_H)
                        row = lambda t: bc(t[:, bass.ds(first + i, 1), u].rearrange("p o u -> p (o u)"), 2, [P, DN_H, P])
                        dve.wait_ge(eb_ready[g], it + 1)
                        v.tensor_tensor(AV[g], bank(4 * g), row(gcum), ALU.subtract).then_inc(dd_ready[g], 1)
                        dve.wait_ge(dd_ready[g], it + 1)
                        v.tensor_scalar(DM[g], AV[g], 0.0, None, ALU.max).then_inc(dd_split[g], 1)
                        v.tensor_scalar(DMT[g], AV[g], 0.0, None, ALU.min).then_inc(dd_split[g], 1)
                    for g in range(2):
                        dve.wait_ge(dm_weighted[g], 2 * own + 1)
                        dve.wait_ge(kk_ready[g], it + 1)
                        v.tensor_tensor(DM[g], DM[g], bank(4 * g + 1), ALU.mult).then_inc(a_ready[g], 1)
                        dve.wait_ge(a_ready[g], it + 1)
                        v.tensor_tensor(X[g], DM[g], bc(level[:, 0, :], 1, [P, DN_H, P]), ALU.mult).then_inc(x0_step[g], 1)
                        dve.wait_ge(x0_step[g], it + 1)
                        v.tensor_tensor(X[g], bc(ident[:, :], 1, [P, DN_H, P]), X[g], ALU.subtract).then_inc(x_ready[g], 1)
                        dve.wait_ge(dm_weighted[g], 2 * own + 2)
                        dve.wait_ge(kq_ready[g], it + 1)
                        v.tensor_tensor(DMT[g], DMT[g], bank(4 * g + 2), ALU.mult).then_inc(attn_ready[g], 1)
                    for l in range(1, n):
                        for g in range(2):
                            dve.wait_ge(tx_summed[g], TS * layer + (n - 1) * (first + i) + l)
                            v.tensor_tensor(packed_sbuf(TD[g], l), packed_bank(4 * g + 1, l), level_mask(l), ALU.mult).then_inc(tx_masked[g], 1)
                        for g in range(2):
                            dve.wait_ge(xd_summed[g], TS * layer + (n - 1) * (first + i) + l)
                            dve.wait_ge(x_turned[g], XS * layer + n * (first + i) + l)
                            v.tensor_tensor(even(X[g], l), even(X[g], l), packed_bank(4 * g + 2, l), ALU.subtract).then_inc(x_ready[g], 1)
                        if l == 1:
                            for g in range(2):
                                u = slice(g * DN_H, (g + 1) * DN_H)
                                row = lambda t: bc(t[:, bass.ds(first + i, 1), u].rearrange("p o u -> p (o u)"), 2, [P, DN_H, P])
                                dve.wait_ge(ks_ready[g], it + 1)
                                v.tensor_tensor(AV[g], bank(4 * g + 3), row(begc), ALU.mult).then_inc(kst_ready[g], 1)
                    for g in range(2):
                        dve.wait_ge(v_weighted[g], it + 1)
                        dve.wait_ge(kst_ready[g], it + 1)
                        v.tensor_tensor(VTOK[g], VTOK[g], AV[g], ALU.subtract).then_inc(r_ready[g], 1)
                    for g in range(2):
                        dve.wait_ge(o_summed[g], it + 1)
                        v.tensor_tensor(S[g], S[g], EB[g][:, :, P - 1:P].broadcast_to([P, DN_H, P]), ALU.mult).then_inc(s_scaled[g], 1)
                    for g in range(2):
                        o = dn_o[:, :, a:a + w][:, :, bass.ds(i * DN_C if g == 0 else w - DN_C - i * DN_C, DN_C)]
                        new = bank(4 * g + 3) if g == 0 else bank(4 * g + 3)[:, :, ::-1]
                        dve.wait_ge(phase_done, 4)
                        dve.wait_ge(o_added[0], own + layer + 1)
                        dve.wait_ge(o_added[1], own + 1)
                        v.tensor_tensor(o, o, new, ALU.add).then_inc(o_added[g], 1)
                        dve.wait_ge(s_scaled[g], it + 1)
                        v.tensor_tensor(S[g], S[g], bank(4 * g + 2), ALU.add).then_inc(s_updated[g], 1)

        ho_squared, ho_summed, ho_rooted, ho_step, mix_saved, h_saved = (
            sem("ho_squared"), sem("ho_summed"), sem("ho_rooted"), sem("ho_step"), sem("mix_saved"), sem("h_saved"))

        ho_spread = sem("ho_spread")

        def act_dn_out(act, layer):
            for u in range(DN_H):
                if u >= 2:
                    act.wait_ge(ho_summed, 2 * DN_H * layer + u - 1)
                nc.scalar.activation(sq[:, u % 2, :], dn_o[:, u, :], ACT.Square).then_inc(ho_squared, 1)
            act.wait_ge(ho_summed, 2 * DN_H * layer + DN_H)
            for s, (a, w) in enumerate(SEGS):
                ins = nc.scalar.activation(conv[0:8, 0, a:a + w], PS[0:8, s, 0:w], ACT.Sqrt, scale=1.0 / P, bias=eps[0:8, 0:1])
            ins.then_inc(ho_rooted, 1)

        def pe_dn_out(pe, layer):
            for u in range(DN_H):
                pe.wait_ge(ho_squared, 2 * DN_H * layer + u + 1)
                for s, (a, w) in enumerate(SEGS):
                    mm = pe.matmul(PS[0:8, s, 0:w], to_row(u), sq[:, u % 2, a:a + w], start=(u == 0), stop=(u == DN_H - 1))
                mm.then_inc(ho_summed, 1)
            pe.wait_ge(ho_step, (1 + 2 * DN_H) * layer + 1)
            for u in range(DN_H):
                for s, (a, w) in enumerate(SEGS):
                    mm = pe.matmul(PS[:, 2 * u + s, 0:w], from_row(u), conv[0:8, 0, a:a + w], start=True, stop=True)
                mm.then_inc(ho_spread, 1)

        def dve_dn_out(dve, layer):
            n = (1 + 2 * DN_H) * layer
            dve.wait_ge(ho_rooted, 2 * layer + 1)
            nc.vector.reciprocal(conv[0:8, 0, 0:T], conv[0:8, 0, 0:T]).then_inc(ho_step, 1)
            for u in range(DN_H):
                dve.wait_ge(ho_spread, 2 * DN_H * layer + u + 1)
                for s, (a, w) in enumerate(SEGS):
                    ins = nc.vector.tensor_tensor(dn_o[:, u, a:a + w], dn_o[:, u, a:a + w], PS[:, 2 * u + s, 0:w], ALU.mult)
                ins.then_inc(ho_step, 1)
                dve.wait_ge(ho_step, n + 2 * u + 2)
                nc.vector.scalar_tensor_tensor(zgate[:, u, :], dn_o[:, u, :], prm[:, layer, 0, A_DNN:A_DNN + 1],
                                               zgate[:, u, :], ALU.mult, ALU.mult).then_inc(ho_step, 1)

        def sp_save_h(sp, layer):
            sp.dma_start(h_save, h[:, :, :].rearrange("p a b -> p (a b)")).then_inc(h_saved, 16)
            sp.wait_ge(h_saved, 16 * (layer + 1))

        def sp_save_mix(sp, layer):
            sp.dma_start(mix_save, zgate[:, :, :].rearrange("p a b -> p (a b)")).then_inc(mix_saved, 16)
            sp.wait_ge(mix_saved, 16 * (layer + 1))

        RB = 15
        rproj = region(12288, RB, T)
        R_, K_, V_ = rproj[:, 0:NB], rproj[:, NB:2 * NB], rproj[:, 2 * NB:3 * NB]
        lora_w, lora_a, lora_g = rproj[:, 12], rproj[:, 13], rproj[:, 14]
        winr_buf = region(43776, 3, KT, P)
        pad3 = region(36864, 3, 776)
        shifted = region(39192, 772)
        winr_landed = [sem(f"winr_landed{b}") for b in range(3)]
        rproj_summed, rproj_moved, shift_step = (
            sem("rproj_summed"), sem("rproj_moved"), sem("shift_step"))

        def sp_proj_rw(sp, layer):
            w = w_in[layer].rearrange("(k p) n -> p k n", p=P)
            with sp.Fori(0, RB // 3) as i:
                for b in range(3):
                    sp.wait_ge(rproj_summed, layer * RB + 3 * i + b + 1)
                    sp.dma_start(winr_buf[:, b], w[:, :, bass.ds((3 * i + b) * P + DN_IN, P)]).then_inc(winr_landed[b], 16)

        def pool_proj_rw(pool, layer):
            nc.gpsimd.memset(pad3[:, :, :], 0.0).then_inc(pad_zeroed, 1)

        def pe_proj_rw(pe, layer):
            if layer == 0:
                pe.sem_inc(rproj_summed, 3)
            with pe.Fori(0, RB // 3) as i:
                for b in range(3):
                    pe.wait_ge(winr_landed[b], 16 * (layer * RB // 3 + i + 1))
                    pe.wait_ge(rproj_moved, layer * RB + 3 * i + b + 1)
                    for k in range(KT):
                        for s, (a, w) in enumerate(SEGS):
                            mm = pe.matmul(PS[:, 2 * b + s, 0:w], winr_buf[:, b, k, :], xn[:, k, a:a + w],
                                           start=(k == 0), stop=(k == KT - 1))
                    mm.then_inc(rproj_summed, 1)

        def act_proj_rw(act, layer):
            if layer == 0:
                act.sem_inc(rproj_moved, 3)
            act.wait_ge(pad_zeroed, 2 * layer + 2)
            with act.Fori(0, RB // 3) as i:
                for b in range(3):
                    n = layer * RB + 3 * i + b
                    act.wait_ge(rproj_summed, 3 + n + 1)
                    if b == 0:
                        act.wait_ge(shift_step, 3 * (layer * RB + 3 * i) + 3)
                    nc.scalar.activation(pad3[:, b, 1:1 + CTX], PS[:, 2 * b, 0:CTX], ACT.Copy)
                    nc.scalar.activation(pad3[:, b, 3 + CTX:3 + T].rearrange("p (c r) -> p r c", r=GRID_H),
                                         PS[:, 2 * b + 1, 0:SEQ].rearrange("p (r c) -> p r c", r=GRID_H),
                                         ACT.Copy).then_inc(rproj_moved, 1)

        def dve_proj_rw(dve, layer):
            v = nc.vector
            if layer == 0:
                dve.sem_inc(shift_step, 3)
            with dve.Fori(0, RB // 3) as i:
                for b in range(3):
                    n = layer * RB + 3 * i + b
                    m = 3 * i + b
                    dve.wait_ge(rproj_moved, 3 + n + 1)
                    dve.wait_ge(shift_step, 3 * n + 3)
                    v.tensor_scalar(shifted[:, 0:770], pad3[:, b, 1:771], drv[:, bass.ds(m, 1)], None,
                                    ALU.mult).then_inc(shift_step, 1)
                    dve.wait_ge(shift_step, 3 * n + 4)
                    v.scalar_tensor_tensor(shifted[:, 0:770], pad3[:, b, 0:770], prm[:, layer, 1, bass.ds(B_MU + m, 1)],
                                           shifted[:, 0:770], ALU.mult, ALU.add).then_inc(shift_step, 1)
                    dve.wait_ge(shift_step, 3 * n + 5)
                    for at, off, w in ((0, 0, CTX), (CTX, CTX + 2, SEQ)):
                        ins = v.scalar_tensor_tensor(rproj[:, bass.ds(m, 1), at:at + w].rearrange("p o w -> p (o w)"),
                                                     pad3[:, b, off + 2:off + 2 + w],
                                                     prm[:, layer, 1, bass.ds(B_MU + RB + m, 1)], shifted[:, off:off + w],
                                                     ALU.mult, ALU.add)
                    ins.then_inc(shift_step, 1)

        KK = region(24576, NB, T)
        KP = [region(0, NB, T), region(38400, NB, T)]
        KKP = [region(3072, NB, T), region(23808, NB, T)]
        RP = [region(6144, NB, T), region(41472, NB, T)]
        BP = [region(9216, NB, T), region(27648, NB, T)]
        BON = region(33792, NB, T)
        g2w = region(36864, RW_W)
        w2w = region(37376, RW_W)
        a2w = region(37888, RW_W)
        SG2, AA2, G2, KD2 = ([region(44544 + n * T, T), region(30720 + m * T, T)] for m, n in enumerate((0, 1, 2, 5)))
        E1, E2 = region(44544 + 3 * T, T), region(44544 + 4 * T, T)
        PC = sb("PC", [P, 2, NB, RW_CHUNKS])
        lora_landed = sem("lora_landed")
        kk_step = sem("kk_step")
        kk_squared, kk_summed, kk_rooted, kk_spread = ho_squared, ho_summed, ho_rooted, ho_spread
        K0 = lambda layer: 2 * NB * layer + NB
        lora_acted, lora_summed, gates_ready, fe_exp, fe_dve, fe_pool = (
            sem("lora_acted"), sem("lora_summed"), sem("gates_ready"), sem("fe_exp"), sem("fe_dve"), sem("fe_pool"))

        def sp_feat(sp, layer):
            sp.dma_start(g2w, rw_g2[layer]).then_inc(lora_landed, 16)
            sp.dma_start(w2w, rw_w2[layer].rearrange("d r c -> (d r) c")).then_inc(lora_landed, 16)
            sp.dma_start(a2w, rw_a2[layer].rearrange("d r c -> (d r) c")).then_inc(lora_landed, 16)

        bonus_summed = sem("bonus_summed")

        def act_feat(act, layer):
            sc = nc.scalar
            sc.activation(lora_w, lora_w, ACT.Tanh)
            sc.activation(lora_g, lora_g, ACT.Sigmoid).then_inc(lora_acted, 1)
            for j in range(NB):
                m = K0(layer) + j
                act.wait_ge(kk_step, (1 + 2 * NB) * layer + j + 1)
                if j >= 2:
                    act.wait_ge(kk_summed, m - 1)
                sc.activation([E1, E2][j % 2], KK[:, j, :], ACT.Square).then_inc(kk_squared, 1)
            act.wait_ge(kk_summed, K0(layer) + NB)
            for s, (a, w) in enumerate(SEGS):
                ins = sc.activation(KD2[0][0:8, a:a + w], PS[0:8, s, 0:w], ACT.Sqrt, bias=eps[0:8, 0:1])
            ins.then_inc(kk_rooted, 1)
            act.wait_ge(h_saved, 16 * (layer + 1))
            for u in range(2 * NB):
                j, d = u // 2, u % 2
                SG_, AA, G_ = SG2[d], AA2[d], G2[d]
                n = 2 * NB * layer + u
                act.wait_ge(lora_summed, n + 1)
                if u >= 2:
                    act.wait_ge(fe_pool, 4 * (n - 1))
                    act.wait_ge(fe_dve, 8 * (n - 1))
                c = 4 * (u % 2)
                for s, (a, w) in enumerate(SEGS):
                    sc.activation(SG_[:, a:a + w], PS[:, c + s, 0:w], ACT.Sigmoid,
                                  bias=prm[:, layer, 1, B_W0 + d * NB + j:B_W0 + d * NB + j + 1])
                    ins = sc.activation(AA[:, a:a + w], PS[:, c + 2 + s, 0:w], ACT.Sigmoid,
                                        bias=prm[:, layer, 1, B_A0 + d * NB + j:B_A0 + d * NB + j + 1])
                ins.then_inc(gates_ready, 1)
                if u >= 1:
                    act.wait_ge(fe_pool, 4 * (n - 1) + 2)
                    act.wait_ge(fe_dve, 8 * n)
                act.wait_ge(fe_dve, 8 * n + 1)
                sc.activation(E1, G_, ACT.Exp, scale=-DECAY_SCALE).then_inc(fe_exp, 1)
                sc.activation(E2, G_, ACT.Exp, scale=DECAY_SCALE).then_inc(fe_exp, 1)
                last = G_[:, RW_C - 1::RW_C] if d == 0 else G_[:, 0::RW_C]
                pc = PC[:, d, j, :] if d == 0 else PC[:, d, j, ::-1]
                sc.activation(pc, last, ACT.Exp, scale=-DECAY_SCALE).then_inc(fe_exp, 1)
                act.wait_ge(fe_dve, 8 * n + 2)
                sc.activation(SG_, SG_, ACT.Exp, scale=-DECAY_SCALE).then_inc(fe_exp, 1)

        def pe_feat(pe, layer):
            for j in range(NB):
                m = K0(layer) + j
                pe.wait_ge(kk_squared, m + 1)
                for s, (a, w) in enumerate(SEGS):
                    mm = pe.matmul(PS[0:8, s, 0:w], to_pair_rows(j), [E1, E2][j % 2][:, a:a + w], start=(j == 0), stop=(j == NB - 1))
                mm.then_inc(kk_summed, 1)
            pe.wait_ge(kk_step, (1 + 2 * NB) * layer + NB + 1)
            for j in range(NB):
                for s, (a, w) in enumerate(SEGS):
                    mm = pe.matmul(PS[:, 2 * j + s, 0:w], from_pair_rows(j), KD2[0][0:8, a:a + w], start=True, stop=True)
                mm.then_inc(kk_spread, 1)
            pe.wait_ge(lora_landed, 48 * (layer + 1))
            pe.wait_ge(lora_acted, layer + 1)
            pe.wait_ge(kk_step, (1 + 2 * NB) * (layer + 1))
            for u in range(2 * NB):
                j, d = u // 2, u % 2
                n = 2 * NB * layer + u
                if u >= 2:
                    pe.wait_ge(gates_ready, n - 1)
                c = 4 * (u % 2)
                rows = slice(64 * d, 64 * d + 64)
                for o, (wt, src) in enumerate(((w2w, lora_w), (a2w, lora_a))):
                    for s, (a, w) in enumerate(SEGS):
                        mm = pe.matmul(PS[:, c + 2 * o + s, 0:w], wt[rows, j * P:(j + 1) * P], src[rows, a:a + w],
                                       start=True, stop=True)
                mm.then_inc(lora_summed, 1)
            for j in range(NB):
                n = NB * layer + j
                pe.wait_ge(fe_dve, 8 * (2 * NB * layer + 2 * j + 2))
                if j == 0:
                    pe.wait_ge(gates_ready, 2 * NB * (layer + 1))
                for s, (a, w) in enumerate(SEGS):
                    mm = pe.matmul(PS[:, 2 * j + s, 0:w], headones[:, :], BON[:, j, a:a + w], start=True, stop=True)
                mm.then_inc(bonus_summed, 1)

        def dve_feat(dve, layer):
            v = nc.vector
            n = (1 + 2 * NB) * layer
            for j in range(NB):
                v.tensor_scalar(KK[:, j, :], K_[:, j, :], prm[:, layer, 1, B_KK + j:B_KK + j + 1], None,
                                ALU.mult).then_inc(kk_step, 1)
            dve.wait_ge(kk_rooted, 2 * layer + 2)
            v.reciprocal(KD2[0][0:8, :], KD2[0][0:8, :]).then_inc(kk_step, 1)
            for j in range(NB):
                dve.wait_ge(kk_spread, 2 * NB * layer + NB + j + 1)
                for s, (a, w) in enumerate(SEGS):
                    ins = v.tensor_tensor(KK[:, j, a:a + w], KK[:, j, a:a + w], PS[:, 2 * j + s, 0:w], ALU.mult)
                ins.then_inc(kk_step, 1)
            dve.wait_ge(kk_step, n + 1 + 2 * NB)
            dve.wait_ge(h_saved, 16 * (layer + 1))
            for u in range(2 * NB):
                j, d = u // 2, u % 2
                n = 2 * NB * layer + u
                way = (lambda t: t) if d == 0 else (lambda t: t[:, ::-1])
                col = lambda c0: prm[:, layer, 1, c0:c0 + 1]
                SG_, AA, G_, KD = SG2[d], AA2[d], G2[d], KD2[d]
                dve.wait_ge(gates_ready, n + 1)
                if u >= 2:
                    dve.wait_ge(fe_pool, 4 * (n - 1))
                v.tensor_tensor_scan(way(G_), keep[:, :], way(SG_), 0.0, ALU.mult, ALU.add).then_inc(fe_dve, 1)
                dve.wait_ge(fe_dve, 8 * n + 1)
                v.tensor_tensor(SG_, G_, SG_, ALU.subtract).then_inc(fe_dve, 1)
                v.tensor_scalar(KD, AA, col(B_KA + j), drv[:, 15 + j:16 + j], ALU.mult, ALU.add).then_inc(fe_dve, 1)
                dve.wait_ge(fe_dve, 8 * n + 3)
                v.tensor_tensor(KD, KD, K_[:, j, :], ALU.mult).then_inc(fe_dve, 1)
                dve.wait_ge(fe_dve, 8 * n + 4)
                dve.wait_ge(fe_exp, 4 * n + 3)
                if d == 0:
                    v.scalar_tensor_tensor(BON[:, j, :], KD, col(B_U + d * NB + j), R_[:, j, :], ALU.mult, ALU.mult).then_inc(fe_dve, 2)
                else:
                    v.scalar_tensor_tensor(G_, KD, col(B_U + d * NB + j), R_[:, j, :], ALU.mult, ALU.mult).then_inc(fe_dve, 1)
                    dve.wait_ge(fe_dve, 8 * n + 5)
                    v.tensor_tensor(BON[:, j, :], BON[:, j, :], G_, ALU.add).then_inc(fe_dve, 1)
                v.tensor_tensor(way(KP[d][:, j, :]), KD, E2, ALU.mult).then_inc(fe_dve, 1)
                v.tensor_tensor(way(RP[d][:, j, :]), R_[:, j, :], E1, ALU.mult).then_inc(fe_dve, 1)
            for j in range(NB):
                n = NB * layer + j
                dve.wait_ge(bonus_summed, n + 1)
                for s, (a, w) in enumerate(SEGS):
                    ins = v.tensor_tensor(BON[:, j, a:a + w], PS[:, 2 * j + s, 0:w], V_[:, j, a:a + w], ALU.mult)

        def pool_feat(pool, layer):
            gp = nc.gpsimd
            for u in range(2 * NB):
                j, d = u // 2, u % 2
                n = 2 * NB * layer + u
                way = (lambda t: t) if d == 0 else (lambda t: t[:, ::-1])
                SG_, AA = SG2[d], AA2[d]
                pool.wait_ge(gates_ready, n + 1)
                pool.wait_ge(fe_dve, 8 * n + 3)
                gp.tensor_tensor(AA, AA, KK[:, j, :], ALU.mult).then_inc(fe_pool, 1)
                pool.wait_ge(fe_pool, 4 * n + 1)
                pool.wait_ge(fe_exp, 4 * n + 2)
                gp.tensor_tensor(way(BP[d][:, j, :]), AA, E2, ALU.mult).then_inc(fe_pool, 1)
                pool.wait_ge(fe_exp, 4 * n + 4)
                gp.tensor_tensor(way(KKP[d][:, j, :]), SG_, KK[:, j, :], ALU.mult).then_inc(fe_pool, 2)

        RWBUF = ([12288 + 1024 * n for n in range(6)] + [21504, 37376] + [44544 + 1024 * n for n in range(4)])

        def rwbuf(n):
            return [region(RWBUF[n] + 512 * g, NB, P) for g in range(2)]

        BDK, BDB, BDKK, BDV, KPT, BPT, VTK, AM, ATT, AUK, ARK, ST = (rwbuf(n) for n in range(12))
        XR, YR, TR = ([region(30720 + 1024 * n + 512 * g, NB, P) for g in range(2)] for n in range(3))
        y_moved = dsem("y_moved")
        bp_built, bpt_ready, bpt_moved, auk_ready, auk_moved = q_decayed, v_weighted, kst_ready, eb_ready, dd_ready

        def rw_loops():
            for (a, w), first, back in zip(SEGS, (0, CTX // RW_C), (SEQ, 0)):
                yield first, w // RW_C, (a, back)

        def pool_rw(pool, layer):
            gp = nc.gpsimd
            for g in range(2):
                gp.memset(ST[g], 0.0).then_inc(s_updated[g], 1)
            for first, steps, base in rw_loops():
                with pool.Fori(0, steps) as i:
                    it, own = STEPS * layer + 6 + first + i, RW_CHUNKS * layer + first + i
                    for g in range(2):
                        fwd = bass.ds(base[g] + i * RW_C, RW_C)
                        v_cols = V_[:, :, fwd if g == 0 else bass.ds(T - base[1] - RW_C - i * RW_C, RW_C)]
                        for dst, cols, ready, used, count in (
                                (BDKK, KKP[g][:, :, fwd], ug_built, ks_ready, it),
                                (BDB, BP[g][:, :, fwd], bp_built, bpt_ready, it),
                                (BDK, KP[g][:, :, fwd], k_built, kq_ready, it),
                                (BDV, v_cols, v_built, vtok_ready, it)):
                            out = dst[g] if dst is not BDV or g == 0 else BDV[1]
                            out = out.rearrange("p u (b t) -> p u b t", b=2)
                            if dst is BDV and g == 1:
                                out = out[:, :, :, ::-1]
                            pool.wait_ge(phase_done, 4)
                            pool.wait_ge(used[g], count)
                            gp.tensor_tensor(out, bc(cols, 2, [P, NB, 2, RW_C]),
                                             bc(headones[:, :].rearrange("p (b t) -> p b t", b=2), 1, [P, NB, 2, RW_C]),
                                             ALU.mult).then_inc(ready[g], 1)

        def quad(pe, bank_, lhs, rhs, start=True, stop=True, width=P, at=0):
            for u in range(NB):
                mm = pe.matmul(PS[:, bank_, at + u * width:at + (u + 1) * width], lhs[:, u, :], rhs[:, u, :],
                               start=start, stop=stop)
            return mm

        def quad_turn(pe, bank_, src):
            for u in range(NB):
                mm = pe.transpose(PS[:, bank_, u * P:(u + 1) * P], src[:, u, :], ident[:, :])
            return mm

        def pe_rw(pe, layer):
            n = LEVELS_RW
            for first, steps, base in rw_loops():
                with pe.Fori(0, steps) as i:
                    it = STEPS * layer + 6 + first + i
                    own = RW_CHUNKS * layer + first + i
                    xs = XS * layer + 6 * LEVELS_DN + n * (first + i)
                    ts = TS * layer + 6 * (LEVELS_DN - 1) + (n - 1) * (first + i)
                    rp = [RP[g][:, :, bass.ds(base[g] + i * RW_C, RW_C)] for g in range(2)]
                    for g in range(2):
                        c = 4 * g
                        pe.wait_ge(s_scaled[g], it)
                        pe.wait_ge(y_moved[g], own + 1)
                        pe.wait_ge(ug_built[g], it + 1)
                        pe.wait_ge(bp_built[g], it + 1)
                        quad(pe, c, BDKK[g], BDB[g]).then_inc(kk_ready[g], 1)
                        pe.wait_ge(k_built[g], it + 1)
                        quad(pe, c + 1, BDK[g], BDKK[g]).then_inc(auk_ready[g], 1)
                        quad_turn(pe, c + 3, BDK[g]).then_inc(ktok_ready[g], 1)
                        quad(pe, c + 2, BDK[g], rp[g], width=RW_C)
                        quad(pe, c + 2, BDB[g], rp[g], width=RW_C, at=NB * RW_C).then_inc(kq_ready[g], 1)
                    for g in range(2):
                        c = 4 * g
                        pe.wait_ge(a_ready[g], it + 1)
                        quad_turn(pe, c, BDB[g]).then_inc(bpt_ready[g], 1)
                        pe.wait_ge(v_built[g], it + 1)
                        pe.wait_ge(auk_moved[g], it + 1)
                        quad_turn(pe, c + 1, BDV[g]).then_inc(vtok_ready[g], 1)
                        pe.wait_ge(ktok_moved[g], it + 1)
                        quad_turn(pe, c + 3, AM[g]).then_inc(at_turned[g], 1)
                    for l in range(n):
                        if l > 0:
                            for g in range(2):
                                pe.wait_ge(x_ready[g], xs + l)
                                if l == 1:
                                    pe.wait_ge(at_moved[g], it + 1)
                                    pe.wait_ge(vtok_moved[g], it + 1)
                                times_even(pe, 4 * g + 1, ATT[g], XR[g], l).then_inc(tx_summed[g], 1)
                            for g in range(2):
                                pe.wait_ge(tx_masked[g], ts + l)
                                pe.wait_ge(y_ready[g], xs + l)
                                if l == 1:
                                    pe.wait_ge(attn_ready[g], it + 1)
                                times_packed(pe, 4 * g + 2, YR[g], TR[g]).then_inc(xd_summed[g], 1)
                        for g in range(2):
                            pe.wait_ge(x_ready[g], xs + l + 1)
                            if l == 0:
                                pe.wait_ge(bpt_moved[g], it + 1)
                            quad_turn(pe, 4 * g, XR[g]).then_inc(x_turned[g], 1)
                        if l == 0:
                            for g in range(2):
                                pe.wait_ge(s_updated[g], it + 2 * (layer + 1))
                                pe.wait_ge(at_moved[g], it + 1)
                                pe.wait_ge(vtok_moved[g], it + 1)
                                for u in range(NB):
                                    o = PS[:, 4 * g + 3, u * P:(u + 1) * P]
                                    pe.matmul(o, BDKK[g][:, u, :], ST[g][:, u, :], start=True, stop=False)
                                    mm = pe.matmul(o, AUK[g][:, u, :], VTK[g][:, u, :], start=False, stop=True)
                                mm.then_inc(ks_ready[g], 1)
                    for g in range(2):
                        pe.wait_ge(y_ready[g], xs + n)
                        pe.wait_ge(r_ready[g], it + 1)
                        quad(pe, 4 * g + 1, YR[g], AM[g]).then_inc(vn_summed[g], 1)
                    for g in range(2):
                        c = 4 * g
                        pe.wait_ge(vn_ready[g], it + 1)
                        for u in range(NB):
                            o = PS[:, c + 2, u * P:(u + 1) * P]
                            pe.matmul(o, KPT[g][:, u, :], VTK[g][:, u, :], start=True, stop=False)
                            mm = pe.matmul(o, BPT[g][:, u, :], ATT[g][:, u, :], start=False, stop=True)
                        mm.then_inc(s_summed[g], 1)
                        for u in range(NB):
                            o = PS[:, c + 3, u * RW_C:(u + 1) * RW_C]
                            pe.matmul(o, ST[g][:, u, :], rp[g][:, u, :], start=True, stop=False)
                            pe.matmul(o, VTK[g][:, u, :], ARK[g].rearrange("p u t -> p (u t)")[:, u * RW_C:(u + 1) * RW_C],
                                      start=False, stop=False)
                            mm = pe.matmul(o, ATT[g][:, u, :],
                                           ARK[g].rearrange("p u t -> p (u t)")[:, (NB + u) * RW_C:(NB + u + 1) * RW_C],
                                           start=False, stop=True)
                        mm.then_inc(o_summed[g], 1)

        def act_rw(act, layer):
            sc = nc.scalar
            n = LEVELS_RW
            if layer == 0:
                for g in range(2):
                    act.sem_inc(y_moved[g], 1)
            for first, steps, base in rw_loops():
                with act.Fori(0, steps) as i:
                    it = STEPS * layer + 6 + first + i
                    own = RW_CHUNKS * layer + first + i
                    xs = XS * layer + 6 * LEVELS_DN + n * (first + i)
                    ts = TS * layer + 6 * (LEVELS_DN - 1) + (n - 1) * (first + i)
                    for g in range(2):
                        act.wait_ge(kk_ready[g], it + 1)
                        sc.activation(AM[g], bank(4 * g), ACT.Copy).then_inc(a_ready[g], 1)
                        act.wait_ge(ktok_ready[g], it + 1)
                        sc.activation(KPT[g], bank(4 * g + 3), ACT.Copy).then_inc(ktok_moved[g], 1)
                    for g in range(2):
                        act.wait_ge(bpt_ready[g], it + 1)
                        sc.activation(BPT[g], bank(4 * g), ACT.Copy).then_inc(bpt_moved[g], 1)
                        act.wait_ge(vtok_ready[g], it + 1)
                        sc.activation(VTK[g], bank(4 * g + 1), ACT.Copy).then_inc(vtok_moved[g], 1)
                        act.wait_ge(at_turned[g], it + 1)
                        sc.activation(ATT[g], bank(4 * g + 3), ACT.Copy).then_inc(at_moved[g], 1)
                    for l in range(n):
                        for g in range(2):
                            act.wait_ge(x_turned[g], xs + l + 1)
                            if l > 0:
                                act.wait_ge(xd_summed[g], ts + l)
                            sc.activation(YR[g], bank(4 * g), ACT.Copy).then_inc(y_ready[g], 1)
                        if l == 1:
                            for g in range(2):
                                act.wait_ge(ks_ready[g], it + 1)
                                act.wait_ge(x0_step[g], it + 1)
                                sc.activation(AM[g], bank(4 * g + 3), ACT.Copy, scale=-1.0).then_inc(r_ready[g], 1)
                    for g in range(2):
                        act.wait_ge(vn_summed[g], it + 1)
                        sc.activation(ATT[g], bank(4 * g + 1), ACT.Copy).then_inc(vn_ready[g], 1)
                    for g in range(2):
                        act.wait_ge(o_summed[g], it + 1)
                        sc.activation(RP[g][:, :, bass.ds(base[g] + i * RW_C, RW_C)],
                                      PS[:, 4 * g + 3, 0:NB * RW_C].rearrange("p (u t) -> p u t", u=NB),
                                      ACT.Copy).then_inc(y_moved[g], 1)

        def dve_rw(dve, layer):
            v = nc.vector
            n = LEVELS_RW
            for first, steps, base in rw_loops():
                with dve.Fori(0, steps) as i:
                    it = STEPS * layer + 6 + first + i
                    own = RW_CHUNKS * layer + first + i
                    xs = XS * layer + 6 * LEVELS_DN + n * (first + i)
                    ts = TS * layer + 6 * (LEVELS_DN - 1) + (n - 1) * (first + i)
                    for g in range(2):
                        dve.wait_ge(auk_ready[g], it + 1)
                        v.tensor_tensor(AUK[g], bank(4 * g + 1), bc(upto_strict[:, :], 1, [P, NB, P]),
                                        ALU.mult).then_inc(auk_moved[g], 1)
                        dve.wait_ge(a_ready[g], it + 1)
                        dve.wait_ge(kq_ready[g], it + 1)
                        dve.wait_ge(bpt_ready[g], it + 1)
                        v.tensor_tensor(XR[g], AM[g], bc(level[:, 0, :], 1, [P, NB, P]), ALU.mult).then_inc(x0_step[g], 1)
                        dve.wait_ge(x0_step[g], it + 1)
                        v.tensor_tensor(XR[g], bc(ident[:, :], 1, [P, NB, P]), XR[g], ALU.subtract).then_inc(x_ready[g], 1)
                        v.tensor_tensor(ARK[g].rearrange("p u t -> p (u t)").rearrange("p (u t) -> p u t", t=RW_C),
                                        PS[:, 4 * g + 2, :].rearrange("p (u t) -> p u t", t=RW_C),
                                        bc(pair_incl[:, :], 1, [P, 2 * NB, RW_C]), ALU.mult).then_inc(attn_ready[g], 1)
                    for l in range(1, n):
                        for g in range(2):
                            dve.wait_ge(tx_summed[g], ts + l)
                            v.tensor_tensor(packed_sbuf(TR[g], l), packed_bank(4 * g + 1, l), level_mask(l), ALU.mult).then_inc(tx_masked[g], 1)
                        for g in range(2):
                            dve.wait_ge(xd_summed[g], ts + l)
                            dve.wait_ge(x_turned[g], xs + l)
                            v.tensor_tensor(even(XR[g], l), even(XR[g], l), packed_bank(4 * g + 2, l), ALU.subtract).then_inc(x_ready[g], 1)
                    for g in range(2):
                        dve.wait_ge(o_summed[g], it + 1)
                        v.tensor_tensor(ST[g], ST[g], bank(4 * g + 2), ALU.add).then_inc(s_scaled[g], 1)
                    for g in range(2):
                        dve.wait_ge(s_scaled[g], it + 1)
                        v.tensor_tensor(ST[g], ST[g], PC[:, g, :, bass.ds(base[g] // RW_C + i, 1)].broadcast_to([P, NB, P]),
                                        ALU.mult).then_inc(s_updated[g], 1)

        go_step, go_summed, go_act = sem("go_step"), sem("go_summed"), sem("go_act")
        h_loaded = sem("h_loaded")
        mix_dn = region(18432, NB, T)
        mix_rw = region(12288, NB, T)
        gtmp = [region(44544 + n * T, T) for n in range(4)]

        def sp_rw_out(sp, layer):
            sp.dma_start(h[:, :, :].rearrange("p a b -> p (a b)"), h_save).then_inc(h_loaded, 16)

        def sp_load_mix(sp, layer):
            sp.dma_start(mix_dn[:, :, :].rearrange("p a b -> p (a b)"), mix_save).then_inc(h_loaded, 16)
            sp.wait_ge(h_loaded, 32 * (layer + 1))

        def dve_rw_out(dve, layer):
            v = nc.vector
            y = RP[0]
            d0, s0, a0 = 28 * layer, 12 * layer, 8 * layer
            for j in range(NB):
                v.tensor_tensor(y[:, j, :], y[:, j, :], RP[1][:, j, ::-1], ALU.add).then_inc(go_step, 1)
                dve.wait_ge(go_step, d0 + 2 * j + 1)
                v.tensor_tensor(y[:, j, :], y[:, j, :], BON[:, j, :], ALU.add).then_inc(go_step, 1)
            for j in range(NB):
                dve.wait_ge(go_step, d0 + 2 * j + 2)
                dve.wait_ge(go_summed, s0 + j + 1)
                for s, (a, w) in enumerate(SEGS):
                    ins = v.scalar_tensor_tensor(y[:, j, a:a + w], PS[:, 2 * j + s, 0:w], -1.0 / 64, y[:, j, a:a + w],
                                                 ALU.mult, ALU.add)
                ins.then_inc(go_step, 1)
            for j in range(NB):
                col = lambda c0: prm[:, layer, 0, c0 + j:c0 + j + 1]
                dve.wait_ge(go_act, a0 + NB + j + 1)
                v.reciprocal(gtmp[j], gtmp[j]).then_inc(go_step, 1)
                dve.wait_ge(go_step, d0 + 12 + 4 * j + 1)
                v.tensor_tensor(y[:, j, :], y[:, j, :], gtmp[j], ALU.mult).then_inc(go_step, 1)
                dve.wait_ge(go_step, d0 + 12 + 4 * j + 2)
                v.tensor_scalar(y[:, j, :], y[:, j, :], col(A_LN), col(A_LN + NB), ALU.mult, ALU.add).then_inc(go_step, 1)
                dve.wait_ge(go_step, d0 + 12 + 4 * j + 3)
                dve.wait_ge(go_summed, s0 + 2 * NB + j + 1)
                v.tensor_tensor(mix_rw[:, j, 0:CTX], y[:, j, 0:CTX], PS[:, 2 * j, 0:CTX], ALU.mult)
                v.tensor_tensor(mix_rw[:, j, CTX:T].rearrange("p (r c) -> p c r", r=GRID_H),
                                y[:, j, CTX:T].rearrange("p (c r) -> p c r", r=GRID_H),
                                PS[:, 2 * j + 1, 0:SEQ].rearrange("p (c r) -> p c r", r=GRID_H),
                                ALU.mult).then_inc(go_step, 1)

        def pe_rw_out(pe, layer):
            y = RP[0]
            d0, s0, a0 = 28 * layer, 12 * layer, 8 * layer

            def spread(lhs, src, j):
                for s, (a, w) in enumerate(SEGS):
                    mm = pe.matmul(PS[:, 2 * j + s, 0:w], lhs, src[:, a:a + w], start=True, stop=True)
                mm.then_inc(go_summed, 1)

            for j in range(NB):
                pe.wait_ge(go_step, d0 + 2 * j + 2)
                spread(headones[:, :], y[:, j, :], j)
            for j in range(NB):
                pe.wait_ge(go_act, a0 + j + 1)
                spread(headones[:, :], gtmp[j], j)
            for j in range(NB):
                pe.wait_ge(go_act, a0 + NB + j + 1)
                spread(g2w[:, j * P:(j + 1) * P], lora_g, j)

        def act_rw_out(act, layer):
            y = RP[0]
            d0, s0 = 28 * layer, 12 * layer
            for j in range(NB):
                act.wait_ge(go_step, d0 + 8 + j + 1)
                nc.scalar.activation(gtmp[j], y[:, j, :], ACT.Square).then_inc(go_act, 1)
            for j in range(NB):
                act.wait_ge(go_summed, s0 + NB + j + 1)
                for s, (a, w) in enumerate(SEGS):
                    ins = nc.scalar.activation(gtmp[j][:, a:a + w], PS[:, 2 * j + s, 0:w], ACT.Sqrt, scale=1.0 / 64, bias=eps[:, 1:2])
                ins.then_inc(go_act, 1)

        WB = DNB + KT

        def sp_wout(sp, layer):
            w = w_out[layer].rearrange("(k p) n -> p k n", p=P)
            with sp.Fori(0, KT // 2) as i:
                for b in range(2):
                    sp.wait_ge(proj_summed, layer * WB + DNB + 2 * i + b + 1)
                    sp.dma_start(win_buf[:, b], w[:, :, bass.ds((2 * i + b) * P, P)]).then_inc(win_landed[b], 16)

        def pe_wout(pe, layer, segs):
            pe.wait_ge(h_loaded, 32 * (layer + 1))
            with pe.Fori(0, KT // 2) as i:
                for b in range(2):
                    pe.wait_ge(win_landed[b], 16 * (layer * WB // 2 + DNB // 2 + i + 1))
                    pe.wait_ge(proj_moved, layer * WB + DNB + 2 * i + b + 1)
                    for k in range(KT):
                        src = mix_dn[:, k, :] if k < NB else mix_rw[:, k - NB, :]
                        for s, (a, w) in enumerate(segs):
                            mm = pe.matmul(PS[:, 2 * b + s, 0:w], win_buf[:, b, k, :], src[:, a:a + w],
                                           start=(k == 0), stop=(k == KT - 1))
                    mm.then_inc(proj_summed, 1)

        def dve_wout(dve, layer, segs):
            dve.wait_ge(h_loaded, 32 * (layer + 1))
            with dve.Fori(0, KT // 2) as i:
                for b in range(2):
                    dve.wait_ge(proj_summed, 2 + layer * WB + DNB + 2 * i + b + 1)
                    for s, (a0, w) in enumerate(segs):
                        at = 0 if a0 == 0 else 1
                        hv = h[:, bass.ds(2 * i + b, 1), a0:a0 + w].rearrange("p o w -> p (o w)")
                        g = mod[:, bass.ds(5 * KT + 2 * i + b, 1), at:at + 1].rearrange("p o w -> p (o w)")
                        ins = nc.vector.scalar_tensor_tensor(hv, PS[:, 2 * b + s, 0:w], g, hv, ALU.mult, ALU.add)
                    ins.then_inc(proj_moved, 1)

        out_tok = region(12288, SEQ // P, D_MODEL)
        out_turned, out_moved, stored = tiles_transposed, tile_moved, tok_landed
        N_LAST = 3 * DEPTH

        def act_final(act):
            act_square(act, N_LAST, SEGS[1:])
            act_root(act, N_LAST, SEGS[1:])
            for k in range(KT):
                act.wait_ge(normed, KT * N_LAST + k + 1)
                nc.scalar.activation(xn[:, k, CTX:T], xn[:, k, CTX:T], ACT.Copy,
                                     scale=prm[:, 0, 0, A_FINAL + k:A_FINAL + k + 1]).then_inc(xn_ready, 1)

        def pe_final(pe):
            pe_square_sum(pe, N_LAST, SEGS[1:])
            pe.wait_ge(xn_ready, KT * (N_LAST + 1))
            pe.wait_ge(rstd_ready, 2 * N_LAST + 2)
            for t in range(SEQ // P):
                for k in range(KT):
                    mm = pe.transpose(PS[:, 2 * t + k // 4, (k % 4) * P:(k % 4 + 1) * P],
                                      xn[:, k, CTX + t * P:CTX + (t + 1) * P], ident[:, :])
                mm.then_inc(out_turned, 1)

        def dve_final(dve):
            dve_norm(dve, N_LAST, SEGS[1:])
            for t in range(SEQ // P):
                dve.wait_ge(out_turned, KT + t + 1)
                nc.vector.tensor_copy(out_tok[:, t, :].rearrange("p (b f) -> p b f", b=2),
                                      PS[:, 2 * t:2 * t + 2, :]).then_inc(out_moved, 1)

        def sp_final(sp):
            o = out[0].rearrange("(t p) f -> t p f", p=P)
            for t in range(SEQ // P):
                sp.wait_ge(out_moved, 2 * KT + t + 1)
                sp.dma_start(o[t], out_tok[:, t, :]).then_inc(stored, 16)
            sp.wait_ge(stored, 32 + 16 * (SEQ // P))

        block = es.enter_context(nc.Block())

        def segs_of(layer):
            return SEGS if layer < DEPTH - 1 else SEGS[1:]

        @block.sync
        def _(sp):
            sp_setup(sp)
            sp_ada_first(sp)
            for layer in range(DEPTH):
                dma_after(sp, start_of(layer, 1))
                sp_ffn(sp, 2 * layer, layer, 0)
                dma_after(sp, start_of(layer, 3))
                sp_proj_dn(sp, layer)
                sp_save_h(sp, layer)
                dma_after(sp, start_of(layer, 7))
                sp_save_mix(sp, layer)
                sp_proj_rw(sp, layer)
                dma_after(sp, start_of(layer, 8))
                sp_feat(sp, layer)
                dma_after(sp, start_of(layer, 10))
                sp_rw_out(sp, layer)
                sp_load_mix(sp, layer)
                dma_after(sp, start_of(layer, 11))
                sp_wout(sp, layer)
                dma_after(sp, start_of(layer, 12))
                sp_ffn(sp, 2 * layer + 1, layer, 1)
            dma_after(sp, start_of(DEPTH, 0))
            sp_final(sp)

        @block.gpsimd
        def _(pool):
            end = lambda: end_phase(pool, "pool")
            pool_setup(pool)
            end()
            for layer in range(DEPTH):
                for _ in range(2):
                    end()
                pool_ada_guest(pool, 2 * layer)
                for _ in range(2):
                    end()
                pool_proj_dn(pool, layer)
                end()
                pool_dn(pool, layer)
                end()
                end()
                pool_proj_rw(pool, layer)
                end()
                pool_feat(pool, layer)
                end()
                pool_rw(pool, layer)
                for _ in range(4):
                    end()
                pool_ada_guest(pool, 2 * layer + 1)
                end()

        @block.tensor
        def _(pe):
            end = lambda: end_phase(pe, "pe")
            pe_setup(pe)
            end()
            for layer in range(DEPTH):
                if layer == 0:
                    pe_ada_first(pe)
                end()
                pe_square_sum(pe, 3 * layer, SEGS)
                end()
                pe_ffn(pe, 2 * layer, SEGS)
                end()
                pe_square_sum(pe, 3 * layer + 1, SEGS)
                end()
                pe_proj_dn(pe, layer)
                end()
                pe_dn(pe, layer)
                end()
                pe_dn_out(pe, layer)
                end()
                pe_proj_rw(pe, layer)
                end()
                pe_feat(pe, layer)
                end()
                pe_rw(pe, layer)
                end()
                pe_rw_out(pe, layer)
                end()
                pe_wout(pe, layer, segs_of(layer))
                end()
                pe_square_sum(pe, 3 * layer + 2, segs_of(layer))
                end()
                pe_ffn(pe, 2 * layer + 1, segs_of(layer))
                end()
            pe_final(pe)

        @block.scalar
        def _(act):
            end = lambda: end_phase(act, "act")
            act_setup(act)
            end()
            for layer in range(DEPTH):
                end()
                act_modulate(act, 3 * layer, 0, SEGS, 2 * layer)
                end()
                act_ffn(act, 2 * layer, SEGS)
                end()
                act_modulate(act, 3 * layer + 1, 1, SEGS)
                end()
                act_proj_dn(act, layer)
                end()
                act_dn(act, layer)
                end()
                act_dn_out(act, layer)
                end()
                act_proj_rw(act, layer)
                end()
                act_feat(act, layer)
                end()
                act_rw(act, layer)
                end()
                act_rw_out(act, layer)
                end()
                end()
                act_modulate(act, 3 * layer + 2, 2, segs_of(layer), 2 * layer + 1)
                end()
                act_ffn(act, 2 * layer + 1, segs_of(layer))
                end()
            act_final(act)

        @block.vector
        def _(dve):
            end = lambda: end_phase(dve, "dve")
            dve_setup(dve)
            end()
            for layer in range(DEPTH):
                if layer == 0:
                    dve_ada_first(dve)
                end()
                dve_norm_split(dve, 3 * layer, 2 * layer, SEGS)
                end()
                dve_ffn(dve, 2 * layer, SEGS, 0)
                end()
                dve_norm(dve, 3 * layer + 1, SEGS)
                end()
                dve_proj_dn(dve, layer)
                end()
                dve_dn(dve, layer)
                end()
                dve_dn_out(dve, layer)
                end()
                dve_proj_rw(dve, layer)
                end()
                dve_feat(dve, layer)
                end()
                dve_rw(dve, layer)
                end()
                dve_rw_out(dve, layer)
                end()
                dve_wout(dve, layer, segs_of(layer))
                end()
                dve_norm_split(dve, 3 * layer + 2, 2 * layer + 1, segs_of(layer))
                end()
                dve_ffn(dve, 2 * layer + 1, segs_of(layer), 2)
                end()
            dve_final(dve)


_INS = ['x', 'c', 'ctx', 'c_ctx', 'ada_w', 'ada_b', 'norm_g', 'ffn_w13', 'ffn_w2', 'w_in', 'dn_conv', 'dn_a_log',
        'dn_dt_bias', 'dn_norm', 'rw_mu', 'rw_w0', 'rw_w2', 'rw_a0', 'rw_a2', 'rw_g2', 'rw_kk', 'rw_ka', 'rw_u',
        'rw_ln', 'w_out', 'final_norm']
_OUTS = [((1, SEQ, D_MODEL), 'float32')]


def kernel(**inputs):
    import numpy as _np
    import concourse.bacc as _bacc
    from concourse import mybir as _mybir
    from concourse.bass_utils import run_bass_kernel_spmd as _run

    nc = _bacc.Bacc("TRN2", target_bir_lowering=False, num_devices=1)
    arrays, args = {}, []
    for name in _INS:
        a = _np.ascontiguousarray(inputs[name])
        arrays[f"in_{name}_dram"] = a
        args.append(nc.dram_tensor(f"in_{name}_dram", a.shape, _mybir.dt.from_np(a.dtype), kind="ExternalInput").ap())
    for i, (shape, dtype) in enumerate(_OUTS):
        dt = _mybir.dt.from_np(_np.dtype(dtype))
        args.append(nc.dram_tensor(f"out_{i}_dram", shape, dt, kind="ExternalOutput").ap())
    build(nc, *args)
    r = _run(nc, [arrays], core_ids=[0])
    got = tuple(r.results[0][f"out_{i}_dram"] for i in range(len(_OUTS)))
    return got[0]
```
